# Optimizing a Trainium2 kernel written in Bass

```python
import math
import jax, jax.numpy as jnp
from jax import lax
import numpy as np

D_MODEL = 1024
BATCH = 1
SEQ = 512
DEPTH = 1

EPS = 1e-6
A_HEADS = 4
A_DK = 48
A_DV = 96
A_LOWRANK = 16
A_GATE_TAU = 16.0
A_CHUNK = 64
B_HEADS = 6
B_HEAD_DIM = 64
IDX_HEADS = 4
IDX_DIM = 32
B_TOPK_MAX = 256
B_QBLOCK = 32
C_HEADS = 6
C_HEAD_DIM = 64
C_PATTERNS = ((128, 1), (512, 4), (2048, 16))
C_QBLOCK = 128
D_WIDTH = 384
D_BLOCKS = 8
D_CONV = 4
D_C = 8.0
REL_BUCKETS = 32
REL_MAX_DIST = 2048
N_SOFTMAX_HEADS = B_HEADS + C_HEADS
N_BRANCH = 4
BRANCH_WIDTH = 384
MOE_GROUPS = 4
MOE_EXPERTS_PER_GROUP = 4
N_EXPERTS = MOE_GROUPS * MOE_EXPERTS_PER_GROUP
MOE_TOPK = 2
MOE_HIDDEN = 512

IN_SPLITS = (A_HEADS * A_DK, A_HEADS * A_DK, A_HEADS * A_DV, A_HEADS * A_DV, A_LOWRANK,
             B_HEADS * B_HEAD_DIM, B_HEADS * B_HEAD_DIM, B_HEADS * B_HEAD_DIM,
             IDX_HEADS * IDX_DIM, IDX_DIM, IDX_HEADS,
             C_HEADS * C_HEAD_DIM, C_HEADS * C_HEAD_DIM, C_HEADS * C_HEAD_DIM,
             D_WIDTH, D_WIDTH)
IN_TOTAL = sum(IN_SPLITS)

kernel_name = "hybrid_gla_dsa_dilated_rglru_hmoe"

def rms_norm(x, gain):
    xf = x.astype(jnp.float32)
    y = xf * lax.rsqrt(jnp.mean(xf * xf, axis=-1, keepdims=True) + EPS)
    return (y * gain.astype(jnp.float32)).astype(x.dtype)

def rel_bucket(dist):
    max_exact = REL_BUCKETS // 2
    n = jnp.maximum(dist, 0)
    nf = jnp.maximum(n, 1).astype(jnp.float32)
    large = max_exact + (jnp.log(nf / max_exact) / math.log(REL_MAX_DIST / max_exact)
                         * (REL_BUCKETS - max_exact)).astype(jnp.int32)
    large = jnp.minimum(large, REL_BUCKETS - 1)
    return jnp.where(n < max_exact, n, large)

def gla_mixer(q, k, v, g, a_lr, w_a2, b_a2, gain):
    f32 = jnp.float32
    bsz, T, _ = q.shape
    n = T // A_CHUNK
    log_a = jax.nn.log_sigmoid((a_lr @ w_a2 + b_a2).astype(f32)) / A_GATE_TAU
    shp_k = (bsz, n, A_CHUNK, A_HEADS, A_DK)
    qf = q.astype(f32).reshape(shp_k) * A_DK ** -0.5
    kf = k.astype(f32).reshape(shp_k)
    vf = v.astype(f32).reshape(bsz, n, A_CHUNK, A_HEADS, A_DV)
    b = jnp.cumsum(log_a.reshape(shp_k), axis=2)
    b_last = b[:, :, -1:]
    q_dec = qf * jnp.exp(b)
    k_dec = kf * jnp.exp(-b)
    k_end = kf * jnp.exp(b_last - b)
    causal = jnp.tril(jnp.ones((A_CHUNK, A_CHUNK), dtype=bool))
    att = jnp.where(causal, jnp.einsum('bnchk,bnshk->bnhcs', q_dec, k_dec), 0.0)
    o_intra = jnp.einsum('bnhcs,bnshv->bnchv', att, vf)
    u = jnp.einsum('bnshk,bnshv->bnhkv', k_end, vf)
    decay = jnp.exp(b_last[:, :, 0])

    def step(S, inp):
        d, uu = inp
        return d[..., None] * S + uu, S

    S0 = jnp.zeros((bsz, A_HEADS, A_DK, A_DV), f32)
    _, S_prev = lax.scan(step, S0, (jnp.moveaxis(decay, 1, 0), jnp.moveaxis(u, 1, 0)))
    S_prev = jnp.moveaxis(S_prev, 0, 1)
    o = o_intra + jnp.einsum('bnchk,bnhkv->bnchv', q_dec, S_prev)
    o = o.reshape(bsz, T, A_HEADS, A_DV)
    o = o * lax.rsqrt(jnp.mean(o * o, axis=-1, keepdims=True) + EPS)
    o = o * gain.astype(f32).reshape(A_HEADS, A_DV)
    o = o.reshape(bsz, T, A_HEADS * A_DV) * jax.nn.silu(g.astype(f32))
    return o.astype(q.dtype)

def dsa_mixer(q, k, v, iq, ik, iw, bias_tab):
    f32 = jnp.float32
    bsz, T, _ = q.shape
    k_sel = min(B_TOPK_MAX, T // 4)
    nb = T // B_QBLOCK
    iqf = iq.astype(f32).reshape(bsz, T, IDX_HEADS, IDX_DIM) * IDX_DIM ** -0.5
    ikf = ik.astype(f32)
    iwf = iw.astype(f32) * IDX_HEADS ** -0.5
    qh = q.astype(f32).reshape(bsz, T, B_HEADS, B_HEAD_DIM) * B_HEAD_DIM ** -0.5
    kh = k.reshape(bsz, T, B_HEADS, B_HEAD_DIM)
    vh = v.reshape(bsz, T, B_HEADS, B_HEAD_DIM)
    key_pos = jnp.arange(T)

    def block(i):
        start = i * B_QBLOCK
        q_pos = start + jnp.arange(B_QBLOCK)
        iq_b = lax.dynamic_slice_in_dim(iqf, start, B_QBLOCK, axis=1)
        iw_b = lax.dynamic_slice_in_dim(iwf, start, B_QBLOCK, axis=1)
        q_b = lax.dynamic_slice_in_dim(qh, start, B_QBLOCK, axis=1)
        s = jax.nn.relu(jnp.einsum('bqhd,bsd->bqhs', iq_b, ikf))
        score = jnp.einsum('bqh,bqhs->bqs', iw_b, s)
        score = jnp.where(key_pos[None, :] <= q_pos[:, None], score, -jnp.inf)
        _, idx = lax.top_k(score, k_sel)
        valid = idx <= q_pos[None, :, None]
        k_g = jax.vmap(lambda kk, ii: kk[ii])(kh, idx).astype(f32)
        v_g = jax.vmap(lambda vv, ii: vv[ii])(vh, idx).astype(f32)
        logits = jnp.einsum('bqhd,bqkhd->bqhk', q_b, k_g)
        bias = bias_tab[rel_bucket(q_pos[None, :, None] - idx)].astype(f32)
        logits = logits + jnp.moveaxis(bias, -1, 2)
        logits = jnp.where(valid[:, :, None, :], logits, -jnp.inf)
        p = jax.nn.softmax(logits, axis=-1)
        return jnp.einsum('bqhk,bqkhd->bqhd', p, v_g).astype(q.dtype)

    out = lax.map(block, jnp.arange(nb))
    return jnp.moveaxis(out, 0, 1).reshape(bsz, T, B_HEADS * B_HEAD_DIM)

def _dilated_window(qh, kh, vh, window, dil, bias_tab):
    bsz, T, H, Dh = qh.shape
    n = T // dil
    span = window // dil
    c = math.gcd(C_QBLOCK, n)
    nb = n // c

    def to_sub(t):
        return t.reshape(bsz, n, dil, H, Dh).transpose(0, 2, 1, 3, 4).reshape(bsz * dil, n, H, Dh)

    pad = ((0, 0), (span, 0), (0, 0), (0, 0))
    qs = to_sub(qh).reshape(bsz * dil, nb, c, H, Dh)
    ks = jnp.pad(to_sub(kh), pad)
    vs = jnp.pad(to_sub(vh), pad)
    kidx = (jnp.arange(nb) * c)[:, None] + jnp.arange(c + span)[None, :]
    kb = ks[:, kidx]
    vb = vs[:, kidx]
    rel = jnp.arange(c)[:, None] - jnp.arange(c + span)[None, :] + span
    kpos = kidx - span
    valid = ((rel >= 0) & (rel <= span))[None] & (kpos >= 0)[:, None, :]
    bias = jnp.transpose(bias_tab[rel_bucket(rel * dil)].astype(jnp.float32), (2, 0, 1))
    logits = jnp.einsum('bnqhd,bnkhd->bnhqk', qs, kb) + bias[None, None]
    logits = jnp.where(valid[None, :, None], logits, -jnp.inf)
    m = jnp.max(logits, axis=-1, keepdims=True)
    p = jnp.exp(logits - m)
    l = jnp.sum(p, axis=-1, keepdims=True)
    o = jnp.einsum('bnhqk,bnkhd->bnqhd', p / l, vb)
    lse = (m + jnp.log(l))[..., 0]
    o = o.reshape(bsz, dil, n, H, Dh).transpose(0, 2, 1, 3, 4).reshape(bsz, T, H, Dh)
    lse = lse.transpose(0, 1, 3, 2).reshape(bsz, dil, n, H).transpose(0, 2, 1, 3).reshape(bsz, T, H)
    return o, lse

def dilated_mixer(q, k, v, bias_tab):
    f32 = jnp.float32
    bsz, T, _ = q.shape
    qh = q.astype(f32).reshape(bsz, T, C_HEADS, C_HEAD_DIM) * C_HEAD_DIM ** -0.5
    kh = k.astype(f32).reshape(bsz, T, C_HEADS, C_HEAD_DIM)
    vh = v.astype(f32).reshape(bsz, T, C_HEADS, C_HEAD_DIM)
    outs, lses = [], []
    for window, dil in C_PATTERNS:
        o, lse = _dilated_window(qh, kh, vh, window, dil, bias_tab)
        outs.append(o)
        lses.append(lse)
    w = jax.nn.softmax(jnp.stack(lses, axis=0), axis=0)
    o = jnp.einsum('pbth,pbthd->bthd', w, jnp.stack(outs, axis=0))
    return o.reshape(bsz, T, C_HEADS * C_HEAD_DIM).astype(q.dtype)

def rglru_mixer(y_in, x_in, conv_w, conv_b, w_r, b_r, w_i, b_i, lam):
    f32 = jnp.float32
    bsz, T, W = x_in.shape
    xc = lax.conv_general_dilated(x_in.astype(f32), conv_w.astype(f32)[:, None, :],
                                  window_strides=(1,), padding=[(D_CONV - 1, 0)],
                                  dimension_numbers=('NWC', 'WIO', 'NWC'),
                                  feature_group_count=W) + conv_b.astype(f32)
    xb = xc.reshape(bsz, T, D_BLOCKS, W // D_BLOCKS)
    r = jax.nn.sigmoid(jnp.einsum('btnc,ncd->btnd', xb, w_r.astype(f32)).reshape(bsz, T, W) + b_r.astype(f32))
    i = jax.nn.sigmoid(jnp.einsum('btnc,ncd->btnd', xb, w_i.astype(f32)).reshape(bsz, T, W) + b_i.astype(f32))
    log_a = -D_C * r * jax.nn.softplus(-lam.astype(f32))
    a = jnp.exp(log_a)
    u = jnp.sqrt(-jnp.expm1(2.0 * log_a)) * (i * xc)

    def combine(left, right):
        a1, b1 = left
        a2, b2 = right
        return a1 * a2, a2 * b1 + b2

    _, h = lax.associative_scan(combine, (a, u), axis=1)
    return (jax.nn.gelu(y_in.astype(f32)) * h).astype(x_in.dtype)

def mixer_block(xn, w_in, a_w2, a_b2, a_gain, conv_w, conv_b, lru_wr, lru_br, lru_wi, lru_bi,
                lru_lambda, w_gate, b_gate, w_branch, w_out, rel_bias):
    proj = xn @ w_in
    offsets = np.cumsum(IN_SPLITS)[:-1].tolist()
    (aq, ak, av, ag, alr, bq, bk, bv, iq, ik, iw, cq, ck, cv, dy, dx) = jnp.split(proj, offsets, axis=-1)
    o_a = gla_mixer(aq, ak, av, ag, alr, a_w2, a_b2, a_gain)
    o_b = dsa_mixer(bq, bk, bv, iq, ik, iw, rel_bias[:, :B_HEADS])
    o_c = dilated_mixer(cq, ck, cv, rel_bias[:, B_HEADS:])
    o_d = rglru_mixer(dy, dx, conv_w, conv_b, lru_wr, lru_br, lru_wi, lru_bi, lru_lambda)
    merged = None
    for gi, ob in enumerate((o_a, o_b, o_c, o_d)):
        gate = jax.nn.sigmoid(xn @ w_gate[gi] + b_gate[gi])
        term = gate * (ob @ w_branch[gi])
        merged = term if merged is None else merged + term
    return merged @ w_out

def hier_moe(x, w_rg, b_rg, w_re, b_re, w_g, w_u, w_d):
    f32 = jnp.float32
    bsz, T, Dm = x.shape
    xt = x.reshape(-1, Dm)
    g_logits = (xt @ w_rg).astype(f32) + b_rg.astype(f32)
    g_prob = jax.nn.softmax(g_logits, axis=-1)
    g_sel = jnp.argmax(g_logits, axis=-1)
    g_w = jnp.take_along_axis(g_prob, g_sel[:, None], axis=-1)
    e_logits = ((xt @ w_re).astype(f32) + b_re.astype(f32)).reshape(-1, MOE_GROUPS, MOE_EXPERTS_PER_GROUP)
    e_in = jnp.take_along_axis(e_logits, g_sel[:, None, None], axis=1)[:, 0]
    top_v, top_i = lax.top_k(e_in, MOE_TOPK)
    top_w = jax.nn.softmax(top_v, axis=-1) * g_w
    expert_id = g_sel[:, None] * MOE_EXPERTS_PER_GROUP + top_i
    gates = jnp.sum(jax.nn.one_hot(expert_id, N_EXPERTS, dtype=f32) * top_w[..., None], axis=1)
    out = jnp.zeros(xt.shape, f32)
    for e in range(N_EXPERTS):
        h = jax.nn.silu(xt @ w_g[e]) * (xt @ w_u[e])
        out = out + gates[:, e:e + 1] * (h @ w_d[e]).astype(f32)
    return out.astype(x.dtype).reshape(bsz, T, Dm)

def setup_inputs(seed: int = 0) -> dict:
    key = jax.random.key(seed)
    ks = jax.random.split(key, 32)
    f32 = jnp.float32

    def nrm(k, shape, fan_in, scale=1.0):
        return jax.random.normal(k, shape, f32) * (scale * fan_in ** -0.5)

    def small(k, shape, s):
        return jax.random.normal(k, shape, f32) * s

    bw = D_WIDTH // D_BLOCKS
    u = jax.random.uniform(ks[11], (DEPTH, D_WIDTH), f32, 0.9, 0.999)
    a0 = u ** (1.0 / D_C)
    return {
        "x": jax.random.normal(ks[0], (BATCH, SEQ, D_MODEL), f32),
        "w_in": nrm(ks[1], (DEPTH, D_MODEL, IN_TOTAL), D_MODEL),
        "a_w2": nrm(ks[2], (DEPTH, A_LOWRANK, A_HEADS * A_DK), A_LOWRANK),
        "a_b2": small(ks[3], (DEPTH, A_HEADS * A_DK), 0.1),
        "a_gain": 1.0 + small(ks[4], (DEPTH, A_HEADS * A_DV), 0.02),
        "conv_w": nrm(ks[5], (DEPTH, D_CONV, D_WIDTH), D_CONV),
        "conv_b": small(ks[6], (DEPTH, D_WIDTH), 0.01),
        "lru_wr": nrm(ks[7], (DEPTH, D_BLOCKS, bw, bw), bw),
        "lru_br": small(ks[8], (DEPTH, D_WIDTH), 0.1),
        "lru_wi": nrm(ks[9], (DEPTH, D_BLOCKS, bw, bw), bw),
        "lru_bi": small(ks[10], (DEPTH, D_WIDTH), 0.1),
        "lru_lambda": jnp.log(a0) - jnp.log1p(-a0),
        "w_gate": nrm(ks[12], (DEPTH, N_BRANCH, D_MODEL, D_MODEL), D_MODEL),
        "b_gate": small(ks[13], (DEPTH, N_BRANCH, D_MODEL), 0.02),
        "w_branch": nrm(ks[14], (DEPTH, N_BRANCH, BRANCH_WIDTH, D_MODEL), BRANCH_WIDTH),
        "w_out": nrm(ks[15], (DEPTH, D_MODEL, D_MODEL), D_MODEL, 0.5),
        "rel_bias": small(ks[16], (REL_BUCKETS, N_SOFTMAX_HEADS), 0.1),
        "norm1": 1.0 + small(ks[17], (DEPTH, D_MODEL), 0.02),
        "norm2": 1.0 + small(ks[18], (DEPTH, D_MODEL), 0.02),
        "norm_f": 1.0 + small(ks[19], (D_MODEL,), 0.02),
        "moe_wrg": nrm(ks[20], (DEPTH, D_MODEL, MOE_GROUPS), D_MODEL),
        "moe_brg": small(ks[21], (DEPTH, MOE_GROUPS), 0.01),
        "moe_wre": nrm(ks[22], (DEPTH, D_MODEL, N_EXPERTS), D_MODEL),
        "moe_bre": small(ks[23], (DEPTH, N_EXPERTS), 0.01),
        "moe_wg": nrm(ks[24], (DEPTH, N_EXPERTS, D_MODEL, MOE_HIDDEN), D_MODEL),
        "moe_wu": nrm(ks[25], (DEPTH, N_EXPERTS, D_MODEL, MOE_HIDDEN), D_MODEL),
        "moe_wd": nrm(ks[26], (DEPTH, N_EXPERTS, MOE_HIDDEN, D_MODEL), MOE_HIDDEN),
    }

def reference(x, w_in, a_w2, a_b2, a_gain, conv_w, conv_b, lru_wr, lru_br, lru_wi, lru_bi,
              lru_lambda, w_gate, b_gate, w_branch, w_out, rel_bias, norm1, norm2, norm_f,
              moe_wrg, moe_brg, moe_wre, moe_bre, moe_wg, moe_wu, moe_wd):
    h = x
    for l in range(DEPTH):
        xn = rms_norm(h, norm1[l])
        h = h + mixer_block(xn, w_in[l], a_w2[l], a_b2[l], a_gain[l], conv_w[l], conv_b[l],
                            lru_wr[l], lru_br[l], lru_wi[l], lru_bi[l], lru_lambda[l],
                            w_gate[l], b_gate[l], w_branch[l], w_out[l], rel_bias)
        h = h + hier_moe(rms_norm(h, norm2[l]), moe_wrg[l], moe_brg[l], moe_wre[l], moe_bre[l],
                         moe_wg[l], moe_wu[l], moe_wd[l])
    return rms_norm(h, norm_f)


_drawn_inputs = setup_inputs


def setup_inputs(seed=0):
    import zlib

    import numpy as np

    out = dict(_drawn_inputs(seed))
    spreads = {}
    factors = {'a_b2': 2.934,
     'a_gain': 12.741,
     'conv_b': 3.941,
     'lru_br': 5.238,
     'lru_bi': 3.815,
     'b_gate': 8.0,
     'rel_bias': 3.636,
     'norm1': 2.795,
     'norm_f': 8.028,
     'moe_brg': 63.928,
     'moe_bre': 52.154,
     'norm2': 6.333}
    for name, (base, spread) in spreads.items():
        noise = np.random.default_rng([zlib.crc32(name.encode()), seed]).standard_normal(out[name].shape)
        drawn = base * np.exp(spread * noise) if base else spread * noise
        out[name] = __import__('jax').numpy.asarray(drawn.astype(out[name].dtype))
    for name, factor in factors.items():
        out[name] = (out[name] * factor).astype(out[name].dtype)
    return out
```

```python
import math
from contextlib import ExitStack

import numpy as np
import concourse.bass as bass
from concourse import mybir

F32 = mybir.dt.float32
ALU = mybir.AluOpType
ACT = mybir.ActivationFunctionType
AX = mybir.AxisListType

P = 128
T = 512
NT = T // P
D = 1024
KD = D // P
EPS = 1e-6
A_HEADS, A_DK, A_DV, A_RANK, A_TAU, A_CHUNK = 4, 48, 96, 16, 16.0, 64
NCH = T // A_CHUNK
HEADS, HD = 6, 64
IDX_HEADS, IDX_DIM = 4, 32
TOPK = 128
PATTERNS = ((128, 1), (512, 4), (2048, 16))
W = 384
KW = W // P
LRU_BLOCKS = 8
LRU_C = 8.0
BUCKETS, MAX_DIST = 32, 2048
NBR = 4
GROUPS, EPG = 4, 4
NE = GROUPS * EPG
HID = 512
KH = HID // P
BIG = -1e30
TAKEN = -3e38
GELU_C = math.sqrt(2.0 / math.pi)

SPLITS = (("aq", 192), ("ak", 192), ("av", 384), ("ag", 384), ("alr", 16), ("bq", 384), ("bk", 384), ("bv", 384),
          ("iq", 128), ("ik", 32), ("iw", 4), ("cq", 384), ("ck", 384), ("cv", 384), ("dy", 384), ("dx", 384))
COL0 = {}
_c = 0
for _n, _w in SPLITS:
    COL0[_n] = _c
    _c += _w

PROJ = (("idx", "iq", 164), ("dx", "dx", 384), ("dy", "dy", 384), ("alr", "alr", 16), ("aqk", "aq", 384),
        ("av", "av", 384), ("ag", "ag", 384), ("bq", "bq", 384), ("bk", "bk", 384), ("bv", "bv", 384),
        ("cq", "cq", 384), ("ck", "ck", 384), ("cv", "cv", 384))
MCOLS = 256
NMC = D // MCOLS
LOADS = ([("proj", n, COL0[c], w) for n, c, w in PROJ]
         + [("merge", b, mc * MCOLS, MCOLS) for mc in range(NMC) for b in range(NBR)]
         + [("out", 0, mc * MCOLS, MCOLS) for mc in range(NMC)])
RING = 3
SLOT = KD * W

MAIN = (("xT", 8), ("iq", 1), ("ik", 1), ("iw", 1), ("dx", 3), ("dy", 3), ("alr", 1), ("aqk", 4), ("av", 4),
        ("ag", 4), ("bq", 3), ("bk", 3), ("bv", 4), ("cq", 3), ("ck", 3), ("cv", 4), ("oTa", 3), ("oTc", 3),
        ("oTb", 3), ("gate", 32), ("x2T", 8))
MEND = {}
_c = 0
for _n, _w in MAIN:
    _c += _w
    MEND[_n] = _c


def load_index(kind, name, col=None):
    for i, l in enumerate(LOADS):
        if l[0] == kind and l[1] == name and (col is None or l[2] == col):
            return i
    raise KeyError((kind, name))


def rel_bucket(dist):
    exact = BUCKETS // 2
    if dist < exact:
        return dist
    big = exact + int(np.float32(np.log(np.float32(dist) / np.float32(exact)) / np.float32(math.log(MAX_DIST / exact))
                                 * np.float32(BUCKETS - exact)))
    return min(big, BUCKETS - 1)


def constants():
    sq = np.zeros((P, 3 * P + 8), np.float32)
    sq[:, 0:P] = np.eye(P)
    r = np.arange(P)
    same = (r[:, None] // A_CHUNK) == (r[None, :] // A_CHUNK)
    sq[:, P:2 * P] = same & (r[None, :] >= r[:, None])
    sq[:, 2 * P:3 * P] = np.where(r[None, :] > r[:, None], BIG, 0.0)
    sq[:, 3 * P:3 * P + 4] = np.arange(4, 0, -1)
    n = T + P
    tab = np.zeros((BUCKETS + 2, n), np.float32)
    for j in range(n):
        dist = T - 1 - j
        if dist < 0:
            tab[BUCKETS:, j] = BIG
            continue
        tab[rel_bucket(dist), j] = 1.0
        tab[BUCKETS + 1, j] = sum(dist % dil == 0 and dist <= win for win, dil in PATTERNS)
        c = tab[BUCKETS + 1, j]
        tab[BUCKETS + 1, j] = math.log(c) if c else BIG
    sel = np.zeros((2, 2 * HEADS), np.float32)
    sel[0, :HEADS] = 1.0
    sel[1, HEADS:] = 1.0
    return sq, tab, sel


def build(nc, d, out):
    ctx = ExitStack()
    with ctx:
        sems = {}

        def S(name):
            if name not in sems:
                sems[name] = ctx.enter_context(nc.semaphore(name))
            return sems[name]

        arena = ctx.enter_context(nc.sbuf_tensor("arena", [P, 49292], F32))

        def view(at, *shape):
            n = int(np.prod(shape))
            v = arena[:, at:at + n]
            if len(shape) == 2:
                v = v.rearrange("p (a b) -> p a b", b=shape[1])
            elif len(shape) == 3:
                v = v.rearrange("p (a b c) -> p a b c", b=shape[1], c=shape[2])
            return v

        ring = [arena[:, i * SLOT:(i + 1) * SLOT] for i in range(RING)]
        xnT = view(9216, KD, T)
        XS = 13312
        xs = view(XS, NT, D)
        wqk = view(XS, KD, 8, 64)
        oA = view(XS, NT, W)
        oA2 = view(XS + 1536, NT, W)
        keR = view(XS + 3072, NT, 2 * P)
        oR = [view(XS, NT, W), view(XS + 1536, NT, W)]
        QKB = 17408
        bd = view(QKB, 2, KW, W)
        bqT, bkT = view(QKB, KW, T), view(QKB + 1536, KW, T)
        CVR = 20480
        xc, tr, ti, sq_ = (view(CVR + 1536 * i, KW, T) for i in range(4))
        bv, cqT, ckT, cv = view(CVR, NT, W), view(CVR + 1536, KW, T), view(CVR + 3072, KW, T), view(CVR + 4608, NT, W)
        hres = view(CVR, NT, D)
        AR = 26624
        aqT, akT, av, ag = view(AR, 2, T), view(AR + 1024, 2, T), view(AR + 2048, NT, W), view(AR + 3584, NT, W)
        DR = 31744
        dxp = view(DR, KW, T + 3)
        dyT = view(DR + 1548, KW, T)
        iqT, ikT, alrT = view(DR + 3084, T), view(DR + 3596, T), view(DR + 4108, T)
        oTd = view(36364, KW, T)
        oT = [view(DR + 1548, KW, T), view(AR, KW, T), view(AR + 1536, KW, T), oTd]
        SEL0 = 37900
        sel = [None, view(SEL0, 256), view(SEL0 + 256, 384), view(SEL0 + 640, 512)]
        rel = view(39052, 2, T)
        gate_t = view(39052, 2, T)
        GR = 40076
        zb, na, b16, eb, kd, ek = (view(GR + 1024 * i, 2, T) for i in range(6))
        seg = arena[:, GR + 5120:GR + 6144]
        attm = view(GR + 6144, 2, 4, P)
        St = view(GR + 7168, 2, NCH + 1, A_DV)
        bias = view(GR, 2 * HEADS, T)
        lg, pr, pT = view(GR + 6144, 2, T), view(GR + 7168, 2, T), view(GR + 8192, 2, T)
        merged = view(GR, KD, T)
        gterm = view(SEL0, T)
        EW = [24576, 36864]
        wg = [view(a, KD, HID) for a in EW]
        wu = [view(a + 4096, KD, HID) for a in EW]
        wd = [view(a + 8192, KH, D) for a in EW]
        hT = view(0, KH, T)
        sg = view(2048, 2, T)
        onorm = view(4096, NT, D)
        nf = arena[:, 8192:8192 + D]

        def sb(name, shape):
            return ctx.enter_context(nc.sbuf_tensor(name, shape, F32))

        cst = sb("cst", [P, 3 * P + 8])
        ident, glamask, future, prio = cst[:, 0:P], cst[:, P:2 * P], cst[:, 2 * P:3 * P], cst[:, 3 * P:3 * P + 4]
        btab = sb("btab", [BUCKETS + 2, T + P])
        relb = sb("relb", [BUCKETS + 2, 2 * HEADS])
        bias_rows = sb("bias_rows", [2 * HEADS, T + P])
        NROW = 74
        rows = sb("rows", [NROW, P])
        cols = sb("cols", [P, NROW])
        c_norm1, c_norm2, c_bgate = cols[:, 0:8], cols[:, 8:16], cols[:, 16:48]
        c_convw, c_convb, c_br, c_bi, c_lam, c_b2 = (cols[:, 48:60], cols[:, 60:63], cols[:, 63:66], cols[:, 66:69],
                                                     cols[:, 69:72], cols[:, 72:74])
        half = sb("half", [P, 38])
        sp = sb("sp", [P, 8, 3])
        ones = sb("ones", [P, 1])
        stat = sb("stat", [P, 4, NT])
        wa2 = sb("wa2", [A_RANK, 4 * 64])
        gain = sb("gain", [P, W])
        iw = sb("iw", [P, NT, IDX_HEADS])
        m8 = sb("m8", [P, 8])
        nmx = sb("nmx", [P, 4])
        lsum = sb("lsum", [P, 2, HEADS])
        rl = sb("rl", [P, 2, HEADS])
        ostat = sb("ostat", [P, NT * A_HEADS])
        wr = sb("wr", [P, KD, GROUPS + NE])
        rbias = sb("rbias", [P, GROUPS + NE])
        rt = sb("rt", [P, 16, NT, 4])
        gates = sb("gates", [P, NT, NE])
        rlog = sb("rlog", [P, NT, GROUPS + NE])

        ps = [ctx.enter_context(nc.psum_tensor(f"bank{i}", [P, 512], F32)) for i in range(8)]
        main, aux, lgb = ps[0:2], ps[2:4], ps[4:6]
        att_bank = (aux, main)
        oa_bank = ((ps[6], ps[7]), (ps[4], ps[5]))
        scratch = d["bias_scratch"]

        block = ctx.enter_context(nc.Block())

        def ring_count(i):
            return 16 * sum(2 if LOADS[j][0] == "merge" else 1 for j in range(i % RING, i + 1, RING))

        def wait_load(eng, i):
            eng.wait_ge(S(f"w_landed{i % RING}"), ring_count(i))

        @block.sync
        def _(sp_):
            for t in range(NT):
                sp_.dma_start(xs[:, t, :], d["x"][0, t * P:(t + 1) * P, :]).then_inc(S(f"x_landed{t}"), 16)
            w_in = d["w_in"][0].rearrange("(k p) n -> p k n", p=P)
            for i, (kind, name, col, width) in enumerate(LOADS):
                if kind == "merge" and (name, col) == (1, 0):
                    sp_.wait_ge(S("o_done"), 2 * NT)
                    sp_.dma_start(hres, d["x"][0].rearrange("(t p) n -> p t n", p=P)).then_inc(S("xres_landed"), 16)
                if i >= RING:
                    sp_.wait_ge(S("w_used"), i - RING + 1)
                dst = ring[i % RING][:, 0:KD * width].rearrange("p (k n) -> p k n", n=width)
                landed = S(f"w_landed{i % RING}")
                if kind == "proj":
                    src = w_in[:, :, col:col + width]
                elif kind == "merge":
                    src = d["w_gate"][0, name].rearrange("(k p) n -> p k n", p=P)[:, :, col:col + width]
                else:
                    src = d["w_out"][0].rearrange("(k p) n -> p k n", p=P)[:, :, col:col + width]
                sp_.dma_start(dst, src).then_inc(landed, 16)
                if kind == "merge":
                    dst2 = ring[i % RING][:, KD * width:(KD + KW) * width].rearrange("p (k n) -> p k n", n=width)
                    sp_.dma_start(dst2, d["w_branch"][0, name].rearrange("(k p) n -> p k n", p=P)[:, :, col:col + width]
                                  ).then_inc(landed, 16)
            for e in range(NE):
                if e == 0:
                    sp_.wait_ge(S("merge_done"), 4 * KD)
                elif e == 1:
                    sp_.wait_ge(S("h_done"), NT * NMC)
                else:
                    sp_.wait_ge(S("e_used"), e - 1)
                s = e % 2
                sp_.dma_start(wg[s], d["moe_wg"][0, e].rearrange("(k p) n -> p k n", p=P)).then_inc(S(f"e_landed{s}"), 16)
                sp_.dma_start(wu[s], d["moe_wu"][0, e].rearrange("(k p) n -> p k n", p=P)).then_inc(S(f"e_landed{s}"), 16)
                sp_.dma_start(wd[s], d["moe_wd"][0, e].rearrange("(k p) n -> p k n", p=P)).then_inc(S(f"e_landed{s}"), 16)
            for t in range(NT):
                sp_.wait_ge(S("y_done"), t + 1)
                sp_.dma_start(out[0, t * P:(t + 1) * P, :], onorm[:, t, :]).then_inc(S("stored"), 16)
            sp_.wait_ge(S("stored"), 16 * NT)

        @block.gpsimd
        def _(pool):
            pool.dma_start(cst[:, :], d["c_sq"]).then_inc(S("cst_landed"), 16)
            pool.memset(rows[:, :], 0.0).then_inc(S("rows_clear"), 1)
            pool.wait_ge(S("rows_clear"), 1)
            at = 0
            for name, n in (("norm1", 8), ("norm2", 8), ("b_gate", 32), ("conv_w", 12), ("conv_b", 3), ("lru_br", 3),
                            ("lru_bi", 3), ("lru_lambda", 3)):
                src = d[name][0]
                if len(src.shape) == 2:
                    src = src.rearrange("a b -> (a b)")
                pool.dma_start(rows[at:at + n, :], src.rearrange("(a b) -> a b", b=P)).then_inc(S("rows_landed"), 16)
                at += n
            for h in range(A_HEADS):
                r, c = at + h // 2, 64 * (h % 2)
                pool.dma_start(rows[r:r + 1, c:c + A_DK], d["a_b2"][0:1, h * A_DK:(h + 1) * A_DK]
                               ).then_inc(S("rows_landed"), 16)
            pool.dma_start(btab[:, :], d["c_tab"]).then_inc(S("btab_landed"), 16)
            pool.dma_start(relb[0:BUCKETS, :], d["rel_bias"]).then_inc(S("btab_landed"), 16)
            pool.dma_start(relb[BUCKETS:BUCKETS + 2, :], d["c_sel"]).then_inc(S("btab_landed"), 16)
            pool.memset(bd, 0.0).then_inc(S("bd_clear"), 1)
            pool.memset(wa2[:, :], 0.0).then_inc(S("bd_clear"), 1)
            pool.wait_ge(S("bd_clear"), 2)
            bw = W // LRU_BLOCKS
            for m, name in enumerate(("lru_wr", "lru_wi")):
                for n in range(LRU_BLOCKS):
                    r = n * bw
                    while r < (n + 1) * bw:
                        e = min((n + 1) * bw, (r // P + 1) * P)
                        pool.dma_start(bd[r % P:r % P + e - r, m, r // P, n * bw:(n + 1) * bw],
                                       d[name][0, n, r - n * bw:e - n * bw, :]).then_inc(S("bd_landed"), 16)
                        r = e
            for h in range(A_HEADS):
                pool.dma_start(wa2[:, 64 * h:64 * h + A_DK], d["a_w2"][0, :, h * A_DK:(h + 1) * A_DK]
                               ).then_inc(S("wa2_landed"), 16)
            pool.dma_start(gain[:, :], d["a_gain"][0:1, :].to_broadcast([P, W])).then_inc(S("gain_landed"), 16)
            pool.dma_start(wr[:, :, 0:GROUPS], d["moe_wrg"][0].rearrange("(k p) n -> p k n", p=P)
                           ).then_inc(S("wr_landed"), 16)
            pool.dma_start(wr[:, :, GROUPS:], d["moe_wre"][0].rearrange("(k p) n -> p k n", p=P)
                           ).then_inc(S("wr_landed"), 16)
            pool.dma_start(rbias[:, 0:GROUPS], d["moe_brg"][0:1, :].to_broadcast([P, GROUPS])).then_inc(S("wr_landed"), 16)
            pool.dma_start(rbias[:, GROUPS:], d["moe_bre"][0:1, :].to_broadcast([P, NE])).then_inc(S("wr_landed"), 16)
            pool.wait_ge(S("bias_rows_ready"), 2)
            pool.dma_start(scratch, bias_rows[:, :].unsqueeze(1).to_broadcast([2 * HEADS, P, T + P])
                           ).then_inc(S("scratch_stored"), 16)
            pool.wait_ge(S("scratch_stored"), 16)
            pool.wait_ge(S("oa_ready"), 1)
            pool.wait_ge(S("attm_ready"), 2 * NT)
            pool.wait_ge(S("gla_pe_done"), NT)
            toeplitz = bass.AP(scratch.tensor, scratch.offset + P - 1,
                               [(T + P - 1, P), (P * (T + P), 2 * HEADS), (1, T)])
            pool.dma_start(bias, toeplitz).then_inc(S("bias_landed"), 16)

        @block.scalar
        def _(act):
            state = {"main": 0, "step": 0}

            def link(ins):
                state["step"] += 1
                ins.then_inc(S("act_step"), 1)
                act.wait_ge(S("act_step"), state["step"])

            def drain_main(fn):
                n = state["main"]
                act.wait_ge(S("main_full"), n + 1)
                fn(main[n % 2]).then_inc(S("main_empty"), 1)
                state["main"] = n + 1

            for t in range(NT):
                act.wait_ge(S(f"x_landed{t}"), 16)
                act.activation(view(CVR + D * t, D), xs[:, t, :], ACT.Square,
                               accum_out=stat[:, 0, t:t + 1]).then_inc(S("ss_ready"), 1)
            act.wait_ge(S("ms_ready"), 1)
            act.activation(stat[:, 2, :], stat[:, 1, :], ACT.Sqrt).then_inc(S("rms_ready"), 1)
            act.wait_ge(S("cols_ready"), 1)
            for c in range(KD):
                drain_main(lambda b, c=c: act.activation(xnT[:, c, :], b[:, :], ACT.Copy, scale=c_norm1[:, c:c + 1]))
            drain_main(lambda b: act.activation(iqT, b[:, :], ACT.Copy, scale=IDX_DIM ** -0.5))
            drain_main(lambda b: act.activation(ikT, b[:, :], ACT.Copy))
            drain_main(lambda b: act.activation(iw[:, :, :].rearrange("p a b -> p (a b)"), b[:, 0:NT * IDX_HEADS], ACT.Copy,
                                                scale=IDX_HEADS ** -0.5))
            for c in range(KW):
                drain_main(lambda b, c=c: act.activation(dxp[:, c, 3:3 + T], b[:, :], ACT.Copy))
            act.wait_ge(S("lam_abs"), 1)
            act.activation(sp[:, 1, :], sp[:, 0, :], ACT.Exp).then_inc(S("lam_exp"), 1)
            n = 0
            for i in range(1, NT):
                for h in range(IDX_HEADS):
                    act.wait_ge(S("idx_full"), n + 1)
                    if n >= 2:
                        act.wait_ge(S("rel_used"), n - 1)
                    act.activation(rel[:, n % 2, 0:(i + 1) * P], lgb[n % 2][:, 0:(i + 1) * P], ACT.Relu
                                   ).then_inc(S("rel_ready"), 1)
                    n += 1
            for c in range(KW):
                drain_main(lambda b, c=c: act.activation(dyT[:, c, :], b[:, :], ACT.Copy))
            act.wait_ge(S("cols_ready"), 2)
            n = 0
            for m, dst in ((0, tr), (1, ti)):
                for c in range(KW):
                    act.wait_ge(S("lru_full"), n + 1)
                    act.activation(dst[:, c, :], aux[n % 2][:, :], ACT.Tanh, scale=0.5,
                                   bias=half[:, 32 + 3 * m + c:33 + 3 * m + c]).then_inc(S("lru_tanh"), 1)
                    n += 1
            act.wait_ge(S("sp_ready"), 1)
            act.wait_ge(S("lru_tanh"), 3)
            for c in range(KW):
                act.activation(tr[:, c, :], tr[:, c, :], ACT.Tanh, scale=sp[:, 7, c:c + 1], bias=sp[:, 7, c:c + 1]
                               ).then_inc(S("lru_t2"), 1)
            act.wait_ge(S("lru_t2"), 3)
            act.activation(sq_, tr, ACT.Sqrt).then_inc(S("lru_sqrt"), 1)
            drain_main(lambda b: act.activation(alrT[0:A_RANK, :], b[0:A_RANK, :], ACT.Copy))
            for i in range(2):
                drain_main(lambda b, i=i: act.activation(aqT[:, i, :], b[:, :], ACT.Copy, scale=A_DK ** -0.5))
            for i in range(2):
                drain_main(lambda b, i=i: act.activation(akT[:, i, :], b[:, :], ACT.Copy))
            for dst in (av, ag):
                for t in range(NT):
                    drain_main(lambda b, t=t, dst=dst: act.activation(dst[:, t, :], b[:, 0:W], ACT.Copy))
            act.wait_ge(S("gla_na"), 1)
            link(act.activation(na, na, ACT.Exp))
            act.activation(na, na, ACT.Ln, bias=ones[:, 0:1]).then_inc(S("gla_ln"), 1)
            act.wait_ge(S("lru_u"), 1)
            act.activation(sq_, dyT, ACT.Square).then_inc(S("y2_ready"), 1)
            act.wait_ge(S("gelu_in"), 1)
            act.activation(sq_, sq_, ACT.Tanh, scale=GELU_C).then_inc(S("gelu_tanh"), 1)
            act.wait_ge(S("gla_b"), 1)
            act.activation(eb, b16, ACT.Exp, scale=1.0 / A_TAU).then_inc(S("gla_e"), 1)
            act.activation(kd, b16, ACT.Exp, scale=-1.0 / A_TAU).then_inc(S("gla_e"), 1)
            act.wait_ge(S("gla_d"), 1)
            act.activation(ek, ek, ACT.Exp, scale=1.0 / A_TAU).then_inc(S("gla_e"), 1)
            for dst, scale in ((bqT, HD ** -0.5), (bkT, 1.0)):
                for c in range(KW):
                    drain_main(lambda b, c=c, dst=dst, scale=scale: act.activation(dst[:, c, :], b[:, :], ACT.Copy, scale=scale))
            for i in range(2):
                act.wait_ge(S("ke_full"), i + 1)
                act.activation(keR[:, :, i * P:(i + 1) * P], ps[6 + i][:, :].rearrange("p (t c) -> p t c", c=P), ACT.Copy
                               ).then_inc(S("ke_ready"), 1)
            act.wait_ge(S("lru_u"), 2)
            for t in range(NT):
                drain_main(lambda b, t=t: act.activation(bv[:, t, :], b[:, 0:W], ACT.Copy))
            for t in range(NT):
                act.wait_ge(S("oa_full"), t + 1)
                for hh in range(2):
                    act.activation(oA[:, t, :].rearrange("p (i h v) -> p i h v", h=2, v=A_DV)[:, :, hh, :],
                                   oa_bank[t % 2][hh][:, 0:2 * A_DV].rearrange("p (i v) -> p i v", v=A_DV), ACT.Copy
                                   ).then_inc(S("oa_copied"), 1)
            act.wait_ge(S("oa_copied"), 2 * NT)
            act.activation(oA2, oA, ACT.Square).then_inc(S("oa_sq"), 1)
            act.wait_ge(S("oa_ms"), 1)
            act.activation(ostat[:, :], ostat[:, :], ACT.Sqrt).then_inc(S("oa_rms"), 1)
            act.wait_ge(S("oa_mean"), 1)
            act.activation(oA2, ag, ACT.Tanh, scale=0.5).then_inc(S("oa_tanh"), 1)
            for dst, scale in ((cqT, HD ** -0.5), (ckT, 1.0)):
                for c in range(KW):
                    drain_main(lambda b, c=c, dst=dst, scale=scale: act.activation(dst[:, c, :], b[:, :], ACT.Copy, scale=scale))
            for t in range(NT):
                drain_main(lambda b, t=t: act.activation(cv[:, t, :], b[:, 0:W], ACT.Copy))
            for c in range(KW):
                drain_main(lambda b, c=c: act.activation(oT[0][:, c, :], b[:, :], ACT.Copy))

            def probs(n):
                i = (n // HEADS) % NT
                nk = (i + 1) * P
                act.wait_ge(S("lg_ready"), n + 1)
                if n >= 2:
                    act.wait_ge(S("p_used"), n - 1)
                if n >= 2 * HEADS and n % HEADS == 0:
                    act.wait_ge(S("rl_ready"), n // HEADS - 1)
                act.activation(pr[:, n % 2, 0:nk], lg[:, n % 2, 0:nk], ACT.Exp, bias=nmx[:, n % 4:n % 4 + 1],
                               accum_out=lsum[:, (n // HEADS) % 2, n % HEADS:n % HEADS + 1]).then_inc(S("p_ready"), 1)

            def ptrans(n):
                i = (n // HEADS) % NT
                nk = (i + 1) * P
                act.wait_ge(S("pT_full"), n + 1)
                if n >= 2:
                    act.wait_ge(S("pT_used"), n - 1)
                act.activation(pT[:, n % 2, 0:nk], aux[n % 2][:, 0:nk], ACT.Copy).then_inc(S("pT_ready"), 1)

            units = 2 * NT * HEADS
            for n in range(units + 1):
                if n < units:
                    probs(n)
                if n >= 1:
                    ptrans(n - 1)
            for k in (2, 1):
                for c in range(KW):
                    drain_main(lambda b, c=c, k=k: act.activation(oT[k][:, c, :], b[:, :], ACT.Copy))
            n = 0
            for mc in range(NMC):
                for b_ in range(NBR):
                    for j in range(MCOLS // P):
                        m = mc * (MCOLS // P) + j
                        if n >= 2:
                            act.wait_ge(S("merge_done"), n - 1)
                        drain_main(lambda b, n=n, m=m, b_=b_: act.activation(
                            gate_t[:, n % 2, :], b[:, :], ACT.Tanh, scale=0.5, bias=half[:, 8 * b_ + m:8 * b_ + m + 1]))
                        n += 1
            for t in range(NT):
                act.wait_ge(S("h_done"), NT * (NMC - 1) + t + 1)
                act.activation(xs[:, t, :], hres[:, t, :], ACT.Square, accum_out=stat[:, 0, t:t + 1]).then_inc(S("ss_ready"), 1)
            act.dma_start(nf, d["norm_f"].rearrange("(a n) -> a n", a=1).to_broadcast([P, D])).then_inc(S("nf_landed"), 16)
            act.wait_ge(S("ms_ready"), 2)
            act.activation(stat[:, 2, :], stat[:, 1, :], ACT.Sqrt).then_inc(S("rms_ready"), 1)
            for c in range(KD):
                drain_main(lambda b, c=c: act.activation(xnT[:, c, :], b[:, :], ACT.Copy, scale=c_norm2[:, c:c + 1]))
            act.wait_ge(S("rt_sub"), 1)
            act.activation(rt[:, 2, :, :], rt[:, 1, :, :], ACT.Exp).then_inc(S("rt_exp"), 1)
            act.wait_ge(S("rt_diff"), 1)
            act.activation(rt[:, 9, :, 0], rt[:, 8, :, 0], ACT.Exp).then_inc(S("rt_exp"), 1)
            n = 0
            for e in range(NE):
                for m in range(KH):
                    act.wait_ge(S("gu_full"), n + 1)
                    if n >= 2:
                        act.wait_ge(S("hT_ready"), n - 1)
                    act.activation(sg[:, n % 2, :], ps[n % 2][:, :], ACT.Tanh, scale=0.5).then_inc(S("sg_ready"), 1)
                    n += 1
            for t in range(NT):
                act.wait_ge(S("acc_done"), NE * NT * 2)
                act.activation(onorm[:, t, :], hres[:, t, :], ACT.Square, accum_out=stat[:, 0, t:t + 1]).then_inc(S("ss_ready"), 1)
            act.wait_ge(S("ms_ready"), 3)
            act.activation(stat[:, 2, :], stat[:, 1, :], ACT.Sqrt).then_inc(S("rms_ready"), 1)

        @block.tensor
        def _(pe):
            state = {"main": 0, "load": 0}

            def main_bank():
                n = state["main"]
                if n >= 2:
                    pe.wait_ge(S("main_empty"), n - 1)
                return main[n % 2]

            def main_full(ins):
                ins.then_inc(S("main_full"), 1)
                state["main"] += 1

            def weights(width):
                i = state["load"]
                wait_load(pe, i)
                return ring[i % RING][:, 0:KD * width].rearrange("p (k n) -> p k n", n=width)

            def used(ins_fn):
                state["load"] += 1
                pe.drain().then_inc(S("w_used"), 1)

            def t_tile(lhs_of_k, rows_=P):
                b = main_bank()
                for k in range(KD):
                    last = pe.matmul(b[0:rows_, :], lhs_of_k(k), xnT[:, k, :], start=(k == 0), stop=(k == KD - 1))
                main_full(last)

            def r_tile(w, t, width):
                b = main_bank()
                for k in range(KD):
                    last = pe.matmul(b[:, 0:width], xnT[:, k, t * P:(t + 1) * P], w[:, k, :], start=(k == 0), stop=(k == KD - 1))
                main_full(last)

            def proj_t():
                w = weights(W)
                for c in range(KW):
                    t_tile(lambda k, c=c: w[:, k, c * P:(c + 1) * P])
                used(None)

            def proj_r():
                w = weights(W)
                for t in range(NT):
                    r_tile(w, t, W)
                used(None)

            pe.wait_ge(S("cst_landed"), 16)
            pe.wait_ge(S("rows_landed"), 16 * 12)
            pe.transpose(ps[6][:, 0:NROW], rows[:, :], ident[0:NROW, 0:NROW]).then_inc(S("rows_T"), 1)
            pe.wait_ge(S("btab_landed"), 48)
            pe.matmul(aux[0][0:2 * HEADS, :], relb[:, :], btab[:, 0:T], start=True, stop=True)
            pe.matmul(aux[1][0:2 * HEADS, 0:P], relb[:, :], btab[:, T:T + P], start=True, stop=True
                      ).then_inc(S("bias_mm"), 1)
            pe.wait_ge(S("xs_ready"), NT)
            for c in range(KD):
                b = main_bank()
                for t in range(NT):
                    last = pe.transpose(b[:, t * P:(t + 1) * P], xs[:, t, c * P:(c + 1) * P], ident)
                main_full(last)
            pe.wait_ge(S("main_empty"), MEND["xT"])
            w = weights(164)
            t_tile(lambda k: w[:, k, 0:P])
            pe.wait_ge(S("ikrep_ready"), 1)
            t_tile(lambda k: rel[:, :, :].rearrange("p a b -> p (a b)")[:, k * P:(k + 1) * P])
            b = main_bank()
            for t in range(NT):
                for k in range(KD):
                    last = pe.matmul(b[:, t * IDX_HEADS:(t + 1) * IDX_HEADS], xnT[:, k, t * P:(t + 1) * P], w[:, k, 160:164],
                                     start=(k == 0), stop=(k == KD - 1))
            main_full(last)
            used(None)
            proj_t()
            pe.wait_ge(S("main_empty"), MEND["iw"])
            n = 0
            for i in range(1, NT):
                for h in range(IDX_HEADS):
                    if n >= 2:
                        pe.wait_ge(S("rel_ready"), n - 1)
                    r = slice(IDX_DIM * h, IDX_DIM * (h + 1))
                    pe.matmul(lgb[n % 2][:, 0:(i + 1) * P], iqT[r, i * P:(i + 1) * P], ikT[r, 0:(i + 1) * P],
                              start=True, stop=True).then_inc(S("idx_full"), 1)
                    n += 1
            proj_t()
            pe.wait_ge(S("bd_landed"), 16 * 20)
            pe.wait_ge(S("xc_ready"), 1)
            pe.wait_ge(S("bias_rows_ready"), 2)
            n = 0
            for m in range(2):
                for c in range(KW):
                    if n >= 2:
                        pe.wait_ge(S("lru_tanh"), n - 1)
                    ks = [k for k in range(KW) if abs(k - c) <= 1]
                    for k in ks:
                        last = pe.matmul(aux[n % 2][:, :], bd[:, m, k, c * P:(c + 1) * P], xc[:, k, :],
                                         start=(k == ks[0]), stop=(k == ks[-1]))
                    last.then_inc(S("lru_full"), 1)
                    n += 1
            w = weights(A_RANK)
            t_tile(lambda k: w[:, k, :], A_RANK)
            used(None)
            weights(W)
            pe.wait_ge(S("wqk_ready"), 1)
            wflat = wqk.rearrange("p k h c -> p k (h c)")
            for c in range(4):
                t_tile(lambda k, c=c: wflat[:, k, c * P:(c + 1) * P])
            used(None)
            pe.wait_ge(S("wa2_landed"), 64)
            pe.wait_ge(S("main_empty"), MEND["alr"])
            pe.wait_ge(S("cols_ready"), 1)
            for i in range(2):
                pe.matmul(ps[6 + i][:, :], wa2[:, i * P:(i + 1) * P], alrT[0:A_RANK, :], start=True, stop=True
                          ).then_inc(S("z_full"), 1)
            proj_r()
            proj_r()
            proj_t()
            proj_t()
            pe.wait_ge(S("ke_T"), 1)
            pe.wait_ge(S("zb_ready"), 2)
            for i in range(2):
                for t in range(NT):
                    last = pe.transpose(ps[6 + i][:, t * P:(t + 1) * P], akT[:, i, t * P:(t + 1) * P], ident)
                last.then_inc(S("ke_full"), 1)
            proj_r()
            pe.wait_ge(S("ke_ready"), 2)
            pe.wait_ge(S("main_empty"), MEND["av"])
            pe.wait_ge(S("rel_ready"), 12)
            for i in range(2):
                if i:
                    pe.wait_ge(S("u_used"), 1)
                for ch in range(NCH):
                    t, r, c = ch // 2, (ch % 2) * A_CHUNK, ch // 2
                    for hh in range(2):
                        h = 2 * i + hh
                        last = pe.matmul(lgb[ch % 2][64 * hh:64 * hh + 64, c * A_DV:(c + 1) * A_DV],
                                         keR[r:r + A_CHUNK, t, h * 64:h * 64 + 64],
                                         av[r:r + A_CHUNK, t, h * A_DV:(h + 1) * A_DV], start=True, stop=True,
                                         skip_group_check=True)
                last.then_inc(S("u_full"), 1)
            pe.wait_ge(S("qk_ready"), 1)
            pe.wait_ge(S("lru_tanh"), 6)

            def gla_att(t):
                if t >= 2:
                    pe.wait_ge(S("attm_ready"), 2 * (t - 1))
                for h in range(A_HEADS):
                    r = slice(64 * (h % 2), 64 * (h % 2) + 64)
                    c0 = (h // 2) * P
                    last = pe.matmul(att_bank[t % 2][h % 2][:, c0:c0 + P], kd[r, h // 2, t * P:(t + 1) * P],
                                     aqT[r, h // 2, t * P:(t + 1) * P], start=True, stop=True, skip_group_check=True)
                last.then_inc(S("att_full"), 1)

            def gla_out(t):
                pe.wait_ge(S("attm_ready"), 2 * (t + 1))
                if t >= 2:
                    pe.wait_ge(S("oa_copied"), 2 * (t - 1))
                for h in range(A_HEADS):
                    i, r0 = h // 2, 64 * (h % 2)
                    b = oa_bank[t % 2][h % 2]
                    cs, vs = slice(i * A_DV, (i + 1) * A_DV), slice(h * A_DV, (h + 1) * A_DV)
                    last = pe.matmul(b[:, cs], attm[:, t % 2, h, :], av[:, t, vs], start=True, stop=False, skip_group_check=True)
                    for hf in range(2):
                        ch = 2 * t + hf
                        if ch == 0:
                            continue
                        last = pe.matmul(b[64 * hf:64 * hf + 64, cs], aqT[r0:r0 + 64, i, ch * A_CHUNK:(ch + 1) * A_CHUNK],
                                         St[r0:r0 + 64, i, ch, :], start=False, stop=True, skip_group_check=True)
                last.then_inc(S("oa_full"), 1)
                pe.drain().then_inc(S("gla_pe_done"), 1)

            pe.wait_ge(S("main_empty"), MEND["bv"])
            gla_att(0)
            pe.wait_ge(S("u_used"), 2)
            for t in range(NT):
                if t + 1 < NT:
                    gla_att(t + 1)
                gla_out(t)
            proj_t()
            proj_t()
            proj_r()

            def to_T(src):
                for c in range(KW):
                    b = main_bank()
                    for t in range(NT):
                        last = pe.transpose(b[:, t * P:(t + 1) * P], src[:, t, c * P:(c + 1) * P], ident)
                    main_full(last)

            pe.wait_ge(S("oa_ready"), 1)
            to_T(oA)

            def unit(n):
                br, i, h = n // (NT * HEADS), (n // HEADS) % NT, n % HEADS
                q, k, v = ((cqT, ckT, cv), (bqT, bkT, bv))[br]
                return br, i, h, q, k, v

            def logits(n):
                br, i, h, q, k, v = unit(n)
                if n >= 2:
                    pe.wait_ge(S("lg_read"), n - 1)
                r = slice(64 * (h % 2), 64 * (h % 2) + 64)
                pe.matmul(lgb[n % 2][:, 0:(i + 1) * P], q[r, h // 2, i * P:(i + 1) * P], k[r, h // 2, 0:(i + 1) * P],
                          start=True, stop=True).then_inc(S("lg_full"), 1)

            def transp(n):
                br, i, h, q, k, v = unit(n)
                pe.wait_ge(S("p_ready"), n + 1)
                if n >= 2:
                    pe.wait_ge(S("pT_ready"), n - 1)
                for b in range(i + 1):
                    last = pe.transpose(aux[n % 2][:, b * P:(b + 1) * P], pr[:, n % 2, b * P:(b + 1) * P], ident)
                last.then_inc(S("pT_full"), 1)
                pe.drain().then_inc(S("p_used"), 1)

            def attend(n):
                br, i, h, q, k, v = unit(n)
                pe.wait_ge(S("pT_ready"), n + 1)
                g = n // HEADS
                if h == 0 and g >= 2:
                    pe.wait_ge(S("o_done"), g - 1)
                for b in range(i + 1):
                    last = pe.matmul(ps[6 + g % 2][:, h * HD:(h + 1) * HD], pT[:, n % 2, b * P:(b + 1) * P],
                                     v[:, b, h * HD:(h + 1) * HD], start=(b == 0), stop=(b == i), skip_group_check=True)
                last.then_inc(S("pT_used"), 1)

            units = 2 * NT * HEADS
            pe.wait_ge(S("main_empty"), MEND["cv"])
            pe.wait_ge(S("u_used"), 2)
            pe.wait_ge(S("attm_ready"), 2 * NT)
            pe.wait_ge(S("oa_copied"), 2 * NT)
            for n in range(units + 2):
                if n < units:
                    logits(n)
                if 1 <= n <= units:
                    transp(n - 1)
                if n >= 2:
                    attend(n - 2)
            pe.wait_ge(S("o_done"), NT)
            to_T(oR[1])
            pe.wait_ge(S("o_done"), 2 * NT)
            to_T(oR[0])
            pe.wait_ge(S("main_empty"), MEND["oTb"])
            n = 0
            for mc in range(NMC):
                for b_ in range(NBR):
                    wait_load(pe, state["load"])
                    slot = ring[state["load"] % RING]
                    wgt = slot[:, 0:KD * MCOLS].rearrange("p (k n) -> p k n", n=MCOLS)
                    wbr = slot[:, KD * MCOLS:(KD + KW) * MCOLS].rearrange("p (k n) -> p k n", n=MCOLS)
                    for j in range(MCOLS // P):
                        t_tile(lambda k, j=j: wgt[:, k, j * P:(j + 1) * P])
                        if n >= 2:
                            pe.wait_ge(S("merge_done"), n - 1)
                        for k in range(KW):
                            last = pe.matmul(aux[n % 2][:, :], wbr[:, k, j * P:(j + 1) * P], oT[b_][:, k, :],
                                             start=(k == 0), stop=(k == KW - 1))
                        last.then_inc(S("br_full"), 1)
                        n += 1
                    used(None)
            pe.wait_ge(S("merge_done"), 4 * KD)
            n = 0
            for mc in range(NMC):
                w = weights(MCOLS)
                for t in range(NT):
                    if n >= 2:
                        pe.wait_ge(S("h_done"), n - 1)
                    for k in range(KD):
                        last = pe.matmul(lgb[n % 2][:, 0:MCOLS], merged[:, k, t * P:(t + 1) * P], w[:, k, :],
                                         start=(k == 0), stop=(k == KD - 1))
                    last.then_inc(S("out_full"), 1)
                    n += 1
                used(None)
            pe.wait_ge(S("xs_ready"), 2 * NT)
            for c in range(KD):
                b = main_bank()
                for t in range(NT):
                    last = pe.transpose(b[:, t * P:(t + 1) * P], xs[:, t, c * P:(c + 1) * P], ident)
                main_full(last)
            pe.wait_ge(S("main_empty"), MEND["x2T"])
            pe.wait_ge(S("wr_landed"), 64)
            nr = GROUPS + NE
            for t in range(NT):
                for k in range(KD):
                    last = pe.matmul(ps[6][:, t * nr:(t + 1) * nr], xnT[:, k, t * P:(t + 1) * P], wr[:, k, :],
                                     start=(k == 0), stop=(k == KD - 1))
            last.then_inc(S("rt_full"), 1)
            n = y = 0
            for e in range(NE):
                s = e % 2
                pe.wait_ge(S(f"e_landed{s}"), 48 * (e // 2 + 1))
                for m in range(KH):
                    if n >= 2:
                        pe.wait_ge(S("hT_ready"), n - 1)
                    for k in range(KD):
                        pe.matmul(ps[n % 2][:, :], wg[s][:, k, m * P:(m + 1) * P], xnT[:, k, :], start=(k == 0), stop=(k == KD - 1))
                    for k in range(KD):
                        last = pe.matmul(ps[2 + n % 2][:, :], wu[s][:, k, m * P:(m + 1) * P], xnT[:, k, :],
                                         start=(k == 0), stop=(k == KD - 1))
                    last.then_inc(S("gu_full"), 1)
                    n += 1
                pe.wait_ge(S("hT_ready"), n)
                if e == 0:
                    pe.wait_ge(S("rt_read"), 1)
                for t in range(NT):
                    for hf in range(2):
                        if y >= 4:
                            pe.wait_ge(S("acc_done"), y - 3)
                        for k in range(KH):
                            last = pe.matmul(ps[4 + y % 4][:, :], hT[:, k, t * P:(t + 1) * P], wd[s][:, k, hf * 512:(hf + 1) * 512],
                                             start=(k == 0), stop=(k == KH - 1))
                        last.then_inc(S("y_full"), 1)
                        y += 1
                pe.drain().then_inc(S("e_used"), 1)

        @block.vector
        def _(dve):
            state = {"step": 0, "sig": {}}

            def link(ins):
                state["step"] += 1
                ins.then_inc(S("dve_step"), 1)
                dve.wait_ge(S("dve_step"), state["step"])

            def sig(name, ins):
                n = state["sig"][name] = state["sig"].get(name, 0) + 1
                ins.then_inc(S(name), 1)
                dve.wait_ge(S(name), n)

            ts, tt, stt = dve.tensor_scalar, dve.tensor_tensor, dve.scalar_tensor_tensor

            def flat(v):
                s = v.shape
                if len(s) == 3:
                    return v.rearrange("p a b -> p (a b)")
                return v

            dve.memset(ones[:, :], 1.0).then_inc(S("memsets"), 1)
            dve.memset(seg, 1.0).then_inc(S("memsets"), 1)
            dve.memset(dxp[:, :, 0:3], 0.0).then_inc(S("memsets"), 1)
            dve.wait_ge(S("memsets"), 3)
            link(dve.memset(seg.rearrange("p (a b) -> p a b", b=A_CHUNK)[:, :, 0:1], 0.0))

            def norm_scale(src, count):
                dve.wait_ge(S("ss_ready"), NT * count)
                sig("ms_ready", ts(stat[:, 1, :], stat[:, 0, :], 1.0 / D, EPS, ALU.mult, ALU.add))
                dve.wait_ge(S("rms_ready"), count)
                link(dve.reciprocal(stat[:, 3, :], stat[:, 2, :]))

            norm_scale(xs, 1)
            for t in range(NT):
                sig("xs_ready", ts(xs[:, t, :], xs[:, t, :], stat[:, 3, t:t + 1], None, ALU.mult))
            dve.wait_ge(S("rows_T"), 1)
            sig("cols_ready", dve.tensor_copy(cols[:, :], ps[6][:, 0:NROW]))
            link(ts(half[:, 0:32], c_bgate, 0.5, None, ALU.mult))
            sig("cols_ready", ts(half[:, 32:38], cols[:, 63:69], 0.5, None, ALU.mult))
            link(ts(sp[:, 0, :], c_lam, -1.0, None, ALU.mult))
            sig("lam_abs", tt(sp[:, 0, :], sp[:, 0, :], c_lam, ALU.min))
            dve.wait_ge(S("bias_mm"), 1)
            sig("bias_rows_ready", dve.tensor_copy(bias_rows[:, 0:T], aux[0][0:2 * HEADS, :]))
            sig("bias_rows_ready", dve.tensor_copy(bias_rows[:, T:T + P], aux[1][0:2 * HEADS, 0:P]))
            wait_load(dve, 0)
            iks = ring[0][:, 0:KD * 164].rearrange("p (k n) -> p k n", n=164)[:, :, P:P + IDX_DIM]
            repv = rel[:, :, :].rearrange("p a b -> p (a b)").rearrange("p (k h c) -> p k h c", h=IDX_HEADS, c=IDX_DIM)
            for h in range(IDX_HEADS - 1):
                dve.tensor_copy(repv[:, :, h, :], iks)
            sig("ikrep_ready", dve.tensor_copy(repv[:, :, IDX_HEADS - 1, :], iks))
            dve.wait_ge(S("lam_exp"), 1)
            e_, z_, z2, pl = sp[:, 1, :], sp[:, 2, :], sp[:, 3, :], sp[:, 4, :]
            link(ts(z_, e_, 2.0, None, ALU.add))
            link(dve.reciprocal(z_, z_))
            link(tt(z_, z_, e_, ALU.mult))
            link(tt(z2, z_, z_, ALU.mult))
            link(ts(pl, z2, 1.0 / 19, 1.0 / 17, ALU.mult, ALU.add))
            for o in (15, 13, 11, 9, 7, 5, 3, 1):
                link(tt(pl, pl, z2, ALU.mult))
                link(ts(pl, pl, 1.0 / o, None, ALU.add))
            link(tt(pl, pl, z_, ALU.mult))
            link(ts(sp[:, 5, :], c_lam, -1.0, 0.0, ALU.mult, ALU.max))
            link(stt(sp[:, 6, :], pl, 2.0, sp[:, 5, :], ALU.mult, ALU.add))
            sig("sp_ready", ts(sp[:, 7, :], sp[:, 6, :], LRU_C / 4, None, ALU.mult))
            dve.wait_ge(S("main_empty"), MEND["dx"])
            for c in range(KW):
                link(ts(xc[:, c, :], dxp[:, c, 3:3 + T], c_convw[:, 9 + c:10 + c], c_convb[:, c:c + 1], ALU.mult, ALU.add))
                for j in range(3):
                    ins = stt(xc[:, c, :], dxp[:, c, j:j + T], c_convw[:, 3 * j + c:3 * j + c + 1], xc[:, c, :], ALU.mult, ALU.add)
                    if c == KW - 1 and j == 2:
                        sig("xc_ready", ins)
                    else:
                        link(ins)
            n = 0
            for i in range(1, NT):
                nk = (i + 1) * P
                for h in range(IDX_HEADS):
                    dve.wait_ge(S("rel_ready"), n + 1)
                    w1 = iw[:, i, h:h + 1]
                    if h == 0:
                        ins = ts(sel[i], rel[:, n % 2, 0:nk], w1, None, ALU.mult)
                    else:
                        ins = stt(sel[i], rel[:, n % 2, 0:nk], w1, sel[i], ALU.mult, ALU.add)
                    sig("rel_used", ins)
                    n += 1
                link(tt(sel[i][:, i * P:nk], sel[i][:, i * P:nk], future, ALU.add))

            def topk(i):
                for _ in range(TOPK // 8):
                    link(dve.max(out=m8[:, :], in_=sel[i]))
                    link(dve.match_replace(out=sel[i], in_to_replace=m8[:, :], in_values=sel[i], imm_value=TAKEN))
                link(ts(sel[i], sel[i], -2e38, BIG, ALU.is_gt, ALU.mult))

            wait_load(dve, 4)
            dve.wait_ge(S("main_full"), MEND["xT"])
            dve.wait_ge(S("main_empty"), MEND["xT"])
            link(dve.memset(wqk.rearrange("p k h c -> p (k h c)"), 0.0))
            src = ring[4 % RING][:, 0:KD * W].rearrange("p (k h c) -> p k h c", h=8, c=A_DK)
            sig("wqk_ready", dve.tensor_copy(wqk[:, :, :, 0:A_DK].rearrange("p k h c -> p (k h) c"),
                                             src.rearrange("p k h c -> p (k h) c")))
            topk(1)
            dve.wait_ge(S("lru_sqrt"), 1)
            link(ts(flat(tr), flat(tr), 1.0, None, ALU.add))
            link(dve.reciprocal(flat(tr), flat(tr)))
            dve.wait_ge(S("lru_tanh"), 6)
            link(stt(flat(ti), flat(ti), 1.0, flat(xc), ALU.add, ALU.mult))
            link(tt(flat(ti), flat(ti), flat(tr), ALU.mult))
            sig("lru_u", tt(flat(ti), flat(ti), flat(sq_), ALU.mult))
            link(ts(flat(tr), flat(tr), 2.0, -1.0, ALU.mult, ALU.add))
            for c in range(KW):
                link(dve.tensor_tensor_scan(out=xc[:, c, :], data0=tr[:, c, :], data1=ti[:, c, :], initial=0.0,
                                            op0=ALU.mult, op1=ALU.add))
            dve.wait_ge(S("z_full"), 2)
            for i in range(2):
                sig("zb_ready", ts(zb[:, i, :], ps[6 + i][:, :], c_b2[:, i:i + 1], None, ALU.add))
            link(ts(flat(na), flat(zb), -1.0, None, ALU.mult))
            sig("gla_na", tt(flat(na), flat(na), flat(zb), ALU.min))
            dve.wait_ge(S("gla_ln"), 1)
            link(stt(flat(zb), flat(zb), 0.0, flat(na), ALU.min, ALU.subtract))
            sig("gla_b", dve.tensor_tensor_scan(out=flat(b16), data0=seg, data1=flat(zb), initial=0.0,
                                                op0=ALU.mult, op1=ALU.add))
            dve.wait_ge(S("y2_ready"), 1)
            link(ts(flat(sq_), flat(sq_), 0.044715, 1.0, ALU.mult, ALU.add))
            sig("gelu_in", tt(flat(sq_), flat(sq_), flat(dyT), ALU.mult))
            b4 = flat(b16).rearrange("p (n c) -> p n c", c=A_CHUNK)
            e4 = flat(ek).rearrange("p (n c) -> p n c", c=A_CHUNK)
            sig("gla_d", tt(e4, b4[:, :, A_CHUNK - 1:A_CHUNK].to_broadcast([P, 2 * NCH, A_CHUNK]), b4, ALU.subtract))
            dve.wait_ge(S("gelu_tanh"), 1)
            link(stt(flat(sq_), flat(sq_), 1.0, flat(dyT), ALU.add, ALU.mult))
            sig("lru_u", stt(flat(oTd), flat(sq_), 0.5, flat(xc), ALU.mult, ALU.mult))
            dve.wait_ge(S("main_empty"), MEND["aqk"])
            dve.wait_ge(S("gla_e"), 3)
            link(tt(flat(kd), flat(kd), flat(akT), ALU.mult))
            sig("ke_T", tt(flat(akT), flat(akT), flat(ek), ALU.mult))
            sig("qk_ready", tt(flat(aqT), flat(aqT), flat(eb), ALU.mult))
            link(dve.memset(St[:, :, 0, :], 0.0))
            topk(2)
            for i in range(2):
                dve.wait_ge(S("u_full"), i + 1)
                for ch in range(NCH):
                    ins = stt(St[:, i, ch + 1, :], St[:, i, ch, :], eb[:, i, ch * A_CHUNK + A_CHUNK - 1:(ch + 1) * A_CHUNK],
                              lgb[ch % 2][:, (ch // 2) * A_DV:(ch // 2 + 1) * A_DV], ALU.mult, ALU.add)
                    if ch == NCH - 1:
                        sig("u_used", ins)
                    else:
                        link(ins)
            for t in range(NT):
                dve.wait_ge(S("att_full"), t + 1)
                if t >= 2:
                    dve.wait_ge(S("gla_pe_done"), t - 1)
                for hh in range(2):
                    sig("attm_ready", tt(attm[:, t % 2, :, :].rearrange("p (i h) c -> p i h c", h=2)[:, :, hh, :],
                                         att_bank[t % 2][hh][:, 0:2 * P].rearrange("p (i c) -> p i c", c=P),
                                         glamask.unsqueeze(1).to_broadcast([P, 2, P]), ALU.mult))
            dve.wait_ge(S("oa_sq"), 1)
            link(dve.tensor_reduce(ostat[:, :], flat(oA2).rearrange("p (n v) -> p n v", v=A_DV), axis=AX.X, op=ALU.add))
            sig("oa_ms", ts(ostat[:, :], ostat[:, :], 1.0 / A_DV, EPS, ALU.mult, ALU.add))
            dve.wait_ge(S("oa_rms"), 1)
            link(dve.reciprocal(ostat[:, :], ostat[:, :]))
            o3 = flat(oA).rearrange("p (n v) -> p n v", v=A_DV)
            sig("oa_mean", tt(o3, o3, ostat[:, :].unsqueeze(2).to_broadcast([P, NT * A_HEADS, A_DV]), ALU.mult))
            dve.wait_ge(S("gain_landed"), 16)
            link(tt(oA, oA, gain[:, :].unsqueeze(1).to_broadcast([P, NT, W]), ALU.mult))
            dve.wait_ge(S("oa_tanh"), 1)
            link(stt(flat(oA2), flat(oA2), 1.0, flat(ag), ALU.add, ALU.mult))
            sig("oa_ready", stt(flat(oA), flat(oA2), 0.5, flat(oA), ALU.mult, ALU.mult))
            topk(3)
            dve.wait_ge(S("bias_landed"), 16)
            units = 2 * NT * HEADS

            def scores(n):
                br, i, h = n // (NT * HEADS), (n // HEADS) % NT, n % HEADS
                nk = (i + 1) * P
                head = h if br else HEADS + h
                dve.wait_ge(S("lg_full"), n + 1)
                if n >= 2:
                    dve.wait_ge(S("p_ready"), n - 1)
                l = lg[:, n % 2, 0:nk]
                sig("lg_read", tt(l, lgb[n % 2][:, 0:nk], bias[:, head, T - nk:T], ALU.add))
                if br and i:
                    link(tt(l, l, sel[i], ALU.add))
                sig("lg_ready", dve.tensor_reduce(nmx[:, n % 4:n % 4 + 1], l, axis=AX.X, op=ALU.max, negate=True))

            def finish(g):
                br, i = g // NT, g % NT
                dve.wait_ge(S("p_ready"), (g + 1) * HEADS)
                sig("rl_ready", dve.reciprocal(rl[:, g % 2, :], lsum[:, g % 2, :]))
                dve.wait_ge(S("pT_used"), (g + 1) * HEADS)
                if g == 0:
                    dve.wait_ge(S("main_empty"), MEND["oTa"])
                sig("o_done", tt(oR[0 if br else 1][:, i, :].rearrange("p (h c) -> p h c", c=HD),
                                 ps[6 + g % 2][:, 0:W].rearrange("p (h c) -> p h c", c=HD),
                                 rl[:, g % 2, :].unsqueeze(2).to_broadcast([P, HEADS, HD]), ALU.mult))

            for n in range(units):
                scores(n)
                if n % HEADS == 3 and n > HEADS:
                    finish(n // HEADS - 1)
            finish(2 * NT - 1)
            n = 0
            for mc in range(NMC):
                for b_ in range(NBR):
                    for j in range(MCOLS // P):
                        m = mc * (MCOLS // P) + j
                        dve.wait_ge(S("br_full"), n + 1)
                        dve.wait_ge(S("main_empty"), MEND["oTb"] + n + 1)
                        if b_ == 0:
                            sig("merge_done", stt(merged[:, m, :], gate_t[:, n % 2, :], 1.0, aux[n % 2][:, :], ALU.add, ALU.mult))
                        else:
                            link(stt(gterm, gate_t[:, n % 2, :], 1.0, aux[n % 2][:, :], ALU.add, ALU.mult))
                            sig("merge_done", tt(merged[:, m, :], merged[:, m, :], gterm, ALU.add))
                        n += 1
            dve.wait_ge(S("xres_landed"), 16)
            n = 0
            for mc in range(NMC):
                for t in range(NT):
                    dve.wait_ge(S("out_full"), n + 1)
                    h_ = hres[:, t, mc * MCOLS:(mc + 1) * MCOLS]
                    sig("h_done", stt(h_, lgb[n % 2][:, 0:MCOLS], 0.5, h_, ALU.mult, ALU.add))
                    n += 1
            norm_scale(hres, 2)
            for t in range(NT):
                sig("xs_ready", ts(xs[:, t, :], hres[:, t, :], stat[:, 3, t:t + 1], None, ALU.mult))
            dve.wait_ge(S("rt_full"), 1)
            nr = GROUPS + NE
            sig("rt_read", tt(rlog[:, :, :], ps[6][:, 0:NT * nr].rearrange("p (t n) -> p t n", n=nr),
                              rbias[:, :].unsqueeze(1).to_broadcast([P, NT, nr]), ALU.add))
            gl = rlog[:, :, 0:GROUPS]

            def R(i):
                return rt[:, i, :, :]

            def R1(i, j=0):
                return rt[:, i, :, j:j + 1]

            def wide(x):
                return x.to_broadcast([P, NT, 4])

            def argmax(dst, src, mx, tmp):
                link(dve.tensor_reduce(mx, src, axis=AX.X, op=ALU.max))
                link(tt(dst, src, wide(mx), ALU.is_equal))
                link(tt(dst, dst, prio.unsqueeze(1).to_broadcast([P, NT, 4]), ALU.mult))
                link(dve.tensor_reduce(tmp, dst, axis=AX.X, op=ALU.max))
                link(tt(dst, dst, wide(tmp), ALU.is_equal))

            argmax(R(3), gl, R1(0), R1(0, 1))
            sig("rt_sub", tt(R(1), gl, wide(R1(0)), ALU.subtract))
            link(tt(R(4), rlog[:, :, GROUPS:GROUPS + EPG], wide(R1(3, 0)), ALU.mult))
            for g in range(1, GROUPS):
                link(tt(R(5), rlog[:, :, GROUPS + g * EPG:GROUPS + (g + 1) * EPG], wide(R1(3, g)), ALU.mult))
                link(tt(R(4), R(4), R(5), ALU.add))
            argmax(R(6), R(4), R1(7, 0), R1(0, 1))
            link(ts(R(5), R(6), BIG, None, ALU.mult))
            link(tt(R(5), R(5), R(4), ALU.add))
            argmax(R(10), R(5), R1(7, 1), R1(0, 1))
            sig("rt_diff", tt(R1(8), R1(7, 1), R1(7, 0), ALU.subtract))
            dve.wait_ge(S("rt_exp"), 2)
            link(dve.tensor_reduce(R1(11), R(2), axis=AX.X, op=ALU.add))
            link(dve.reciprocal(R1(11), R1(11)))
            link(ts(R1(12), R1(9), 1.0, None, ALU.add))
            link(dve.reciprocal(R1(12), R1(12)))
            link(tt(R1(12), R1(12), R1(11), ALU.mult))
            link(tt(R1(13), R1(12), R1(9), ALU.mult))
            link(tt(R(6), R(6), wide(R1(12)), ALU.mult))
            link(tt(R(10), R(10), wide(R1(13)), ALU.mult))
            link(tt(R(6), R(6), R(10), ALU.add))
            link(ts(R(6), R(6), 0.5, None, ALU.mult))
            for g in range(GROUPS):
                link(tt(gates[:, :, g * EPG:(g + 1) * EPG], R(6), wide(R1(3, g)), ALU.mult))
            n = y = 0
            for e in range(NE):
                for m in range(KH):
                    dve.wait_ge(S("sg_ready"), n + 1)
                    if m == 0 and e >= 1:
                        dve.wait_ge(S("e_used"), e)
                    link(stt(sg[:, n % 2, :], sg[:, n % 2, :], 1.0, ps[n % 2][:, :], ALU.add, ALU.mult))
                    sig("hT_ready", tt(hT[:, m, :], sg[:, n % 2, :], ps[2 + n % 2][:, :], ALU.mult))
                    n += 1
                for t in range(NT):
                    for hf in range(2):
                        dve.wait_ge(S("y_full"), y + 1)
                        h_ = hres[:, t, hf * 512:(hf + 1) * 512]
                        sig("acc_done", stt(h_, ps[4 + y % 4][:, :], gates[:, t, e:e + 1], h_, ALU.mult, ALU.add))
                        y += 1
            norm_scale(hres, 3)
            dve.wait_ge(S("nf_landed"), 16)
            for t in range(NT):
                sig("y_done", stt(onorm[:, t, :], hres[:, t, :], stat[:, 3, t:t + 1], nf, ALU.mult, ALU.mult))


_INS = ["x", "w_in", "a_w2", "a_b2", "a_gain", "conv_w", "conv_b", "lru_wr", "lru_br", "lru_wi", "lru_bi", "lru_lambda",
        "w_gate", "b_gate", "w_branch", "w_out", "rel_bias", "norm1", "norm2", "norm_f", "moe_wrg", "moe_brg",
        "moe_wre", "moe_bre", "moe_wg", "moe_wu", "moe_wd"]


def kernel(**inputs):
    import concourse.bacc as _bacc
    from concourse.bass_utils import run_bass_kernel_spmd as _run

    nc = _bacc.Bacc("TRN2", target_bir_lowering=False, num_devices=1)
    arrays, d = {}, {}
    given = {n: np.ascontiguousarray(inputs[n]) for n in _INS}
    given.update(zip(("c_sq", "c_tab", "c_sel"), constants()))
    for name, a in given.items():
        arrays[f"in_{name}"] = a
        d[name] = nc.dram_tensor(f"in_{name}", a.shape, mybir.dt.from_np(a.dtype), kind="ExternalInput").ap()
    d["bias_scratch"] = nc.dram_tensor("bias_scratch", (2 * HEADS, P, T + P), F32, kind="Internal").ap()
    out = nc.dram_tensor("out_0", (1, T, D), F32, kind="ExternalOutput").ap()
    build(nc, d, out)
    r = _run(nc, [arrays], core_ids=[0])
    return r.results[0]["out_0"]
```

```python
import math
from contextlib import ExitStack

import numpy as np
import concourse.bass as bass
from concourse import mybir

F32 = mybir.dt.float32
F16 = mybir.dt.float16
U32 = mybir.dt.uint32
I32 = mybir.dt.int32
ALU = mybir.AluOpType
ACT = mybir.ActivationFunctionType
AX = mybir.AxisListType

P = 128
T = 512
NT = T // P
D = 1024
KD = D // P
EPS = 1e-6
A_HEADS, A_DK, A_DV, A_RANK, A_TAU, A_CHUNK = 4, 48, 96, 16, 16.0, 64
NCH = T // A_CHUNK
HEADS, HD = 6, 64
IDX_HEADS, IDX_DIM = 4, 32
TOPK = 128
PATTERNS = ((128, 1), (512, 4), (2048, 16))
W = 384
KW = W // P
LRU_BLOCKS = 8
LRU_C = 8.0
BUCKETS, MAX_DIST = 32, 2048
NBR = 4
GROUPS, EPG = 4, 4
NE = GROUPS * EPG
HID = 512
KH = HID // P
CAP = P
NEC = 6
CHUNK = 2048
WSCALE = 64.0
HSCALE = 1.0 / 16
AHEAD = 4
BIG = -1e30
TAKEN = -3e38
GELU_C = math.sqrt(2.0 / math.pi)

SPLITS = (("aq", 192), ("ak", 192), ("av", 384), ("ag", 384), ("alr", 16), ("bq", 384), ("bk", 384), ("bv", 384),
          ("iq", 128), ("ik", 32), ("iw", 4), ("cq", 384), ("ck", 384), ("cv", 384), ("dy", 384), ("dx", 384))
COL0 = {}
_c = 0
for _n, _w in SPLITS:
    COL0[_n] = _c
    _c += _w

PROJ = (("idx", "iq", 164), ("dx", "dx", 384), ("dy", "dy", 384), ("alr", "alr", 16), ("aqk", "aq", 384),
        ("av", "av", 384), ("ag", "ag", 384), ("bq", "bq", 384), ("bk", "bk", 384), ("bv", "bv", 384),
        ("cq", "cq", 384), ("ck", "ck", 384), ("cv", "cv", 384))
MCOLS = 256
NMC = D // MCOLS
LOADS = ([("proj", n, COL0[c], w) for n, c, w in PROJ]
         + [("merge", b, mc * MCOLS, MCOLS) for mc in range(NMC) for b in range(NBR)]
         + [("out", 0, mc * MCOLS, MCOLS) for mc in range(NMC)])
RING = 3
SLOT = KD * W

MAIN = (("xT", 8), ("iq", 1), ("ik", 1), ("iw", 1), ("dx", 3), ("dy", 3), ("alr", 1), ("aqk", 4), ("av", 4),
        ("ag", 4), ("bq", 3), ("bk", 3), ("bv", 4), ("cq", 3), ("ck", 3), ("cv", 4), ("oTa", 3), ("oTc", 3),
        ("oTb", 3), ("gate", 32), ("x2T", 8))
MEND = {}
_c = 0
for _n, _w in MAIN:
    _c += _w
    MEND[_n] = _c


STEPS = []
for _e in range(NE + 1):
    if _e < NE:
        STEPS += [("g", _e, 0), ("g", _e, 1), ("u", _e, 0), ("u", _e, 1)]
    if _e >= 1:
        STEPS += [("d", _e - 1, 0), ("d", _e - 1, 1)]


def load_index(kind, name, col=None):
    for i, l in enumerate(LOADS):
        if l[0] == kind and l[1] == name and (col is None or l[2] == col):
            return i
    raise KeyError((kind, name))


def rel_bucket(dist):
    exact = BUCKETS // 2
    if dist < exact:
        return dist
    big = exact + int(np.float32(np.log(np.float32(dist) / np.float32(exact)) / np.float32(math.log(MAX_DIST / exact))
                                 * np.float32(BUCKETS - exact)))
    return min(big, BUCKETS - 1)


NCST = 6 * P + 24


def constants():
    sq = np.zeros((P, NCST), np.float32)
    sq[:, 0:P] = np.eye(P)
    r = np.arange(P)
    same = (r[:, None] // A_CHUNK) == (r[None, :] // A_CHUNK)
    sq[:, P:2 * P] = same & (r[None, :] >= r[:, None])
    sq[:, 2 * P:3 * P] = np.where(r[None, :] > r[:, None], BIG, 0.0)
    sq[:, 3 * P:3 * P + 4] = np.arange(4, 0, -1)
    sq[:, 3 * P + 4:3 * P + 8] = r[:, None] + P * np.arange(NT)[None, :]
    sq[:, 3 * P + 8:3 * P + 24] = CAP * np.arange(NE)
    sq[:, 3 * P + 24:4 * P + 24] = r
    sq[:, 4 * P + 24:5 * P + 24] = r[:, None] < r[None, :]
    sq[:, 5 * P + 24:6 * P + 24] = 1.0
    n = T + P
    tab = np.zeros((BUCKETS + 2, n), np.float32)
    for j in range(n):
        dist = T - 1 - j
        if dist < 0:
            tab[BUCKETS:, j] = BIG
            continue
        tab[rel_bucket(dist), j] = 1.0
        tab[BUCKETS + 1, j] = sum(dist % dil == 0 and dist <= win for win, dil in PATTERNS)
        c = tab[BUCKETS + 1, j]
        tab[BUCKETS + 1, j] = math.log(c) if c else BIG
    sel = np.zeros((2, 2 * HEADS), np.float32)
    sel[0, :HEADS] = 1.0
    sel[1, HEADS:] = 1.0
    return sq, tab, sel


def build(nc, d, out):
    ctx = ExitStack()
    with ctx:
        sems = {}

        def S(name):
            if name not in sems:
                sems[name] = ctx.enter_context(nc.semaphore(name))
            return sems[name]

        arena = ctx.enter_context(nc.sbuf_tensor("arena", [P, 49292], F32))

        def view(at, *shape):
            n = int(np.prod(shape))
            v = arena[:, at:at + n]
            if len(shape) == 2:
                v = v.rearrange("p (a b) -> p a b", b=shape[1])
            elif len(shape) == 3:
                v = v.rearrange("p (a b c) -> p a b c", b=shape[1], c=shape[2])
            return v

        ring = [arena[:, i * SLOT:(i + 1) * SLOT] for i in range(RING)]
        xnT = view(9216, KD, T)
        XS = 13312
        xs = view(XS, NT, D)
        wqk = view(XS, KD, 8, 64)
        oA = view(XS, NT, W)
        oA2 = view(XS + 1536, NT, W)
        keR = view(XS + 3072, NT, 2 * P)
        oR = [view(XS, NT, W), view(XS + 1536, NT, W)]
        QKB = 17408
        bd = view(QKB, 2, KW, W)
        bqT, bkT = view(QKB, KW, T), view(QKB + 1536, KW, T)
        CVR = 20480
        xc, tr, ti, sq_ = (view(CVR + 1536 * i, KW, T) for i in range(4))
        bv, cqT, ckT, cv = view(CVR, NT, W), view(CVR + 1536, KW, T), view(CVR + 3072, KW, T), view(CVR + 4608, NT, W)
        hres = view(CVR, NT, D)
        AR = 26624
        aqT, akT, av, ag = view(AR, 2, T), view(AR + 1024, 2, T), view(AR + 2048, NT, W), view(AR + 3584, NT, W)
        DR = 31744
        dxp = view(DR, KW, T + 3)
        dyT = view(DR + 1548, KW, T)
        iqT, ikT, alrT = view(DR + 3084, T), view(DR + 3596, T), view(DR + 4108, T)
        oTd = view(36364, KW, T)
        oT = [view(DR + 1548, KW, T), view(AR, KW, T), view(AR + 1536, KW, T), oTd]
        SEL0 = 37900
        sel = [None, view(SEL0, 256), view(SEL0 + 256, 384), view(SEL0 + 640, 512)]
        rel = view(39052, 2, T)
        gate_t = view(39052, 2, T)
        GR = 40076
        zb, na, b16, eb, kd, ek = (view(GR + 1024 * i, 2, T) for i in range(6))
        seg = arena[:, GR + 5120:GR + 6144]
        attm = view(GR + 6144, 2, 4, P)
        St = view(GR + 7168, 2, NCH + 1, A_DV)
        bias = view(GR, 2 * HEADS, T)
        lg, pr, pT = view(GR + 6144, 2, T), view(GR + 7168, 2, T), view(GR + 8192, 2, T)
        merged = view(GR, KD, T)
        gterm = view(SEL0, T)
        EW = [24576, 36864]
        wg = [view(a, KD, HID) for a in EW]
        wu = [view(a + 4096, KD, HID) for a in EW]
        wd = [view(a + 8192, KH, D) for a in EW]
        hT = view(0, KH, T)
        sg = view(2048, 2, T)
        onorm = view(4096, NT, D)
        STAGE = [17408, 24576, 29696, 44172, 46220, 26624, 33292, 35340]
        EARLY = 5
        SPLIT = [0, 2048, 4096, 6144, 40076, 42124, 37388]
        NS, NW = len(STAGE), len(SPLIT)
        stage = [arena[:, a:a + CHUNK] for a in STAGE]
        w_hi = [arena[:, a:a + CHUNK // 2].bitcast(F16) for a in SPLIT]
        w_lo = [arena[:, a + CHUNK // 2:a + CHUNK].bitcast(F16) for a in SPLIT]
        gain2 = arena[:, 48268:48268 + D]
        onehot = view(0, NT, CHUNK // 2).bitcast(F16)
        xg = [arena[:, 9216 + D * i:9216 + D * (i + 1)] for i in range(2)]
        xgT = [[arena[:, 11264 + 1024 * i + 512 * j:11264 + 1024 * i + 512 * (j + 1)].bitcast(F16)
                .rearrange("p (k c) -> p k c", c=P) for j in range(2)] for i in range(2)]
        yout = [arena[:, XS + D * i:XS + D * (i + 1)] for i in range(2)]
        sgr = [arena[:, XS + 2048 + HID * i:XS + 2048 + HID * (i + 1)] for i in range(2)]
        hrow = [arena[:, XS + 3072 + HID * i:XS + 3072 + HID * (i + 1)] for i in range(2)]
        hgT = [[arena[:, 19456 + 512 * i + 256 * j:19456 + 512 * i + 256 * (j + 1)].bitcast(F16)
                .rearrange("p (k c) -> p k c", c=P) for j in range(2)] for i in range(2)]
        yg = [[arena[:, STAGE[t] + D * j:STAGE[t] + D * (j + 1)] for j in range(2)] for t in range(NT)]
        nf = arena[:, 8192:8192 + D]

        def sb(name, shape):
            return ctx.enter_context(nc.sbuf_tensor(name, shape, F32))

        cst = sb("cst", [P, NCST])
        tokid, slot0 = cst[:, 3 * P + 4:3 * P + 8], cst[:, 3 * P + 8:3 * P + 24]
        slots, earlier, allones = (cst[:, i * P + 24:(i + 1) * P + 24] for i in (3, 4, 5))
        ident, glamask, future, prio = cst[:, 0:P], cst[:, P:2 * P], cst[:, 2 * P:3 * P], cst[:, 3 * P:3 * P + 4]
        btab = arena[0:BUCKETS + 2, CVR + 4608:CVR + 4608 + T + P]
        bias_rows = arena[0:2 * HEADS, CVR + 5248:CVR + 5248 + T + P]
        relb = sb("relb", [BUCKETS + 2, 2 * HEADS])
        NROW = 74
        rows = sb("rows", [NROW, P])
        cols = sb("cols", [P, NROW])
        c_norm1, c_norm2, c_bgate = cols[:, 0:8], cols[:, 8:16], cols[:, 16:48]
        c_convw, c_convb, c_br, c_bi, c_lam, c_b2 = (cols[:, 48:60], cols[:, 60:63], cols[:, 63:66], cols[:, 66:69],
                                                     cols[:, 69:72], cols[:, 72:74])
        half = sb("half", [P, 38])
        sp = sb("sp", [P, 8, 3])
        ones = sb("ones", [P, 1])
        stat = sb("stat", [P, 4, NT])
        wa2 = sb("wa2", [A_RANK, 4 * 64])
        gain = sb("gain", [P, W])
        iw = sb("iw", [P, NT, IDX_HEADS])
        m8 = sb("m8", [P, 8])
        nmx = sb("nmx", [P, 4])
        lsum = sb("lsum", [P, 2, HEADS])
        rl = sb("rl", [P, 2, HEADS])
        ostat = sb("ostat", [P, NT * A_HEADS])
        wr = sb("wr", [P, KD, GROUPS + NE])
        rbias = sb("rbias", [P, GROUPS + NE])
        rt = sb("rt", [P, 16, NT, 4])
        gates = sb("gates", [P, NT, NE])
        rlog = sb("rlog", [P, NT, GROUPS + NE])
        sel16 = sb("sel16", [P, NT, NE])
        selj = sb("selj", [P, 2, NT, NE])
        rank = sb("rank", [P, NT, NE])
        tmp16 = sb("tmp16", [P, NT, NE])
        slotf = sb("slotf", [P, 2, NT])
        total = sb("total", [P, 2])
        wsel = sb("wsel", [P, 2, NT])
        tok16 = ctx.enter_context(nc.sbuf_tensor("tok16", [P, NT], F16))
        slot_of = ctx.enter_context(nc.sbuf_tensor("slot_of", [P, 2 * NT], U32))
        token_of = ctx.enter_context(nc.sbuf_tensor("token_of", [P, NE], U32))
        dense = ctx.enter_context(nc.sbuf_tensor("dense", [1, 1], I32))

        ps = [ctx.enter_context(nc.psum_tensor(f"bank{i}", [P, 512], F32)) for i in range(8)]
        main, aux, lgb = ps[0:2], ps[2:4], ps[4:6]
        att_bank = (aux, main)
        oa_bank = ((ps[6], ps[7]), (ps[4], ps[5]))
        scratch, x2_rows, y_rows = d["bias_scratch"], d["x2_rows"], d["y_rows"]

        block = ctx.enter_context(nc.Block())

        def ring_count(i):
            return 16 * sum(2 if LOADS[j][0] == "merge" else 1 for j in range(i % RING, i + 1, RING))

        def wait_load(eng, i):
            eng.wait_ge(S(f"w_landed{i % RING}"), ring_count(i))

        @block.sync
        def _(sp_):
            for t in range(NT):
                sp_.dma_start(xs[:, t, :], d["x"][0, t * P:(t + 1) * P, :]).then_inc(S(f"x_landed{t}"), 16)
            w_in = d["w_in"][0].rearrange("(k p) n -> p k n", p=P)
            for i, (kind, name, col, width) in enumerate(LOADS):
                if kind == "merge" and (name, col) == (1, 0):
                    sp_.wait_ge(S("o_done"), 2 * NT)
                    sp_.dma_start(hres, d["x"][0].rearrange("(t p) n -> p t n", p=P)).then_inc(S("xres_landed"), 16)
                if i >= RING:
                    sp_.wait_ge(S("w_used"), i - RING + 1)
                dst = ring[i % RING][:, 0:KD * width].rearrange("p (k n) -> p k n", n=width)
                landed = S(f"w_landed{i % RING}")
                if kind == "proj":
                    src = w_in[:, :, col:col + width]
                elif kind == "merge":
                    src = d["w_gate"][0, name].rearrange("(k p) n -> p k n", p=P)[:, :, col:col + width]
                else:
                    src = d["w_out"][0].rearrange("(k p) n -> p k n", p=P)[:, :, col:col + width]
                sp_.dma_start(dst, src).then_inc(landed, 16)
                if kind == "merge":
                    dst2 = ring[i % RING][:, KD * width:(KD + KW) * width].rearrange("p (k n) -> p k n", n=width)
                    sp_.dma_start(dst2, d["w_branch"][0, name].rearrange("(k p) n -> p k n", p=P)[:, :, col:col + width]
                                  ).then_inc(landed, 16)

            def stage_load(c):
                kind, e, hf = STEPS[c]
                if kind == "d":
                    src = d["moe_wd"][0, e].rearrange("(k p) n -> p k n", p=P)[:, 2 * hf:2 * hf + 2, :]
                else:
                    src = d["moe_w" + kind][0, e].rearrange("(k p) n -> p k n", p=P)[:, 4 * hf:4 * hf + 4, :]
                sp_.dma_start(stage[c % NS].rearrange("p (k n) -> p k n", k=src.shape[1]), src
                              ).then_inc(S(f"stage_landed{c % NS}"), 16)

            for c in range(NS):
                if c == EARLY:
                    sp_.wait_ge(S("merge_done"), 4 * KD)
                stage_load(c)
            sp_.wait_ge(S("dense_known"), 1)
            over = sp_.value_load(dense[:, :], min_val=0, max_val=1)
            with sp_.If(over):
                for c in range(NS):
                    sp_.wait_ge(S(f"stage_landed{c}"), 16)
                for e in range(NE):
                    if e >= 2:
                        sp_.wait_ge(S("e_used"), e - 1)
                    s = e % 2
                    for w, name in ((wg, "moe_wg"), (wu, "moe_wu"), (wd, "moe_wd")):
                        sp_.dma_start(w[s], d[name][0, e].rearrange("(k p) n -> p k n", p=P)
                                      ).then_inc(S(f"e_landed{s}"), 16)
            with sp_.Else():
                for c in range(NS, len(STEPS)):
                    sp_.wait_ge(S("split_done"), c - NS + 1)
                    stage_load(c)
            for t in range(NT):
                sp_.wait_ge(S("y_done"), t + 1)
                sp_.dma_start(out[0, t * P:(t + 1) * P, :], onorm[:, t, :]).then_inc(S("stored"), 16)
            sp_.wait_ge(S("stored"), 16 * NT)

        @block.gpsimd
        def _(pool):
            pool.dma_start(cst[:, :], d["c_sq"]).then_inc(S("cst_landed"), 16)
            pool.memset(rows[:, :], 0.0).then_inc(S("rows_clear"), 1)
            pool.wait_ge(S("rows_clear"), 1)
            at = 0
            for name, n in (("norm1", 8), ("norm2", 8), ("b_gate", 32), ("conv_w", 12), ("conv_b", 3), ("lru_br", 3),
                            ("lru_bi", 3), ("lru_lambda", 3)):
                src = d[name][0]
                if len(src.shape) == 2:
                    src = src.rearrange("a b -> (a b)")
                pool.dma_start(rows[at:at + n, :], src.rearrange("(a b) -> a b", b=P)).then_inc(S("rows_landed"), 16)
                at += n
            for h in range(A_HEADS):
                r, c = at + h // 2, 64 * (h % 2)
                pool.dma_start(rows[r:r + 1, c:c + A_DK], d["a_b2"][0:1, h * A_DK:(h + 1) * A_DK]
                               ).then_inc(S("rows_landed"), 16)
            pool.dma_start(btab, d["c_tab"]).then_inc(S("btab_landed"), 16)
            pool.dma_start(relb[0:BUCKETS, :], d["rel_bias"]).then_inc(S("btab_landed"), 16)
            pool.dma_start(relb[BUCKETS:BUCKETS + 2, :], d["c_sel"]).then_inc(S("btab_landed"), 16)
            pool.memset(bd, 0.0).then_inc(S("bd_clear"), 1)
            pool.memset(wa2[:, :], 0.0).then_inc(S("bd_clear"), 1)
            pool.wait_ge(S("bd_clear"), 2)
            bw = W // LRU_BLOCKS
            for m, name in enumerate(("lru_wr", "lru_wi")):
                for n in range(LRU_BLOCKS):
                    r = n * bw
                    while r < (n + 1) * bw:
                        e = min((n + 1) * bw, (r // P + 1) * P)
                        pool.dma_start(bd[r % P:r % P + e - r, m, r // P, n * bw:(n + 1) * bw],
                                       d[name][0, n, r - n * bw:e - n * bw, :]).then_inc(S("bd_landed"), 16)
                        r = e
            for h in range(A_HEADS):
                pool.dma_start(wa2[:, 64 * h:64 * h + A_DK], d["a_w2"][0, :, h * A_DK:(h + 1) * A_DK]
                               ).then_inc(S("wa2_landed"), 16)
            pool.dma_start(gain[:, :], d["a_gain"][0:1, :].to_broadcast([P, W])).then_inc(S("gain_landed"), 16)
            pool.dma_start(wr[:, :, 0:GROUPS], d["moe_wrg"][0].rearrange("(k p) n -> p k n", p=P)
                           ).then_inc(S("wr_landed"), 16)
            pool.dma_start(wr[:, :, GROUPS:], d["moe_wre"][0].rearrange("(k p) n -> p k n", p=P)
                           ).then_inc(S("wr_landed"), 16)
            pool.dma_start(rbias[:, 0:GROUPS], d["moe_brg"][0:1, :].to_broadcast([P, GROUPS])).then_inc(S("wr_landed"), 16)
            pool.dma_start(rbias[:, GROUPS:], d["moe_bre"][0:1, :].to_broadcast([P, NE])).then_inc(S("wr_landed"), 16)
            pool.wait_ge(S("bias_rows_ready"), 2)
            pool.dma_start(scratch, bias_rows.unsqueeze(1).to_broadcast([2 * HEADS, P, T + P])
                           ).then_inc(S("scratch_stored"), 16)
            pool.wait_ge(S("scratch_stored"), 16)
            pool.wait_ge(S("oa_ready"), 1)
            pool.wait_ge(S("attm_ready"), 2 * NT)
            pool.wait_ge(S("gla_pe_done"), NT)
            toeplitz = bass.AP(scratch.tensor, scratch.offset + P - 1,
                               [(T + P - 1, P), (P * (T + P), 2 * HEADS), (1, T)])
            pool.dma_start(bias, toeplitz).then_inc(S("bias_landed"), 16)
            pool.wait_ge(S("o_done"), 2 * NT)
            pool.dma_start(gain2, d["norm2"][0:1, :].to_broadcast([P, D])).then_inc(S("gain2_landed"), 16)
            for t in range(NT):
                pool.wait_ge(S("x2_ready"), t + 1)
                pool.dma_start(x2_rows[t * P:(t + 1) * P, :], xs[:, t, :]).then_inc(S("x2_stored"), 16)
            pool.wait_ge(S("x2_stored"), 16 * NT)
            pool.wait_ge(S("dense_known"), 1)
            over = pool.value_load(dense[:, :], min_val=0, max_val=1)
            with pool.If(over):
                pool.wait_ge(S("x2_stored"), 16 * NT)
            with pool.Else():
                pool.wait_ge(S("rt_full"), 1)
                for e in range(NE):
                    if e >= 2:
                        pool.wait_ge(S("xg_used"), e - 1)
                    pool.indirect_dma_start(out=xg[e % 2], out_offset=None, in_=x2_rows,
                                            in_offset=bass.IndirectOffsetOnAxis(ap=token_of[:, e:e + 1], axis=0)
                                            ).then_inc(S(f"xg_landed{e % 2}"), 16)
                for i in range(2):
                    pool.wait_ge(S(f"y_stored{i}"), 16 * (NE // 2))
                pool.wait_ge(S("split_done"), len(STEPS))
                for t in range(NT):
                    for j in range(2):
                        pool.indirect_dma_start(out=yg[t][j], out_offset=None, in_=y_rows,
                                                in_offset=bass.IndirectOffsetOnAxis(
                                                    ap=slot_of[:, j * NT + t:j * NT + t + 1], axis=0)
                                                ).then_inc(S(f"yg_landed{t}"), 16)

        @block.scalar
        def _(act):
            state = {"main": 0, "step": 0}

            def link(ins):
                state["step"] += 1
                ins.then_inc(S("act_step"), 1)
                act.wait_ge(S("act_step"), state["step"])

            def drain_main(fn):
                n = state["main"]
                act.wait_ge(S("main_full"), n + 1)
                fn(main[n % 2]).then_inc(S("main_empty"), 1)
                state["main"] = n + 1

            for t in range(NT):
                act.wait_ge(S(f"x_landed{t}"), 16)
                act.activation(view(CVR + D * t, D), xs[:, t, :], ACT.Square,
                               accum_out=stat[:, 0, t:t + 1]).then_inc(S("ss_ready"), 1)
            act.wait_ge(S("ms_ready"), 1)
            act.activation(stat[:, 2, :], stat[:, 1, :], ACT.Sqrt).then_inc(S("rms_ready"), 1)
            act.wait_ge(S("cols_ready"), 1)
            for c in range(KD):
                drain_main(lambda b, c=c: act.activation(xnT[:, c, :], b[:, :], ACT.Copy, scale=c_norm1[:, c:c + 1]))
            drain_main(lambda b: act.activation(iqT, b[:, :], ACT.Copy, scale=IDX_DIM ** -0.5))
            drain_main(lambda b: act.activation(ikT, b[:, :], ACT.Copy))
            drain_main(lambda b: act.activation(iw[:, :, :].rearrange("p a b -> p (a b)"), b[:, 0:NT * IDX_HEADS], ACT.Copy,
                                                scale=IDX_HEADS ** -0.5))
            for c in range(KW):
                drain_main(lambda b, c=c: act.activation(dxp[:, c, 3:3 + T], b[:, :], ACT.Copy))
            act.wait_ge(S("lam_abs"), 1)
            act.activation(sp[:, 1, :], sp[:, 0, :], ACT.Exp).then_inc(S("lam_exp"), 1)
            n = 0
            for i in range(1, NT):
                for h in range(IDX_HEADS):
                    act.wait_ge(S("idx_full"), n + 1)
                    if n >= 2:
                        act.wait_ge(S("rel_used"), n - 1)
                    act.activation(rel[:, n % 2, 0:(i + 1) * P], lgb[n % 2][:, 0:(i + 1) * P], ACT.Relu
                                   ).then_inc(S("rel_ready"), 1)
                    n += 1
            for c in range(KW):
                drain_main(lambda b, c=c: act.activation(dyT[:, c, :], b[:, :], ACT.Copy))
            act.wait_ge(S("cols_ready"), 2)
            n = 0
            for m, dst in ((0, tr), (1, ti)):
                for c in range(KW):
                    act.wait_ge(S("lru_full"), n + 1)
                    act.activation(dst[:, c, :], aux[n % 2][:, :], ACT.Tanh, scale=0.5,
                                   bias=half[:, 32 + 3 * m + c:33 + 3 * m + c]).then_inc(S("lru_tanh"), 1)
                    n += 1
            act.wait_ge(S("sp_ready"), 1)
            act.wait_ge(S("lru_tanh"), 3)
            for c in range(KW):
                act.activation(tr[:, c, :], tr[:, c, :], ACT.Tanh, scale=sp[:, 7, c:c + 1], bias=sp[:, 7, c:c + 1]
                               ).then_inc(S("lru_t2"), 1)
            act.wait_ge(S("lru_t2"), 3)
            act.wait_ge(S("scratch_stored"), 16)
            act.activation(sq_, tr, ACT.Sqrt).then_inc(S("lru_sqrt"), 1)
            drain_main(lambda b: act.activation(alrT[0:A_RANK, :], b[0:A_RANK, :], ACT.Copy))
            for i in range(2):
                drain_main(lambda b, i=i: act.activation(aqT[:, i, :], b[:, :], ACT.Copy, scale=A_DK ** -0.5))
            for i in range(2):
                drain_main(lambda b, i=i: act.activation(akT[:, i, :], b[:, :], ACT.Copy))
            for dst in (av, ag):
                for t in range(NT):
                    drain_main(lambda b, t=t, dst=dst: act.activation(dst[:, t, :], b[:, 0:W], ACT.Copy))
            act.wait_ge(S("gla_na"), 1)
            link(act.activation(na, na, ACT.Exp))
            act.activation(na, na, ACT.Ln, bias=ones[:, 0:1]).then_inc(S("gla_ln"), 1)
            act.wait_ge(S("lru_u"), 1)
            act.activation(sq_, dyT, ACT.Square).then_inc(S("y2_ready"), 1)
            act.wait_ge(S("gelu_in"), 1)
            act.activation(sq_, sq_, ACT.Tanh, scale=GELU_C).then_inc(S("gelu_tanh"), 1)
            act.wait_ge(S("gla_b"), 1)
            act.activation(eb, b16, ACT.Exp, scale=1.0 / A_TAU).then_inc(S("gla_e"), 1)
            act.activation(kd, b16, ACT.Exp, scale=-1.0 / A_TAU).then_inc(S("gla_e"), 1)
            act.wait_ge(S("gla_d"), 1)
            act.activation(ek, ek, ACT.Exp, scale=1.0 / A_TAU).then_inc(S("gla_e"), 1)
            for dst, scale in ((bqT, HD ** -0.5), (bkT, 1.0)):
                for c in range(KW):
                    drain_main(lambda b, c=c, dst=dst, scale=scale: act.activation(dst[:, c, :], b[:, :], ACT.Copy, scale=scale))
            for i in range(2):
                act.wait_ge(S("ke_full"), i + 1)
                act.activation(keR[:, :, i * P:(i + 1) * P], ps[6 + i][:, :].rearrange("p (t c) -> p t c", c=P), ACT.Copy
                               ).then_inc(S("ke_ready"), 1)
            act.wait_ge(S("lru_u"), 2)
            for t in range(NT):
                drain_main(lambda b, t=t: act.activation(bv[:, t, :], b[:, 0:W], ACT.Copy))
            for t in range(NT):
                act.wait_ge(S("oa_full"), t + 1)
                for hh in range(2):
                    act.activation(oA[:, t, :].rearrange("p (i h v) -> p i h v", h=2, v=A_DV)[:, :, hh, :],
                                   oa_bank[t % 2][hh][:, 0:2 * A_DV].rearrange("p (i v) -> p i v", v=A_DV), ACT.Copy
                                   ).then_inc(S("oa_copied"), 1)
            act.wait_ge(S("oa_copied"), 2 * NT)
            act.activation(oA2, oA, ACT.Square).then_inc(S("oa_sq"), 1)
            act.wait_ge(S("oa_ms"), 1)
            act.activation(ostat[:, :], ostat[:, :], ACT.Sqrt).then_inc(S("oa_rms"), 1)
            act.wait_ge(S("oa_mean"), 1)
            act.activation(oA2, ag, ACT.Tanh, scale=0.5).then_inc(S("oa_tanh"), 1)
            for dst, scale in ((cqT, HD ** -0.5), (ckT, 1.0)):
                for c in range(KW):
                    drain_main(lambda b, c=c, dst=dst, scale=scale: act.activation(dst[:, c, :], b[:, :], ACT.Copy, scale=scale))
            for t in range(NT):
                drain_main(lambda b, t=t: act.activation(cv[:, t, :], b[:, 0:W], ACT.Copy))
            for c in range(KW):
                drain_main(lambda b, c=c: act.activation(oT[0][:, c, :], b[:, :], ACT.Copy))

            def probs(n):
                i = (n // HEADS) % NT
                nk = (i + 1) * P
                act.wait_ge(S("lg_ready"), n + 1)
                if n >= 2:
                    act.wait_ge(S("p_used"), n - 1)
                if n >= 2 * HEADS and n % HEADS == 0:
                    act.wait_ge(S("rl_ready"), n // HEADS - 1)
                act.activation(pr[:, n % 2, 0:nk], lg[:, n % 2, 0:nk], ACT.Exp, bias=nmx[:, n % 4:n % 4 + 1],
                               accum_out=lsum[:, (n // HEADS) % 2, n % HEADS:n % HEADS + 1]).then_inc(S("p_ready"), 1)

            def ptrans(n):
                i = (n // HEADS) % NT
                nk = (i + 1) * P
                act.wait_ge(S("pT_full"), n + 1)
                if n >= 2:
                    act.wait_ge(S("pT_used"), n - 1)
                act.activation(pT[:, n % 2, 0:nk], aux[n % 2][:, 0:nk], ACT.Copy).then_inc(S("pT_ready"), 1)

            units = 2 * NT * HEADS
            for n in range(units + 1):
                if n < units:
                    probs(n)
                if n >= 1:
                    ptrans(n - 1)
            for k in (2, 1):
                for c in range(KW):
                    drain_main(lambda b, c=c, k=k: act.activation(oT[k][:, c, :], b[:, :], ACT.Copy))
            n = 0
            for mc in range(NMC):
                for b_ in range(NBR):
                    for j in range(MCOLS // P):
                        m = mc * (MCOLS // P) + j
                        if n >= 2:
                            act.wait_ge(S("merge_done"), n - 1)
                        drain_main(lambda b, n=n, m=m, b_=b_: act.activation(
                            gate_t[:, n % 2, :], b[:, :], ACT.Tanh, scale=0.5, bias=half[:, 8 * b_ + m:8 * b_ + m + 1]))
                        n += 1
            for t in range(NT):
                act.wait_ge(S("h_done"), NT * (NMC - 1) + t + 1)
                act.activation(xs[:, t, :], hres[:, t, :], ACT.Square, accum_out=stat[:, 0, t:t + 1]).then_inc(S("ss_ready"), 1)
            act.dma_start(nf, d["norm_f"].rearrange("(a n) -> a n", a=1).to_broadcast([P, D])).then_inc(S("nf_landed"), 16)
            act.wait_ge(S("ms_ready"), 2)
            act.activation(stat[:, 2, :], stat[:, 1, :], ACT.Sqrt).then_inc(S("rms_ready"), 1)
            for c in range(KD):
                drain_main(lambda b, c=c: act.activation(xnT[:, c, :], b[:, :], ACT.Copy))
            act.wait_ge(S("rt_sub"), 1)
            act.activation(rt[:, 2, :, :], rt[:, 1, :, :], ACT.Exp).then_inc(S("rt_exp"), 1)
            act.wait_ge(S("rt_diff"), 1)
            act.activation(rt[:, 9, :, 0], rt[:, 8, :, 0], ACT.Exp).then_inc(S("rt_exp"), 1)
            act.wait_ge(S("dense_known"), 1)
            over = act.value_load(dense[:, :], min_val=0, max_val=1)
            with act.If(over):
                n = 0
                for e in range(NE):
                    for m in range(KH):
                        act.wait_ge(S("gu_full"), n + 1)
                        if n >= 2:
                            act.wait_ge(S("hT_ready"), n - 1)
                        act.activation(sg[:, n % 2, :], ps[n % 2][:, :], ACT.Tanh, scale=0.5).then_inc(S("sg_ready"), 1)
                        n += 1
            with act.Else():
                def split(c):
                    act.wait_ge(S(f"stage_landed{c % NS}"), 16 * (c // NS + 1))
                    if c >= NW:
                        act.wait_ge(S("chunk_used"), c - NW + 1)
                    act.activation(w_hi[c % NW], stage[c % NS], ACT.Copy, scale=WSCALE).then_inc(S("hi_done"), 1)

                def x_hi(e):
                    for j in range(2):
                        act.wait_ge(S("xgT_full"), 2 * e + j + 1)
                        if e >= 2:
                            act.wait_ge(S("gu_used"), e - 1)
                        act.activation(xgT[e % 2][0][:, 4 * j:4 * j + 4, :].rearrange("p a b -> p (a b)"), ps[6 + j][:, :],
                                       ACT.Copy).then_inc(S("xhi_done"), 1)

                for c in range(AHEAD):
                    split(c)
                x_hi(0)
                for c, (kind, e, hf) in enumerate(STEPS):
                    if c + AHEAD < len(STEPS):
                        split(c + AHEAD)
                    if kind == "g" and hf:
                        act.wait_ge(S("g_full"), e + 1)
                        if e >= 2:
                            act.wait_ge(S("h_ready"), e - 1)
                        act.activation(sgr[e % 2], ps[2 * (e % 2)][:, :], ACT.Tanh, scale=0.5 / WSCALE).then_inc(S("sgr_ready"), 1)
                    if kind == "u" and not hf and e >= 1:
                        act.wait_ge(S("hgT_full"), e)
                        if e >= 3:
                            act.wait_ge(S("d_full"), e - 2)
                        act.activation(hgT[(e - 1) % 2][0].rearrange("p a b -> p (a b)"), ps[6][:, :], ACT.Copy
                                       ).then_inc(S("hhi_done"), 1)
                    if kind == "u" and hf and e + 1 < NE:
                        x_hi(e + 1)
                    if kind == "d" and hf:
                        act.wait_ge(S("d_full"), e + 1)
                        if e >= 2:
                            act.wait_ge(S(f"y_stored{e % 2}"), 16 * (e // 2))
                        for j in range(2):
                            act.activation(yout[e % 2][:, 512 * j:512 * (j + 1)], ps[4 + j][:, :], ACT.Copy,
                                           scale=1.0 / (WSCALE * HSCALE)).then_inc(S("y_out"), 1)
                        act.wait_ge(S("y_out"), 2 * (e + 1))
                        act.dma_start(y_rows[e * CAP:(e + 1) * CAP, :], yout[e % 2]).then_inc(S(f"y_stored{e % 2}"), 16)
                    if kind == "d" and not hf and e == NE - 1:
                        act.wait_ge(S("hgT_full"), NE)
                        act.activation(hgT[(NE - 1) % 2][0].rearrange("p a b -> p (a b)"), ps[6][:, :], ACT.Copy
                                       ).then_inc(S("hhi_done"), 1)
            for t in range(NT):
                act.wait_ge(S("moe_done"), t + 1)
                act.activation(onorm[:, t, :], hres[:, t, :], ACT.Square, accum_out=stat[:, 0, t:t + 1]).then_inc(S("ss_ready"), 1)
            act.wait_ge(S("ms_ready"), 3)
            act.activation(stat[:, 2, :], stat[:, 1, :], ACT.Sqrt).then_inc(S("rms_ready"), 1)

        @block.tensor
        def _(pe):
            state = {"main": 0, "load": 0}

            def main_bank():
                n = state["main"]
                if n >= 2:
                    pe.wait_ge(S("main_empty"), n - 1)
                return main[n % 2]

            def main_full(ins):
                ins.then_inc(S("main_full"), 1)
                state["main"] += 1

            def weights(width):
                i = state["load"]
                wait_load(pe, i)
                return ring[i % RING][:, 0:KD * width].rearrange("p (k n) -> p k n", n=width)

            def used(ins_fn):
                state["load"] += 1
                pe.drain().then_inc(S("w_used"), 1)

            def t_tile(lhs_of_k, rows_=P):
                b = main_bank()
                for k in range(KD):
                    last = pe.matmul(b[0:rows_, :], lhs_of_k(k), xnT[:, k, :], start=(k == 0), stop=(k == KD - 1))
                main_full(last)

            def r_tile(w, t, width):
                b = main_bank()
                for k in range(KD):
                    last = pe.matmul(b[:, 0:width], xnT[:, k, t * P:(t + 1) * P], w[:, k, :], start=(k == 0), stop=(k == KD - 1))
                main_full(last)

            def proj_t():
                w = weights(W)
                for c in range(KW):
                    t_tile(lambda k, c=c: w[:, k, c * P:(c + 1) * P])
                used(None)

            def proj_r():
                w = weights(W)
                for t in range(NT):
                    r_tile(w, t, W)
                used(None)

            pe.wait_ge(S("cst_landed"), 16)
            pe.wait_ge(S("rows_landed"), 16 * 12)
            pe.transpose(ps[6][:, 0:NROW], rows[:, :], ident[0:NROW, 0:NROW]).then_inc(S("rows_T"), 1)
            pe.wait_ge(S("btab_landed"), 48)
            pe.matmul(aux[0][0:2 * HEADS, :], relb[:, :], btab[:, 0:T], start=True, stop=True)
            pe.matmul(aux[1][0:2 * HEADS, 0:P], relb[:, :], btab[:, T:T + P], start=True, stop=True
                      ).then_inc(S("bias_mm"), 1)
            pe.wait_ge(S("xs_ready"), NT)
            for c in range(KD):
                b = main_bank()
                for t in range(NT):
                    last = pe.transpose(b[:, t * P:(t + 1) * P], xs[:, t, c * P:(c + 1) * P], ident)
                main_full(last)
            pe.wait_ge(S("main_empty"), MEND["xT"])
            w = weights(164)
            t_tile(lambda k: w[:, k, 0:P])
            pe.wait_ge(S("ikrep_ready"), 1)
            t_tile(lambda k: rel[:, :, :].rearrange("p a b -> p (a b)")[:, k * P:(k + 1) * P])
            b = main_bank()
            for t in range(NT):
                for k in range(KD):
                    last = pe.matmul(b[:, t * IDX_HEADS:(t + 1) * IDX_HEADS], xnT[:, k, t * P:(t + 1) * P], w[:, k, 160:164],
                                     start=(k == 0), stop=(k == KD - 1))
            main_full(last)
            used(None)
            proj_t()
            pe.wait_ge(S("main_empty"), MEND["iw"])
            n = 0
            for i in range(1, NT):
                for h in range(IDX_HEADS):
                    if n >= 2:
                        pe.wait_ge(S("rel_ready"), n - 1)
                    r = slice(IDX_DIM * h, IDX_DIM * (h + 1))
                    pe.matmul(lgb[n % 2][:, 0:(i + 1) * P], iqT[r, i * P:(i + 1) * P], ikT[r, 0:(i + 1) * P],
                              start=True, stop=True).then_inc(S("idx_full"), 1)
                    n += 1
            proj_t()
            pe.wait_ge(S("bd_landed"), 16 * 20)
            pe.wait_ge(S("xc_ready"), 1)
            pe.wait_ge(S("bias_rows_ready"), 2)
            n = 0
            for m in range(2):
                for c in range(KW):
                    if n >= 2:
                        pe.wait_ge(S("lru_tanh"), n - 1)
                    ks = [k for k in range(KW) if abs(k - c) <= 1]
                    for k in ks:
                        last = pe.matmul(aux[n % 2][:, :], bd[:, m, k, c * P:(c + 1) * P], xc[:, k, :],
                                         start=(k == ks[0]), stop=(k == ks[-1]))
                    last.then_inc(S("lru_full"), 1)
                    n += 1
            w = weights(A_RANK)
            t_tile(lambda k: w[:, k, :], A_RANK)
            used(None)
            weights(W)
            pe.wait_ge(S("wqk_ready"), 1)
            wflat = wqk.rearrange("p k h c -> p k (h c)")
            for c in range(4):
                t_tile(lambda k, c=c: wflat[:, k, c * P:(c + 1) * P])
            used(None)
            pe.wait_ge(S("wa2_landed"), 64)
            pe.wait_ge(S("main_empty"), MEND["alr"])
            pe.wait_ge(S("cols_ready"), 1)
            for i in range(2):
                pe.matmul(ps[6 + i][:, :], wa2[:, i * P:(i + 1) * P], alrT[0:A_RANK, :], start=True, stop=True
                          ).then_inc(S("z_full"), 1)
            proj_r()
            proj_r()
            proj_t()
            proj_t()
            pe.wait_ge(S("ke_T"), 1)
            pe.wait_ge(S("zb_ready"), 2)
            for i in range(2):
                for t in range(NT):
                    last = pe.transpose(ps[6 + i][:, t * P:(t + 1) * P], akT[:, i, t * P:(t + 1) * P], ident)
                last.then_inc(S("ke_full"), 1)
            proj_r()
            pe.wait_ge(S("ke_ready"), 2)
            pe.wait_ge(S("main_empty"), MEND["av"])
            pe.wait_ge(S("rel_ready"), 12)
            for i in range(2):
                if i:
                    pe.wait_ge(S("u_used"), 1)
                for ch in range(NCH):
                    t, r, c = ch // 2, (ch % 2) * A_CHUNK, ch // 2
                    for hh in range(2):
                        h = 2 * i + hh
                        last = pe.matmul(lgb[ch % 2][64 * hh:64 * hh + 64, c * A_DV:(c + 1) * A_DV],
                                         keR[r:r + A_CHUNK, t, h * 64:h * 64 + 64],
                                         av[r:r + A_CHUNK, t, h * A_DV:(h + 1) * A_DV], start=True, stop=True,
                                         skip_group_check=True)
                last.then_inc(S("u_full"), 1)
            pe.wait_ge(S("qk_ready"), 1)
            pe.wait_ge(S("lru_tanh"), 6)

            def gla_att(t):
                if t >= 2:
                    pe.wait_ge(S("attm_ready"), 2 * (t - 1))
                for h in range(A_HEADS):
                    r = slice(64 * (h % 2), 64 * (h % 2) + 64)
                    c0 = (h // 2) * P
                    last = pe.matmul(att_bank[t % 2][h % 2][:, c0:c0 + P], kd[r, h // 2, t * P:(t + 1) * P],
                                     aqT[r, h // 2, t * P:(t + 1) * P], start=True, stop=True, skip_group_check=True)
                last.then_inc(S("att_full"), 1)

            def gla_out(t):
                pe.wait_ge(S("attm_ready"), 2 * (t + 1))
                if t >= 2:
                    pe.wait_ge(S("oa_copied"), 2 * (t - 1))
                for h in range(A_HEADS):
                    i, r0 = h // 2, 64 * (h % 2)
                    b = oa_bank[t % 2][h % 2]
                    cs, vs = slice(i * A_DV, (i + 1) * A_DV), slice(h * A_DV, (h + 1) * A_DV)
                    last = pe.matmul(b[:, cs], attm[:, t % 2, h, :], av[:, t, vs], start=True, stop=False, skip_group_check=True)
                    for hf in range(2):
                        ch = 2 * t + hf
                        if ch == 0:
                            continue
                        last = pe.matmul(b[64 * hf:64 * hf + 64, cs], aqT[r0:r0 + 64, i, ch * A_CHUNK:(ch + 1) * A_CHUNK],
                                         St[r0:r0 + 64, i, ch, :], start=False, stop=True, skip_group_check=True)
                last.then_inc(S("oa_full"), 1)
                pe.drain().then_inc(S("gla_pe_done"), 1)

            pe.wait_ge(S("main_empty"), MEND["bv"])
            gla_att(0)
            pe.wait_ge(S("u_used"), 2)
            for t in range(NT):
                if t + 1 < NT:
                    gla_att(t + 1)
                gla_out(t)
            proj_t()
            proj_t()
            proj_r()

            def to_T(src):
                for c in range(KW):
                    b = main_bank()
                    for t in range(NT):
                        last = pe.transpose(b[:, t * P:(t + 1) * P], src[:, t, c * P:(c + 1) * P], ident)
                    main_full(last)

            pe.wait_ge(S("oa_ready"), 1)
            to_T(oA)

            def unit(n):
                br, i, h = n // (NT * HEADS), (n // HEADS) % NT, n % HEADS
                q, k, v = ((cqT, ckT, cv), (bqT, bkT, bv))[br]
                return br, i, h, q, k, v

            def logits(n):
                br, i, h, q, k, v = unit(n)
                if n >= 2:
                    pe.wait_ge(S("lg_read"), n - 1)
                r = slice(64 * (h % 2), 64 * (h % 2) + 64)
                pe.matmul(lgb[n % 2][:, 0:(i + 1) * P], q[r, h // 2, i * P:(i + 1) * P], k[r, h // 2, 0:(i + 1) * P],
                          start=True, stop=True).then_inc(S("lg_full"), 1)

            def transp(n):
                br, i, h, q, k, v = unit(n)
                pe.wait_ge(S("p_ready"), n + 1)
                if n >= 2:
                    pe.wait_ge(S("pT_ready"), n - 1)
                for b in range(i + 1):
                    last = pe.transpose(aux[n % 2][:, b * P:(b + 1) * P], pr[:, n % 2, b * P:(b + 1) * P], ident)
                last.then_inc(S("pT_full"), 1)
                pe.drain().then_inc(S("p_used"), 1)

            def attend(n):
                br, i, h, q, k, v = unit(n)
                pe.wait_ge(S("pT_ready"), n + 1)
                g = n // HEADS
                if h == 0 and g >= 2:
                    pe.wait_ge(S("o_done"), g - 1)
                for b in range(i + 1):
                    last = pe.matmul(ps[6 + g % 2][:, h * HD:(h + 1) * HD], pT[:, n % 2, b * P:(b + 1) * P],
                                     v[:, b, h * HD:(h + 1) * HD], start=(b == 0), stop=(b == i), skip_group_check=True)
                last.then_inc(S("pT_used"), 1)

            units = 2 * NT * HEADS
            pe.wait_ge(S("main_empty"), MEND["cv"])
            pe.wait_ge(S("u_used"), 2)
            pe.wait_ge(S("attm_ready"), 2 * NT)
            pe.wait_ge(S("oa_copied"), 2 * NT)
            for n in range(units + 2):
                if n < units:
                    logits(n)
                if 1 <= n <= units:
                    transp(n - 1)
                if n >= 2:
                    attend(n - 2)
            pe.wait_ge(S("o_done"), NT)
            to_T(oR[1])
            pe.wait_ge(S("o_done"), 2 * NT)
            to_T(oR[0])
            pe.wait_ge(S("main_empty"), MEND["oTb"])
            n = 0
            for mc in range(NMC):
                for b_ in range(NBR):
                    wait_load(pe, state["load"])
                    slot = ring[state["load"] % RING]
                    wgt = slot[:, 0:KD * MCOLS].rearrange("p (k n) -> p k n", n=MCOLS)
                    wbr = slot[:, KD * MCOLS:(KD + KW) * MCOLS].rearrange("p (k n) -> p k n", n=MCOLS)
                    for j in range(MCOLS // P):
                        t_tile(lambda k, j=j: wgt[:, k, j * P:(j + 1) * P])
                        if n >= 2:
                            pe.wait_ge(S("merge_done"), n - 1)
                        for k in range(KW):
                            last = pe.matmul(aux[n % 2][:, :], wbr[:, k, j * P:(j + 1) * P], oT[b_][:, k, :],
                                             start=(k == 0), stop=(k == KW - 1))
                        last.then_inc(S("br_full"), 1)
                        n += 1
                    used(None)
            pe.wait_ge(S("merge_done"), 4 * KD)
            n = 0
            for mc in range(NMC):
                w = weights(MCOLS)
                for t in range(NT):
                    if n >= 2:
                        pe.wait_ge(S("h_done"), n - 1)
                    for k in range(KD):
                        last = pe.matmul(lgb[n % 2][:, 0:MCOLS], merged[:, k, t * P:(t + 1) * P], w[:, k, :],
                                         start=(k == 0), stop=(k == KD - 1))
                    last.then_inc(S("out_full"), 1)
                    n += 1
                used(None)
            pe.wait_ge(S("x2_ready"), NT)
            for c in range(KD):
                b = main_bank()
                for t in range(NT):
                    last = pe.transpose(b[:, t * P:(t + 1) * P], xs[:, t, c * P:(c + 1) * P], ident)
                main_full(last)
            pe.wait_ge(S("main_empty"), MEND["x2T"])
            pe.wait_ge(S("wr_landed"), 64)
            nr = GROUPS + NE
            for t in range(NT):
                for k in range(KD):
                    last = pe.matmul(ps[6][:, t * nr:(t + 1) * nr], xnT[:, k, t * P:(t + 1) * P], wr[:, k, :],
                                     start=(k == 0), stop=(k == KD - 1))
            last.then_inc(S("rt_full"), 1)
            pe.wait_ge(S("sel_ready"), 1)
            pe.wait_ge(S("h_done"), NT * NMC)
            for t in range(NT):
                for t2 in range(t + 1):
                    pe.matmul(ps[5][:, t * NE:(t + 1) * NE], earlier if t2 == t else allones, sel16[:, t2, :],
                              start=(t2 == 0), stop=(t2 == t))
            for t in range(NT):
                last = pe.matmul(ps[5][:, NT * NE:(NT + 1) * NE], allones, sel16[:, t, :], start=(t == 0), stop=(t == NT - 1))
            last.then_inc(S("rank_full"), 1)
            pe.wait_ge(S("onehot_ready"), NT)
            for e in range(NE):
                for t in range(NT):
                    last = pe.matmul(ps[7][:, e:e + 1], onehot[:, t, e * P:(e + 1) * P], tok16[:, t:t + 1],
                                     start=(t == 0), stop=(t == NT - 1))
            last.then_inc(S("token_full"), 1)
            pe.wait_ge(S("dense_known"), 1)
            over = pe.value_load(dense[:, :], min_val=0, max_val=1)
            with pe.If(over):
                n = y = 0
                for e in range(NE):
                    s = e % 2
                    pe.wait_ge(S(f"e_landed{s}"), 48 * (e // 2 + 1))
                    for m in range(KH):
                        if n >= 2:
                            pe.wait_ge(S("hT_ready"), n - 1)
                        for k in range(KD):
                            pe.matmul(ps[n % 2][:, :], wg[s][:, k, m * P:(m + 1) * P], xnT[:, k, :], start=(k == 0), stop=(k == KD - 1))
                        for k in range(KD):
                            last = pe.matmul(ps[2 + n % 2][:, :], wu[s][:, k, m * P:(m + 1) * P], xnT[:, k, :],
                                             start=(k == 0), stop=(k == KD - 1))
                        last.then_inc(S("gu_full"), 1)
                        n += 1
                    pe.wait_ge(S("hT_ready"), n)
                    if e == 0:
                        pe.wait_ge(S("rt_read"), 1)
                    for t in range(NT):
                        for hf in range(2):
                            if y >= 4:
                                pe.wait_ge(S("acc_done"), y - 3)
                            for k in range(KH):
                                last = pe.matmul(ps[4 + y % 4][:, :], hT[:, k, t * P:(t + 1) * P], wd[s][:, k, hf * 512:(hf + 1) * 512],
                                                 start=(k == 0), stop=(k == KH - 1))
                            last.then_inc(S("y_full"), 1)
                            y += 1
                    pe.drain().then_inc(S("e_used"), 1)
            with pe.Else():
                def x_transposes(e):
                    pe.wait_ge(S(f"xg_landed{e % 2}"), 16 * (e // 2 + 1))
                    if e == 0:
                        pe.wait_ge(S("token_read"), 1)
                    else:
                        pe.wait_ge(S("xlo_done"), 2 * e)
                        pe.wait_ge(S("hlo_done"), e - 1) if e >= 2 else None
                    for j in range(2):
                        for k in range(4):
                            last = pe.transpose(ps[6 + j][:, k * P:(k + 1) * P], xg[e % 2][:, (4 * j + k) * P:(4 * j + k + 1) * P],
                                                ident)
                        last.then_inc(S("xgT_full"), 1)
                    pe.wait_ge(S("xgT_full"), 2 * e + 2)
                    pe.nop().then_inc(S("xg_used"), 1)

                def h_transposes(e):
                    pe.wait_ge(S("h_ready"), e + 1)
                    pe.wait_ge(S("xlo_done"), 2 * min(e + 2, NE))
                    for k in range(KH):
                        last = pe.transpose(ps[6][:, k * P:(k + 1) * P], hrow[e % 2][:, k * P:(k + 1) * P], ident)
                    last.then_inc(S("hgT_full"), 1)

                def products(outb, hi, lo, whi, wlo, first, last_):
                    pe.matmul(outb, hi, whi, start=first, stop=False)
                    pe.matmul(outb, hi, wlo, start=False, stop=False)
                    return pe.matmul(outb, lo, whi, start=False, stop=last_)

                x_transposes(0)
                for c, (kind, e, hf) in enumerate(STEPS):
                    if kind == "u" and not hf and e >= 1:
                        h_transposes(e - 1)
                    if kind == "d" and not hf:
                        if e == NE - 1:
                            h_transposes(e)
                        pe.wait_ge(S("hlo_done"), e + 1)
                        if e >= 1:
                            pe.wait_ge(S("y_out"), 2 * e)
                    if kind == "g" and not hf:
                        pe.wait_ge(S("xlo_done"), 2 * (e + 1))
                        if e >= 2:
                            pe.wait_ge(S("h_ready"), e - 1)
                    pe.wait_ge(S("split_done"), c + 1)
                    if kind == "d":
                        v = [w[c % NW].rearrange("p (k n) -> p k n", k=2) for w in (w_hi, w_lo)]
                        hi, lo = hgT[e % 2]
                        for k in range(2):
                            for j in range(2):
                                cs = slice(512 * j, 512 * (j + 1))
                                last = products(ps[4 + j][:, :], hi[:, 2 * hf + k, :], lo[:, 2 * hf + k, :], v[0][:, k, cs],
                                                v[1][:, k, cs], hf == 0 and k == 0, hf == 1 and k == 1)
                    else:
                        v = [w[c % NW].rearrange("p (k n) -> p k n", k=4) for w in (w_hi, w_lo)]
                        hi, lo = xgT[e % 2]
                        bank = ps[2 * (e % 2) + (kind == "u")]
                        for k in range(4):
                            last = products(bank[:, :], hi[:, 4 * hf + k, :], lo[:, 4 * hf + k, :], v[0][:, k, :], v[1][:, k, :],
                                            hf == 0 and k == 0, hf == 1 and k == 3)
                    last.then_inc(S("chunk_used"), 1)
                    if hf:
                        pe.wait_ge(S("chunk_used"), c + 1)
                        pe.nop().then_inc(S({"g": "g_full", "u": "gu_used", "d": "d_full"}[kind]), 1)
                    if kind == "u" and hf and e + 1 < NE:
                        x_transposes(e + 1)

        @block.vector
        def _(dve):
            state = {"chain": "dve_step", "step": 0, "sig": {}}

            def link(ins):
                state["step"] += 1
                ins.then_inc(S(state["chain"]), 1)
                dve.wait_ge(S(state["chain"]), state["step"])

            def new_chain(name, sig):
                state.update(chain=name, step=0, sig=dict(sig))

            def sig(name, ins):
                n = state["sig"][name] = state["sig"].get(name, 0) + 1
                ins.then_inc(S(name), 1)
                dve.wait_ge(S(name), n)

            ts, tt, stt = dve.tensor_scalar, dve.tensor_tensor, dve.scalar_tensor_tensor

            def flat(v):
                s = v.shape
                if len(s) == 3:
                    return v.rearrange("p a b -> p (a b)")
                return v

            dve.memset(ones[:, :], 1.0).then_inc(S("memsets"), 1)
            dve.memset(seg, 1.0).then_inc(S("memsets"), 1)
            dve.memset(dxp[:, :, 0:3], 0.0).then_inc(S("memsets"), 1)
            dve.wait_ge(S("memsets"), 3)
            link(dve.memset(seg.rearrange("p (a b) -> p a b", b=A_CHUNK)[:, :, 0:1], 0.0))

            def norm_scale(src, count):
                dve.wait_ge(S("ss_ready"), NT * count)
                sig("ms_ready", ts(stat[:, 1, :], stat[:, 0, :], 1.0 / D, EPS, ALU.mult, ALU.add))
                dve.wait_ge(S("rms_ready"), count)
                link(dve.reciprocal(stat[:, 3, :], stat[:, 2, :]))

            norm_scale(xs, 1)
            for t in range(NT):
                sig("xs_ready", ts(xs[:, t, :], xs[:, t, :], stat[:, 3, t:t + 1], None, ALU.mult))
            dve.wait_ge(S("rows_T"), 1)
            sig("cols_ready", dve.tensor_copy(cols[:, :], ps[6][:, 0:NROW]))
            link(ts(half[:, 0:32], c_bgate, 0.5, None, ALU.mult))
            sig("cols_ready", ts(half[:, 32:38], cols[:, 63:69], 0.5, None, ALU.mult))
            link(ts(sp[:, 0, :], c_lam, -1.0, None, ALU.mult))
            sig("lam_abs", tt(sp[:, 0, :], sp[:, 0, :], c_lam, ALU.min))
            dve.wait_ge(S("bias_mm"), 1)
            sig("bias_rows_ready", dve.tensor_copy(bias_rows[:, 0:T], aux[0][0:2 * HEADS, :]))
            sig("bias_rows_ready", dve.tensor_copy(bias_rows[:, T:T + P], aux[1][0:2 * HEADS, 0:P]))
            wait_load(dve, 0)
            iks = ring[0][:, 0:KD * 164].rearrange("p (k n) -> p k n", n=164)[:, :, P:P + IDX_DIM]
            repv = rel[:, :, :].rearrange("p a b -> p (a b)").rearrange("p (k h c) -> p k h c", h=IDX_HEADS, c=IDX_DIM)
            for h in range(IDX_HEADS - 1):
                dve.tensor_copy(repv[:, :, h, :], iks)
            sig("ikrep_ready", dve.tensor_copy(repv[:, :, IDX_HEADS - 1, :], iks))
            dve.wait_ge(S("lam_exp"), 1)
            e_, z_, z2, pl = sp[:, 1, :], sp[:, 2, :], sp[:, 3, :], sp[:, 4, :]
            link(ts(z_, e_, 2.0, None, ALU.add))
            link(dve.reciprocal(z_, z_))
            link(tt(z_, z_, e_, ALU.mult))
            link(tt(z2, z_, z_, ALU.mult))
            link(ts(pl, z2, 1.0 / 19, 1.0 / 17, ALU.mult, ALU.add))
            for o in (15, 13, 11, 9, 7, 5, 3, 1):
                link(tt(pl, pl, z2, ALU.mult))
                link(ts(pl, pl, 1.0 / o, None, ALU.add))
            link(tt(pl, pl, z_, ALU.mult))
            link(ts(sp[:, 5, :], c_lam, -1.0, 0.0, ALU.mult, ALU.max))
            link(stt(sp[:, 6, :], pl, 2.0, sp[:, 5, :], ALU.mult, ALU.add))
            sig("sp_ready", ts(sp[:, 7, :], sp[:, 6, :], LRU_C / 4, None, ALU.mult))
            dve.wait_ge(S("main_empty"), MEND["dx"])
            for c in range(KW):
                link(ts(xc[:, c, :], dxp[:, c, 3:3 + T], c_convw[:, 9 + c:10 + c], c_convb[:, c:c + 1], ALU.mult, ALU.add))
                for j in range(3):
                    ins = stt(xc[:, c, :], dxp[:, c, j:j + T], c_convw[:, 3 * j + c:3 * j + c + 1], xc[:, c, :], ALU.mult, ALU.add)
                    if c == KW - 1 and j == 2:
                        sig("xc_ready", ins)
                    else:
                        link(ins)
            n = 0
            for i in range(1, NT):
                nk = (i + 1) * P
                for h in range(IDX_HEADS):
                    dve.wait_ge(S("rel_ready"), n + 1)
                    w1 = iw[:, i, h:h + 1]
                    if h == 0:
                        ins = ts(sel[i], rel[:, n % 2, 0:nk], w1, None, ALU.mult)
                    else:
                        ins = stt(sel[i], rel[:, n % 2, 0:nk], w1, sel[i], ALU.mult, ALU.add)
                    sig("rel_used", ins)
                    n += 1
                link(tt(sel[i][:, i * P:nk], sel[i][:, i * P:nk], future, ALU.add))

            def topk(i):
                for _ in range(TOPK // 8):
                    link(dve.max(out=m8[:, :], in_=sel[i]))
                    link(dve.match_replace(out=sel[i], in_to_replace=m8[:, :], in_values=sel[i], imm_value=TAKEN))
                link(ts(sel[i], sel[i], -2e38, BIG, ALU.is_gt, ALU.mult))

            wait_load(dve, 4)
            dve.wait_ge(S("main_full"), MEND["xT"])
            dve.wait_ge(S("main_empty"), MEND["xT"])
            link(dve.memset(wqk.rearrange("p k h c -> p (k h c)"), 0.0))
            src = ring[4 % RING][:, 0:KD * W].rearrange("p (k h c) -> p k h c", h=8, c=A_DK)
            sig("wqk_ready", dve.tensor_copy(wqk[:, :, :, 0:A_DK].rearrange("p k h c -> p (k h) c"),
                                             src.rearrange("p k h c -> p (k h) c")))
            topk(1)
            dve.wait_ge(S("lru_sqrt"), 1)
            link(ts(flat(tr), flat(tr), 1.0, None, ALU.add))
            link(dve.reciprocal(flat(tr), flat(tr)))
            dve.wait_ge(S("lru_tanh"), 6)
            link(stt(flat(ti), flat(ti), 1.0, flat(xc), ALU.add, ALU.mult))
            link(tt(flat(ti), flat(ti), flat(tr), ALU.mult))
            sig("lru_u", tt(flat(ti), flat(ti), flat(sq_), ALU.mult))
            link(ts(flat(tr), flat(tr), 2.0, -1.0, ALU.mult, ALU.add))
            for c in range(KW):
                link(dve.tensor_tensor_scan(out=xc[:, c, :], data0=tr[:, c, :], data1=ti[:, c, :], initial=0.0,
                                            op0=ALU.mult, op1=ALU.add))
            dve.wait_ge(S("z_full"), 2)
            for i in range(2):
                sig("zb_ready", ts(zb[:, i, :], ps[6 + i][:, :], c_b2[:, i:i + 1], None, ALU.add))
            link(ts(flat(na), flat(zb), -1.0, None, ALU.mult))
            sig("gla_na", tt(flat(na), flat(na), flat(zb), ALU.min))
            dve.wait_ge(S("gla_ln"), 1)
            link(stt(flat(zb), flat(zb), 0.0, flat(na), ALU.min, ALU.subtract))
            sig("gla_b", dve.tensor_tensor_scan(out=flat(b16), data0=seg, data1=flat(zb), initial=0.0,
                                                op0=ALU.mult, op1=ALU.add))
            dve.wait_ge(S("y2_ready"), 1)
            link(ts(flat(sq_), flat(sq_), 0.044715, 1.0, ALU.mult, ALU.add))
            sig("gelu_in", tt(flat(sq_), flat(sq_), flat(dyT), ALU.mult))
            b4 = flat(b16).rearrange("p (n c) -> p n c", c=A_CHUNK)
            e4 = flat(ek).rearrange("p (n c) -> p n c", c=A_CHUNK)
            sig("gla_d", tt(e4, b4[:, :, A_CHUNK - 1:A_CHUNK].to_broadcast([P, 2 * NCH, A_CHUNK]), b4, ALU.subtract))
            dve.wait_ge(S("gelu_tanh"), 1)
            link(stt(flat(sq_), flat(sq_), 1.0, flat(dyT), ALU.add, ALU.mult))
            sig("lru_u", stt(flat(oTd), flat(sq_), 0.5, flat(xc), ALU.mult, ALU.mult))
            dve.wait_ge(S("main_empty"), MEND["aqk"])
            dve.wait_ge(S("gla_e"), 3)
            link(tt(flat(kd), flat(kd), flat(akT), ALU.mult))
            sig("ke_T", tt(flat(akT), flat(akT), flat(ek), ALU.mult))
            sig("qk_ready", tt(flat(aqT), flat(aqT), flat(eb), ALU.mult))
            link(dve.memset(St[:, :, 0, :], 0.0))
            topk(2)
            for i in range(2):
                dve.wait_ge(S("u_full"), i + 1)
                for ch in range(NCH):
                    ins = stt(St[:, i, ch + 1, :], St[:, i, ch, :], eb[:, i, ch * A_CHUNK + A_CHUNK - 1:(ch + 1) * A_CHUNK],
                              lgb[ch % 2][:, (ch // 2) * A_DV:(ch // 2 + 1) * A_DV], ALU.mult, ALU.add)
                    if ch == NCH - 1:
                        sig("u_used", ins)
                    else:
                        link(ins)
            for t in range(NT):
                dve.wait_ge(S("att_full"), t + 1)
                if t >= 2:
                    dve.wait_ge(S("gla_pe_done"), t - 1)
                for hh in range(2):
                    sig("attm_ready", tt(attm[:, t % 2, :, :].rearrange("p (i h) c -> p i h c", h=2)[:, :, hh, :],
                                         att_bank[t % 2][hh][:, 0:2 * P].rearrange("p (i c) -> p i c", c=P),
                                         glamask.unsqueeze(1).to_broadcast([P, 2, P]), ALU.mult))
            dve.wait_ge(S("oa_sq"), 1)
            link(dve.tensor_reduce(ostat[:, :], flat(oA2).rearrange("p (n v) -> p n v", v=A_DV), axis=AX.X, op=ALU.add))
            sig("oa_ms", ts(ostat[:, :], ostat[:, :], 1.0 / A_DV, EPS, ALU.mult, ALU.add))
            dve.wait_ge(S("oa_rms"), 1)
            link(dve.reciprocal(ostat[:, :], ostat[:, :]))
            o3 = flat(oA).rearrange("p (n v) -> p n v", v=A_DV)
            sig("oa_mean", tt(o3, o3, ostat[:, :].unsqueeze(2).to_broadcast([P, NT * A_HEADS, A_DV]), ALU.mult))
            dve.wait_ge(S("gain_landed"), 16)
            link(tt(oA, oA, gain[:, :].unsqueeze(1).to_broadcast([P, NT, W]), ALU.mult))
            dve.wait_ge(S("oa_tanh"), 1)
            link(stt(flat(oA2), flat(oA2), 1.0, flat(ag), ALU.add, ALU.mult))
            sig("oa_ready", stt(flat(oA), flat(oA2), 0.5, flat(oA), ALU.mult, ALU.mult))
            topk(3)
            dve.wait_ge(S("bias_landed"), 16)
            units = 2 * NT * HEADS

            def scores(n):
                br, i, h = n // (NT * HEADS), (n // HEADS) % NT, n % HEADS
                nk = (i + 1) * P
                head = h if br else HEADS + h
                dve.wait_ge(S("lg_full"), n + 1)
                if n >= 2:
                    dve.wait_ge(S("p_ready"), n - 1)
                l = lg[:, n % 2, 0:nk]
                sig("lg_read", tt(l, lgb[n % 2][:, 0:nk], bias[:, head, T - nk:T], ALU.add))
                if br and i:
                    link(tt(l, l, sel[i], ALU.add))
                sig("lg_ready", dve.tensor_reduce(nmx[:, n % 4:n % 4 + 1], l, axis=AX.X, op=ALU.max, negate=True))

            def finish(g):
                br, i = g // NT, g % NT
                dve.wait_ge(S("p_ready"), (g + 1) * HEADS)
                sig("rl_ready", dve.reciprocal(rl[:, g % 2, :], lsum[:, g % 2, :]))
                dve.wait_ge(S("pT_used"), (g + 1) * HEADS)
                if g == 0:
                    dve.wait_ge(S("main_empty"), MEND["oTa"])
                sig("o_done", tt(oR[0 if br else 1][:, i, :].rearrange("p (h c) -> p h c", c=HD),
                                 ps[6 + g % 2][:, 0:W].rearrange("p (h c) -> p h c", c=HD),
                                 rl[:, g % 2, :].unsqueeze(2).to_broadcast([P, HEADS, HD]), ALU.mult))

            for n in range(units):
                scores(n)
                if n % HEADS == 3 and n > HEADS:
                    finish(n // HEADS - 1)
            finish(2 * NT - 1)
            n = 0
            for mc in range(NMC):
                for b_ in range(NBR):
                    for j in range(MCOLS // P):
                        m = mc * (MCOLS // P) + j
                        dve.wait_ge(S("br_full"), n + 1)
                        dve.wait_ge(S("main_empty"), MEND["oTb"] + n + 1)
                        if b_ == 0:
                            sig("merge_done", stt(merged[:, m, :], gate_t[:, n % 2, :], 1.0, aux[n % 2][:, :], ALU.add, ALU.mult))
                        else:
                            link(stt(gterm, gate_t[:, n % 2, :], 1.0, aux[n % 2][:, :], ALU.add, ALU.mult))
                            sig("merge_done", tt(merged[:, m, :], merged[:, m, :], gterm, ALU.add))
                        n += 1
            dve.wait_ge(S("xres_landed"), 16)
            n = 0
            for mc in range(NMC):
                for t in range(NT):
                    dve.wait_ge(S("out_full"), n + 1)
                    h_ = hres[:, t, mc * MCOLS:(mc + 1) * MCOLS]
                    sig("h_done", stt(h_, lgb[n % 2][:, 0:MCOLS], 0.5, h_, ALU.mult, ALU.add))
                    n += 1
            norm_scale(hres, 2)
            dve.wait_ge(S("gain2_landed"), 16)
            for t in range(NT):
                sig("x2_ready", stt(xs[:, t, :], hres[:, t, :], stat[:, 3, t:t + 1], gain2, ALU.mult, ALU.mult))
            dve.wait_ge(S("rt_full"), 1)
            nr = GROUPS + NE
            sig("rt_read", tt(rlog[:, :, :], ps[6][:, 0:NT * nr].rearrange("p (t n) -> p t n", n=nr),
                              rbias[:, :].unsqueeze(1).to_broadcast([P, NT, nr]), ALU.add))
            gl = rlog[:, :, 0:GROUPS]

            def R(i):
                return rt[:, i, :, :]

            def R1(i, j=0):
                return rt[:, i, :, j:j + 1]

            def wide(x):
                return x.to_broadcast([P, NT, 4])

            def argmax(dst, src, mx, tmp):
                link(dve.tensor_reduce(mx, src, axis=AX.X, op=ALU.max))
                link(tt(dst, src, wide(mx), ALU.is_equal))
                link(tt(dst, dst, prio.unsqueeze(1).to_broadcast([P, NT, 4]), ALU.mult))
                link(dve.tensor_reduce(tmp, dst, axis=AX.X, op=ALU.max))
                link(tt(dst, dst, wide(tmp), ALU.is_equal))

            argmax(R(3), gl, R1(0), R1(0, 1))
            sig("rt_sub", tt(R(1), gl, wide(R1(0)), ALU.subtract))
            link(tt(R(4), rlog[:, :, GROUPS:GROUPS + EPG], wide(R1(3, 0)), ALU.mult))
            for g in range(1, GROUPS):
                link(tt(R(5), rlog[:, :, GROUPS + g * EPG:GROUPS + (g + 1) * EPG], wide(R1(3, g)), ALU.mult))
                link(tt(R(4), R(4), R(5), ALU.add))
            argmax(R(6), R(4), R1(7, 0), R1(0, 1))
            link(ts(R(5), R(6), BIG, None, ALU.mult))
            link(tt(R(5), R(5), R(4), ALU.add))
            argmax(R(10), R(5), R1(7, 1), R1(0, 1))
            sig("rt_diff", tt(R1(8), R1(7, 1), R1(7, 0), ALU.subtract))
            dve.wait_ge(S("rt_exp"), 2)
            link(dve.tensor_reduce(R1(11), R(2), axis=AX.X, op=ALU.add))
            link(dve.reciprocal(R1(11), R1(11)))
            link(ts(R1(12), R1(9), 1.0, None, ALU.add))
            link(dve.reciprocal(R1(12), R1(12)))
            link(tt(R1(12), R1(12), R1(11), ALU.mult))
            link(tt(R1(13), R1(12), R1(9), ALU.mult))
            link(dve.tensor_copy(wsel[:, 0, :].unsqueeze(2), R1(12)))
            link(dve.tensor_copy(wsel[:, 1, :].unsqueeze(2), R1(13)))
            for j, r in ((0, R(6)), (1, R(10))):
                for g in range(GROUPS):
                    link(tt(selj[:, j, :, g * EPG:(g + 1) * EPG], r, wide(R1(3, g)), ALU.mult))
            link(tt(R(6), R(6), wide(R1(12)), ALU.mult))
            link(tt(R(10), R(10), wide(R1(13)), ALU.mult))
            link(tt(R(6), R(6), R(10), ALU.add))
            link(ts(R(6), R(6), 0.5, None, ALU.mult))
            for g in range(GROUPS):
                link(tt(gates[:, :, g * EPG:(g + 1) * EPG], R(6), wide(R1(3, g)), ALU.mult))
            sig("sel_ready", tt(sel16[:, :, :], selj[:, 0, :, :], selj[:, 1, :, :], ALU.add))
            dve.wait_ge(S("rank_full"), 1)
            link(dve.tensor_reduce(total[:, 0:1], ps[5][:, NT * NE:(NT + 1) * NE], axis=AX.X, op=ALU.max))
            link(dve.tensor_copy(rank[:, :, :], ps[5][:, 0:NT * NE].rearrange("p (t e) -> p t e", e=NE)))
            link(ts(dense[:, :], total[0:1, 0:1], float(CAP), None, ALU.is_gt))
            link(tt(tmp16[:, :, :], rank[:, :, :], slot0.unsqueeze(1).to_broadcast([P, NT, NE]), ALU.add))
            for j in range(2):
                link(tt(selj[:, j, :, :], selj[:, j, :, :], tmp16[:, :, :], ALU.mult))
                link(dve.tensor_reduce(slotf[:, j, :], selj[:, j, :, :], axis=AX.X, op=ALU.add))
            link(dve.tensor_copy(slot_of[:, :], slotf[:, :, :].rearrange("p a b -> p (a b)")))
            link(stt(rank[:, :, :], rank[:, :, :], 1.0, sel16[:, :, :], ALU.add, ALU.mult))
            link(ts(rank[:, :, :], rank[:, :, :], -1.0, None, ALU.add))
            link(dve.tensor_copy(tok16[:, :], tokid))
            for t in range(NT):
                sig("onehot_ready", tt(onehot[:, t, :].rearrange("p (e c) -> p e c", c=P),
                                       slots.unsqueeze(1).to_broadcast([P, NE, P]),
                                       rank[:, t, :].unsqueeze(2).to_broadcast([P, NE, P]), ALU.is_equal))
            dve.wait_ge(S("token_full"), 1)
            sig("token_read", dve.tensor_copy(token_of[:, :], ps[7][:, 0:NE]))
            sig("dense_known", ts(total[:, 1:2], total[:, 0:1], 1.0, None, ALU.mult))
            over = dve.value_load(dense[:, :], min_val=0, max_val=1)
            before = dict(state["sig"])
            with dve.If(over):
                new_chain("dve_step_dense", before)
                n = y = 0
                for e in range(NE):
                    for m in range(KH):
                        dve.wait_ge(S("sg_ready"), n + 1)
                        if m == 0 and e >= 1:
                            dve.wait_ge(S("e_used"), e)
                        link(stt(sg[:, n % 2, :], sg[:, n % 2, :], 1.0, ps[n % 2][:, :], ALU.add, ALU.mult))
                        sig("hT_ready", tt(hT[:, m, :], sg[:, n % 2, :], ps[2 + n % 2][:, :], ALU.mult))
                        n += 1
                    for t in range(NT):
                        for hf in range(2):
                            dve.wait_ge(S("y_full"), y + 1)
                            h_ = hres[:, t, hf * 512:(hf + 1) * 512]
                            sig("acc_done", stt(h_, ps[4 + y % 4][:, :], gates[:, t, e:e + 1], h_, ALU.mult, ALU.add))
                            y += 1
                for t in range(NT):
                    sig("moe_done", ts(total[:, 1:2], total[:, 0:1], 1.0, None, ALU.mult))
            with dve.Else():
                new_chain("dve_step_routed", before)
                def split(c):
                    dve.wait_ge(S("hi_done"), c + 1)
                    sig("split_done", stt(w_lo[c % NW], stage[c % NS], WSCALE, w_hi[c % NW], ALU.mult, ALU.subtract))

                def x_lo(e):
                    for j in range(2):
                        dve.wait_ge(S("xhi_done"), 2 * e + j + 1)
                        sig("xlo_done", tt(xgT[e % 2][1][:, 4 * j:4 * j + 4, :].rearrange("p a b -> p (a b)"), ps[6 + j][:, :],
                                           xgT[e % 2][0][:, 4 * j:4 * j + 4, :].rearrange("p a b -> p (a b)"), ALU.subtract))

                def h_lo(e):
                    dve.wait_ge(S("hhi_done"), e + 1)
                    sig("hlo_done", tt(hgT[e % 2][1].rearrange("p a b -> p (a b)"), ps[6][:, :],
                                       hgT[e % 2][0].rearrange("p a b -> p (a b)"), ALU.subtract))

                for c in range(AHEAD):
                    split(c)
                x_lo(0)
                for c, (kind, e, hf) in enumerate(STEPS):
                    if c + AHEAD < len(STEPS):
                        split(c + AHEAD)
                    if kind == "u" and not hf and e >= 1:
                        h_lo(e - 1)
                    if kind == "d" and not hf and e == NE - 1:
                        h_lo(e)
                    if kind == "u" and hf:
                        if e + 1 < NE:
                            x_lo(e + 1)
                        dve.wait_ge(S("sgr_ready"), e + 1)
                        dve.wait_ge(S("gu_used"), e + 1)
                        if e >= 2:
                            dve.wait_ge(S("hgT_full"), e - 1)
                        b0 = 2 * (e % 2)
                        link(stt(sgr[e % 2], sgr[e % 2], 1.0, ps[b0][:, :], ALU.add, ALU.mult))
                        sig("h_ready", stt(hrow[e % 2], sgr[e % 2], 0.5 * HSCALE / WSCALE ** 2, ps[b0 + 1][:, :], ALU.mult, ALU.mult))
                for t in range(NT):
                    dve.wait_ge(S(f"yg_landed{t}"), 32)
                    link(stt(hres[:, t, :], yg[t][0], wsel[:, 0, t:t + 1], hres[:, t, :], ALU.mult, ALU.add))
                    sig("moe_done", stt(hres[:, t, :], yg[t][1], wsel[:, 1, t:t + 1], hres[:, t, :], ALU.mult, ALU.add))
            new_chain("dve_step_end", dict(before, moe_done=NT))
            norm_scale(hres, 3)
            dve.wait_ge(S("nf_landed"), 16)
            for t in range(NT):
                sig("y_done", stt(onorm[:, t, :], hres[:, t, :], stat[:, 3, t:t + 1], nf, ALU.mult, ALU.mult))


_INS = ["x", "w_in", "a_w2", "a_b2", "a_gain", "conv_w", "conv_b", "lru_wr", "lru_br", "lru_wi", "lru_bi", "lru_lambda",
        "w_gate", "b_gate", "w_branch", "w_out", "rel_bias", "norm1", "norm2", "norm_f", "moe_wrg", "moe_brg",
        "moe_wre", "moe_bre", "moe_wg", "moe_wu", "moe_wd"]


def kernel(**inputs):
    import concourse.bacc as _bacc
    from concourse.bass_utils import run_bass_kernel_spmd as _run

    nc = _bacc.Bacc("TRN2", target_bir_lowering=False, num_devices=1)
    arrays, d = {}, {}
    given = {n: np.ascontiguousarray(inputs[n]) for n in _INS}
    given.update(zip(("c_sq", "c_tab", "c_sel"), constants()))
    for name, a in given.items():
        arrays[f"in_{name}"] = a
        d[name] = nc.dram_tensor(f"in_{name}", a.shape, mybir.dt.from_np(a.dtype), kind="ExternalInput").ap()
    d["bias_scratch"] = nc.dram_tensor("bias_scratch", (2 * HEADS, P, T + P), F32, kind="Internal").ap()
    d["x2_rows"] = nc.dram_tensor("x2_rows", (T, D), F32, kind="Internal").ap()
    d["y_rows"] = nc.dram_tensor("y_rows", (NE * CAP, D), F32, kind="Internal").ap()
    out = nc.dram_tensor("out_0", (1, T, D), F32, kind="ExternalOutput").ap()
    build(nc, d, out)
    r = _run(nc, [arrays], core_ids=[0])
    return r.results[0]["out_0"]
```

```python
import math
from contextlib import ExitStack

import numpy as np
import concourse.bass as bass
from concourse import mybir

F32 = mybir.dt.float32
F16 = mybir.dt.float16
U32 = mybir.dt.uint32
I32 = mybir.dt.int32
ALU = mybir.AluOpType
ACT = mybir.ActivationFunctionType
AX = mybir.AxisListType

P = 128
T = 512
NT = T // P
D = 1024
KD = D // P
EPS = 1e-6
A_HEADS, A_DK, A_DV, A_RANK, A_TAU, A_CHUNK = 4, 48, 96, 16, 16.0, 64
NCH = T // A_CHUNK
HEADS, HD = 6, 64
IDX_HEADS, IDX_DIM = 4, 32
TOPK = 128
PATTERNS = ((128, 1), (512, 4), (2048, 16))
W = 384
KW = W // P
LRU_BLOCKS = 8
LRU_C = 8.0
BUCKETS, MAX_DIST = 32, 2048
NBR = 4
GROUPS, EPG = 4, 4
NE = GROUPS * EPG
HID = 512
KH = HID // P
CAP = P
CHUNK = 2048
WSCALE = 64.0
HSCALE = 1.0 / 16
AHEAD = 4
FIRST = 5
SPLIT_AT = (1, 2, 3, 5, 6)
NOWHERE = 65536
BIG = -1e30
TAKEN = -3e38
GELU_C = math.sqrt(2.0 / math.pi)

SPLITS = (("aq", 192), ("ak", 192), ("av", 384), ("ag", 384), ("alr", 16), ("bq", 384), ("bk", 384), ("bv", 384),
          ("iq", 128), ("ik", 32), ("iw", 4), ("cq", 384), ("ck", 384), ("cv", 384), ("dy", 384), ("dx", 384))
COL0 = {}
_c = 0
for _n, _w in SPLITS:
    COL0[_n] = _c
    _c += _w

PROJ = (("iq", "T"), ("ik", "ik"), ("iw", "iw"), ("dx", "T"), ("dy", "T"), ("alr", "T"), ("aqk", "pad"), ("av", "R"),
        ("ag", "R"), ("bq", "T"), ("bk", "T"), ("bv", "R"), ("cq", "T"), ("ck", "T"), ("cv", "R"))
WIDTH = dict(SPLITS)
CHUNKS, CEND = [], {}
for _n, _kind in PROJ:
    if _kind == "pad":
        CHUNKS += [(_kind, "w_in", COL0["aq"] + 2 * A_DK * _i, 2 * A_DK) for _i in range(4)]
    else:
        _w = WIDTH[_n]
        CHUNKS += [(_kind, "w_in", COL0[_n] + _i, min(P, _w)) for _i in range(0, _w, P)]
    CEND[_n] = len(CHUNKS)
EARLY_M = 2
for _m in range(EARLY_M):
    CHUNKS += [("gate", _b, _m * P, P) for _b in range(NBR)]
CEND["early"] = len(CHUNKS)
PAIR0 = {}
for _m in range(KD):
    for _b in (0, 2):
        PAIR0[_m, _b] = len(CHUNKS)
        if _m >= EARLY_M:
            CHUNKS += [("gate", _b, _m * P, P), ("gate", _b + 1, _m * P, P)]
        CHUNKS += [("branch", _b, _m * P, P)]
CEND["merge"] = len(CHUNKS)
CHUNKS += [("out", "w_out", _m * P, P) for _m in range(KD)]
NC_ = len(CHUNKS)
CS, CW, CLEN = 4, 5, KD * P

MAIN = (("xT", KD), ("iq", 1), ("ik", 1), ("iw", 1), ("dx", 3), ("dy", 3), ("alr", 1), ("aqk", 4), ("av", 3),
        ("ag", 3), ("bq", 3), ("bk", 3), ("bv", 3), ("cq", 3), ("ck", 3), ("cv", 3), ("oTa", 3),
        ("early", NBR * EARLY_M), ("oTc", 3), ("oTb", 3), ("gate", NBR * (KD - EARLY_M)), ("hgT", 8), ("x2T", 8))
MEND = {}
_c = 0
for _n, _w in MAIN:
    _c += _w
    MEND[_n] = _c

USED, _br = [], 0
for _c in range(NC_):
    _kind = CHUNKS[_c][0]
    if _c < CEND["cv"]:
        USED.append(("main_full", KD + _c + 1))
    elif _c < CEND["early"]:
        USED.append(("main_full", MEND["oTa"] + _c - CEND["cv"] + 1))
    elif _kind == "gate":
        USED.append(("main_full", MEND["oTb"] + sum(CHUNKS[_i][0] == "gate" for _i in range(CEND["early"], _c)) + 1))
    elif _kind == "branch":
        _br += 2
        USED.append(("br_full", _br))
    else:
        USED.append(("out_full", _c - CEND["merge"] + 1))

STEPS = []
for _e in range(NE + 1):
    if _e < NE:
        STEPS += [("g", _e, 0), ("g", _e, 1), ("u", _e, 0), ("u", _e, 1)]
    if _e >= 1:
        STEPS += [("d", _e - 1, 0), ("d", _e - 1, 1)]


def steps_to(kind, e):
    return STEPS.index((kind, e, 1)) + 1


def rel_bucket(dist):
    exact = BUCKETS // 2
    if dist < exact:
        return dist
    big = exact + int(np.float32(np.log(np.float32(dist) / np.float32(exact)) / np.float32(math.log(MAX_DIST / exact))
                                 * np.float32(BUCKETS - exact)))
    return min(big, BUCKETS - 1)


NCST = 3 * P + 8


def constants():
    sq = np.zeros((P, NCST), np.float32)
    sq[:, 0:P] = np.eye(P)
    r = np.arange(P)
    same = (r[:, None] // A_CHUNK) == (r[None, :] // A_CHUNK)
    sq[:, P:2 * P] = same & (r[None, :] >= r[:, None])
    sq[:, 2 * P:3 * P] = np.where(r[None, :] > r[:, None], BIG, 0.0)
    sq[:, 3 * P:3 * P + 4] = np.arange(4, 0, -1)
    sq[:, 3 * P + 4:3 * P + 8] = r[:, None] + P * np.arange(NT)[None, :]
    half = np.zeros((P, 2 * P), np.float16)
    half[:, 0:P] = r[:, None] < r[None, :]
    half[:, P:2 * P] = 1.0
    numbers = np.repeat(np.arange(CAP, dtype=np.float16), NE)[None, :]
    n = T + P
    tab = np.zeros((BUCKETS + 2, n), np.float32)
    for j in range(n):
        dist = T - 1 - j
        if dist < 0:
            tab[BUCKETS:, j] = BIG
            continue
        tab[rel_bucket(dist), j] = 1.0
        tab[BUCKETS + 1, j] = sum(dist % dil == 0 and dist <= win for win, dil in PATTERNS)
        c = tab[BUCKETS + 1, j]
        tab[BUCKETS + 1, j] = math.log(c) if c else BIG
    sel = np.zeros((2, 2 * HEADS), np.float32)
    sel[0, :HEADS] = 1.0
    sel[1, HEADS:] = 1.0
    return sq, half, numbers, tab, sel


def build(nc, d, out):
    ctx = ExitStack()
    with ctx:
        sems = {}

        def S(name):
            if name not in sems:
                sems[name] = ctx.enter_context(nc.semaphore(name))
            return sems[name]

        arena = ctx.enter_context(nc.sbuf_tensor("arena", [P, 49292], F32))

        def view(at, *shape):
            n = int(np.prod(shape))
            v = arena[:, at:at + n]
            if len(shape) == 2:
                v = v.rearrange("p (a b) -> p a b", b=shape[1])
            elif len(shape) == 3:
                v = v.rearrange("p (a b c) -> p a b c", b=shape[1], c=shape[2])
            return v

        cstage = [arena[:, i * CLEN:(i + 1) * CLEN] for i in range(CS)]
        c_hi = [arena[:, (CS + i) * CLEN:(CS + i) * CLEN + CLEN // 2].bitcast(F16) for i in range(CW)]
        c_lo = [arena[:, (CS + i) * CLEN + CLEN // 2:(CS + i + 1) * CLEN].bitcast(F16) for i in range(CW)]
        xnT = view(9216, KD, T)
        xh, xl = view(9216, KD, T // 2).bitcast(F16), view(9216 + 2048, KD, T // 2).bitcast(F16)
        XS = 13312
        xs = view(XS, NT, D)
        oA = view(XS, NT, W)
        oA2 = view(XS + 1536, NT, W)
        keR = view(XS + 3072, NT, 2 * P)
        oR = [view(XS, NT, W), view(XS + 1536, NT, W)]
        QKB = 17408
        bd = view(QKB, 2, KW, W)
        bqT, bkT = view(QKB, KW, T), view(QKB + 1536, KW, T)
        CVR = 20480
        xc, tr, ti, sq_ = (view(CVR + 1536 * i, KW, T) for i in range(4))
        bv, cqT, ckT, cv = view(CVR, NT, W), view(CVR + 1536, KW, T), view(CVR + 3072, KW, T), view(CVR + 4608, NT, W)
        hres = view(CVR, NT, D)
        AR = 26624
        aqT, akT, av, ag = view(AR, 2, T), view(AR + 1024, 2, T), view(AR + 2048, NT, W), view(AR + 3584, NT, W)
        DR = 31744
        dxp = view(DR, KW, T + 3)
        dyT = view(DR + 1548, KW, T)
        iqT, ikT, alrT = view(DR + 3084, T), view(DR + 3596, T), view(DR + 4108, T)
        OT = (DR + 1548, AR, AR + 1536, 36364)
        oTh = [view(a, KW, T // 2).bitcast(F16) for a in OT]
        oTl = [view(a + 768, KW, T // 2).bitcast(F16) for a in OT]
        SEL0 = 37900
        sel = [None, view(SEL0, 256), view(SEL0 + 256, 384), view(SEL0 + 640, 512)]
        rel = view(39052, 2, T)
        gate_t = view(39052, 2, T)
        GR = 40076
        zb, na, b16, eb, kd, ek = (view(GR + 1024 * i, 2, T) for i in range(6))
        seg = arena[:, GR + 5120:GR + 6144]
        attm = view(GR + 6144, 2, 4, P)
        St = view(GR + 7168, 2, NCH + 1, A_DV)
        bias = view(GR, 2 * HEADS, T)
        lg = [view(a, T) for a in (GR + 6144, GR + 6656, 39052)]
        pr = [view(a, T) for a in (GR + 7168, GR + 7680, 39052 + T)]
        pT = view(GR + 8192, 2, T)
        merged = view(GR, KD, T)
        mh, ml = view(XS, KD, T // 2).bitcast(F16), view(XS + 2048, KD, T // 2).bitcast(F16)
        gterm = view(SEL0, T)
        gate_early = [view(a + T * i, T) for a, n in ((DR, 3), (34828, 3), (XS + 3072, 2)) for i in range(n)]
        hg = view(9216, NT, D)
        hgT_f = view(28672, 2, T)
        sq_dump = view(DR, NT, P)
        EW = [24576, 36864]
        wg = [view(a, KD, HID) for a in EW]
        wu = [view(a + 4096, KD, HID) for a in EW]
        wd = [view(a + 8192, KH, D) for a in EW]
        hT = view(0, KH, T)
        sg = view(2048, 2, T)
        onorm = view(4096, NT, D)
        STAGE = [17408, 24576, 29696, 44172, 46220, 26624, 33292, 35340]
        EARLY = 5
        SPLIT = [40076, 42124, 37388, 0, 2048, 6144, 4096]
        NS, NW = len(STAGE), len(SPLIT)
        stage = [arena[:, a:a + CHUNK] for a in STAGE]
        w_hi = [arena[:, a:a + CHUNK // 2].bitcast(F16) for a in SPLIT]
        w_lo = [arena[:, a + CHUNK // 2:a + CHUNK].bitcast(F16) for a in SPLIT]
        gain2 = arena[:, 48268:48268 + D]
        onehot = view(4096, NT, CHUNK // 2).bitcast(F16)
        slots = view(32256, CHUNK // 2).bitcast(F16)
        xg = [arena[:, 9216 + D * i:9216 + D * (i + 1)] for i in range(2)]
        xgT = [[arena[:, 11264 + 1024 * i + 512 * j:11264 + 1024 * i + 512 * (j + 1)].bitcast(F16)
                .rearrange("p (k c) -> p k c", c=P) for j in range(2)] for i in range(2)]
        yout = [arena[:, XS + D * i:XS + D * (i + 1)] for i in range(2)]
        sgr = [arena[:, XS + 2048 + HID * i:XS + 2048 + HID * (i + 1)] for i in range(2)]
        hrow = [arena[:, XS + 3072 + HID * i:XS + 3072 + HID * (i + 1)] for i in range(2)]
        hgT = [[arena[:, 19456 + 512 * i + 256 * j:19456 + 512 * i + 256 * (j + 1)].bitcast(F16)
                .rearrange("p (k c) -> p k c", c=P) for j in range(2)] for i in range(2)]
        yg = [view(STAGE[t], 2, D) for t in range(NT)]
        nf = arena[:, 8192:8192 + D]

        def sb(name, shape):
            return ctx.enter_context(nc.sbuf_tensor(name, shape, F32))

        cst = sb("cst", [P, NCST])
        tokid = cst[:, 3 * P + 4:3 * P + 8]
        cst16 = ctx.enter_context(nc.sbuf_tensor("cst16", [P, 2 * P], F16))
        earlier, allones = cst16[:, 0:P], cst16[:, P:2 * P]
        ident, glamask, future, prio = cst[:, 0:P], cst[:, P:2 * P], cst[:, 2 * P:3 * P], cst[:, 3 * P:3 * P + 4]
        btab = arena[0:BUCKETS + 2, CVR + 4608:CVR + 4608 + T + P]
        bias_rows = arena[0:2 * HEADS, CVR + 5248:CVR + 5248 + T + P]
        relb = sb("relb", [BUCKETS + 2, 2 * HEADS])
        NROW = 74
        rows = sb("rows", [NROW, P])
        cols = sb("cols", [P, NROW])
        c_norm1, c_norm2, c_bgate = cols[:, 0:8], cols[:, 8:16], cols[:, 16:48]
        c_convw, c_convb, c_br, c_bi, c_lam, c_b2 = (cols[:, 48:60], cols[:, 60:63], cols[:, 63:66], cols[:, 66:69],
                                                     cols[:, 69:72], cols[:, 72:74])
        half = sb("half", [P, 38])
        sp = sb("sp", [P, 8, 3])
        ones = sb("ones", [P, 1])
        stat = sb("stat", [P, 4, NT])
        wa2 = sb("wa2", [A_RANK, 4 * 64])
        gain = sb("gain", [P, W])
        iw = sb("iw", [P, NT, IDX_HEADS])
        m8 = sb("m8", [P, 8])
        nmx = sb("nmx", [P, 4])
        lsum = sb("lsum", [P, 2, HEADS])
        rl = sb("rl", [P, 2, HEADS])
        ostat = sb("ostat", [P, NT * A_HEADS])
        wr = sb("wr", [P, KD, GROUPS + NE])
        rbias = sb("rbias", [P, GROUPS + NE])
        rt = sb("rt", [P, 16, NT, 4])
        gates = sb("gates", [P, NT, NE])
        rlog = sb("rlog", [P, NT, GROUPS + NE])
        glog = sb("glog", [P, NT, GROUPS])
        elog = sb("elog", [P, NT, NE])
        ssq = sb("ssq", [P, NT, KD])
        sel16 = ctx.enter_context(nc.sbuf_tensor("sel16", [P, NT, NE], F16))
        selj = sb("selj", [P, 2, NT, NE])
        rank = ctx.enter_context(nc.sbuf_tensor("rank", [P, NT, NE], F16))
        total = sb("total", [P, 2])
        wsel = sb("wsel", [P, 2, NT])
        told = ctx.enter_context(nc.sbuf_tensor("told", [P, NT, 3, NE], F16))
        slotv = sb("slotv", [P, 3, NE])
        row_of = ctx.enter_context(nc.sbuf_tensor("row_of", [P, NE], U32))
        token_of = ctx.enter_context(nc.sbuf_tensor("token_of", [P, NE], U32))
        dense = ctx.enter_context(nc.sbuf_tensor("dense", [1, 1], I32))

        ps = [ctx.enter_context(nc.psum_tensor(f"bank{i}", [P, 512], F32)) for i in range(8)]
        main, aux, lgb = ps[0:2], ps[2:4], ps[4:6]
        att_bank = (aux, main)
        oa_bank = ((ps[6], ps[7]), (ps[4], ps[5]))
        rt_bank = (ps[6], ps[7], ps[2], ps[3])
        scratch, x2_rows, y_rows = d["bias_scratch"], d["x2_rows"], d["y_rows"]

        block = ctx.enter_context(nc.Block())

        def onehot_views(t):
            return (onehot[:, t, :].rearrange("p (c e) -> p c e", e=NE), slots.rearrange("p (c e) -> p c e", e=NE),
                    rank[:, t, :].unsqueeze(1).to_broadcast([P, P, NE]))

        def landed_count(c):
            return 16 * sum(2 if CHUNKS[j][0] == "branch" else 1 for j in range(c % CS, c + 1, CS))

        def split_views(c, halves):
            kind, _, _, width = CHUNKS[c]
            dst, src = halves[c % CW], cstage[c % CS]
            if kind == "ik":
                return (dst.rearrange("p (k h c) -> p k h c", h=IDX_HEADS, c=IDX_DIM),
                        src[:, 0:KD * width].rearrange("p (k c) -> p k c", c=width).unsqueeze(2)
                        .to_broadcast([P, KD, IDX_HEADS, width]))
            if kind == "pad":
                return (dst.rearrange("p (a c) -> p a c", c=64)[:, :, 0:A_DK],
                        src[:, 0:KD * width].rearrange("p (a c) -> p a c", c=A_DK))
            n = 2 * KW * P if kind == "branch" else KD * width
            return dst[:, 0:n], src[:, 0:n]

        @block.sync
        def _(sp_):
            for t in range(NT):
                sp_.dma_start(xs[:, t, :], d["x"][0, t * P:(t + 1) * P, :]).then_inc(S(f"x_landed{t}"), 16)

            def mixer_load(c):
                kind, name, col, width = CHUNKS[c]
                if c >= CS:
                    sp_.wait_ge(S("c_split"), c - CS + 1)
                landed, slot = S(f"c_landed{c % CS}"), cstage[c % CS]
                if kind == "branch":
                    for j in range(2):
                        src = d["w_branch"][0, name + j].rearrange("(k p) n -> p k n", p=P)[:, :, col:col + width]
                        sp_.dma_start(slot[:, j * KW * P:(j + 1) * KW * P].rearrange("p (k n) -> p k n", n=P), src
                                      ).then_inc(landed, 16)
                    return
                src = d["w_gate"][0, name] if kind == "gate" else d[name][0]
                sp_.dma_start(slot[:, 0:KD * width].rearrange("p (k n) -> p k n", n=width),
                              src.rearrange("(k p) n -> p k n", p=P)[:, :, col:col + width]).then_inc(landed, 16)

            def stage_load(c):
                kind, e, hf = STEPS[c]
                if kind == "d":
                    src = d["moe_wd"][0, e].rearrange("(k p) n -> p k n", p=P)[:, 2 * hf:2 * hf + 2, :]
                else:
                    src = d["moe_w" + kind][0, e].rearrange("(k p) n -> p k n", p=P)[:, 4 * hf:4 * hf + 4, :]
                sp_.dma_start(stage[c % NS].rearrange("p (k n) -> p k n", k=src.shape[1]), src
                              ).then_inc(S(f"stage_landed{c % NS}"), 16)

            for c in range(NC_):
                if c == CEND["early"] + 9:
                    sp_.wait_ge(S("o_done"), 2 * NT)
                    sp_.dma_start(hres, d["x"][0].rearrange("(t p) n -> p t n", p=P)).then_inc(S("xres_landed"), 16)
                    for e in range(EARLY):
                        stage_load(e)
                mixer_load(c)
            sp_.wait_ge(S("merge_done"), 4 * KD)
            for c in range(EARLY, NS):
                stage_load(c)
            for t in range(NT):
                sp_.wait_ge(S("x2_ready"), t + 1)
                sp_.dma_start(x2_rows[t * P:(t + 1) * P, :], xs[:, t, :]).then_inc(S("x2_stored"), 16)
            for c in range(NS, NS + FIRST):
                sp_.wait_ge(S("split_done"), c - NS + 1)
                stage_load(c)
            sp_.wait_ge(S("dense_known"), 1)
            over = sp_.value_load(dense[:, :], min_val=0, max_val=1)
            with sp_.If(over):
                for c in range(NS):
                    sp_.wait_ge(S(f"stage_landed{c}"), 32 if c < FIRST else 16)
                sp_.wait_ge(S("split_done"), NW)
                for e in range(NE):
                    if e >= 2:
                        sp_.wait_ge(S("e_used"), e - 1)
                    s = e % 2
                    for w, name in ((wg, "moe_wg"), (wu, "moe_wu"), (wd, "moe_wd")):
                        sp_.dma_start(w[s], d[name][0, e].rearrange("(k p) n -> p k n", p=P)
                                      ).then_inc(S(f"e_landed{s}"), 16)
            with sp_.Else():
                for c in range(NS + FIRST, len(STEPS)):
                    sp_.wait_ge(S("split_done"), c - NS + 1)
                    stage_load(c)
                for i in range(2):
                    sp_.wait_ge(S(f"y_stored{i}"), 16 * (NE // 2))
                sp_.wait_ge(S("split_done"), len(STEPS))
                for t in range(NT):
                    sp_.dma_start(yg[t], y_rows.rearrange("(j t p) n -> t p j n", j=2, p=P)[t]
                                  ).then_inc(S(f"yg_landed{t}"), 16)
            for t in range(NT):
                sp_.wait_ge(S("y_done"), t + 1)
                sp_.dma_start(out[0, t * P:(t + 1) * P, :], onorm[:, t, :]).then_inc(S("stored"), 16)
            sp_.wait_ge(S("stored"), 16 * NT)

        @block.gpsimd
        def _(pool):
            pool.dma_start(cst[:, :], d["c_sq"]).then_inc(S("cst_landed"), 16)
            pool.memset(rows[:, :], 0.0).then_inc(S("pool_step"), 1)
            pool.dma_start(btab, d["c_tab"]).then_inc(S("btab_landed"), 16)
            pool.dma_start(relb[0:BUCKETS, :], d["rel_bias"]).then_inc(S("btab_landed"), 16)
            pool.dma_start(relb[BUCKETS:BUCKETS + 2, :], d["c_sel"]).then_inc(S("btab_landed"), 16)
            pool.memset(bd, 0.0).then_inc(S("pool_step"), 1)
            pool.memset(wa2[:, :], 0.0).then_inc(S("pool_step"), 1)
            pool.wait_ge(S("pool_step"), 3)
            bw = W // LRU_BLOCKS
            for m, name in enumerate(("lru_wr", "lru_wi")):
                for n in range(LRU_BLOCKS):
                    r = n * bw
                    while r < (n + 1) * bw:
                        e = min((n + 1) * bw, (r // P + 1) * P)
                        pool.dma_start(bd[r % P:r % P + e - r, m, r // P, n * bw:(n + 1) * bw],
                                       d[name][0, n, r - n * bw:e - n * bw, :]).then_inc(S("bd_landed"), 16)
                        r = e
            for h in range(A_HEADS):
                pool.dma_start(wa2[:, 64 * h:64 * h + A_DK], d["a_w2"][0, :, h * A_DK:(h + 1) * A_DK]
                               ).then_inc(S("wa2_landed"), 16)
            pool.dma_start(gain[:, :], d["a_gain"][0:1, :].to_broadcast([P, W])).then_inc(S("gain_landed"), 16)
            pool.dma_start(wr[:, :, 0:GROUPS], d["moe_wrg"][0].rearrange("(k p) n -> p k n", p=P)
                           ).then_inc(S("wr_landed"), 16)
            pool.dma_start(wr[:, :, GROUPS:], d["moe_wre"][0].rearrange("(k p) n -> p k n", p=P)
                           ).then_inc(S("wr_landed"), 16)
            pool.dma_start(rbias[:, 0:GROUPS], d["moe_brg"][0:1, :].to_broadcast([P, GROUPS])).then_inc(S("wr_landed"), 16)
            pool.dma_start(rbias[:, GROUPS:], d["moe_bre"][0:1, :].to_broadcast([P, NE])).then_inc(S("wr_landed"), 16)
            pool.dma_start(cst16[:, :], d["c_half"]).then_inc(S("wr_landed"), 16)
            pool.wait_ge(S("bias_rows_ready"), 2)
            pool.dma_start(scratch, bias_rows.unsqueeze(1).to_broadcast([2 * HEADS, P, T + P])
                           ).then_inc(S("scratch_stored"), 16)
            pool.wait_ge(S("scratch_stored"), 16)
            pool.wait_ge(S("oa_ready"), 1)
            pool.wait_ge(S("attm_ready"), 2 * NT)
            pool.wait_ge(S("gla_pe_done"), NT)
            toeplitz = bass.AP(scratch.tensor, scratch.offset + P - 1,
                               [(T + P - 1, P), (P * (T + P), 2 * HEADS), (1, T)])
            pool.dma_start(bias, toeplitz).then_inc(S("bias_landed"), 16)
            pool.wait_ge(S("o_done"), 2 * NT)
            pool.dma_start(gain2, d["norm2"][0:1, :].to_broadcast([P, D])).then_inc(S("gain2_landed"), 16)
            pool.wait_ge(S("merge_done"), NBR * EARLY_M)
            pool.dma_start(slots, d["c_slots"].to_broadcast([P, CAP * NE])).then_inc(S("gain2_landed"), 16)
            pool.wait_ge(S("x2_ready"), NT)
            pool.memset(arena[:, 9216:9216 + 2 * D], 0.0).then_inc(S("xg_clear"), 1)
            pool.wait_ge(S("x2_stored"), 16 * NT)
            pool.wait_ge(S("dense_known"), 1)
            over = pool.value_load(dense[:, :], min_val=0, max_val=1)
            with pool.If(over):
                pool.wait_ge(S("x2_stored"), 16 * NT)
            with pool.Else():
                for n in range(NE + 4):
                    if n < NE:
                        e = n
                        if e < 2:
                            pool.wait_ge(S("xg_clear"), 1)
                        else:
                            pool.wait_ge(S("xgT_full"), 2 * (e - 1))
                        pool.indirect_dma_start(out=xg[e % 2], out_offset=None, in_=x2_rows,
                                                in_offset=bass.IndirectOffsetOnAxis(ap=token_of[:, e:e + 1], axis=0),
                                                bounds_check=T - 1, oob_is_err=False).then_inc(S(f"xg_landed{e % 2}"), 16)
                    if n >= 4:
                        e = n - 4
                        pool.wait_ge(S("y_out"), 2 * (e + 1))
                        if e >= 2:
                            pool.wait_ge(S(f"y_stored{e % 2}"), 16 * (e // 2))
                        pool.indirect_dma_start(out=y_rows, out_offset=bass.IndirectOffsetOnAxis(ap=row_of[:, e:e + 1], axis=0),
                                                in_=yout[e % 2], in_offset=None, bounds_check=2 * T - 1, oob_is_err=False
                                                ).then_inc(S(f"y_stored{e % 2}"), 16)

        @block.scalar
        def _(act):
            state = {"main": 0, "step": 0, "chunk": 0}

            def link(ins):
                state["step"] += 1
                ins.then_inc(S("act_step"), 1)
                act.wait_ge(S("act_step"), state["step"])

            def drain_main(fn):
                n = state["main"]
                act.wait_ge(S("main_full"), n + 1)
                fn(main[n % 2]).then_inc(S("main_empty"), 1)
                state["main"] = n + 1

            def csplit(c):
                kind, name, col, width = CHUNKS[c]
                act.wait_ge(S(f"c_landed{c % CS}"), landed_count(c))
                if c >= CW:
                    act.wait_ge(S(USED[c - CW][0]), USED[c - CW][1])
                act.activation(*split_views(c, c_hi), ACT.Copy, scale=WSCALE).then_inc(S("c_hi_done"), 1)

            act.wait_ge(S("pool_step"), 1)
            at = 0
            for name, n in (("norm1", 8), ("norm2", 8), ("b_gate", 32), ("conv_w", 12), ("conv_b", 3), ("lru_br", 3),
                            ("lru_bi", 3), ("lru_lambda", 3)):
                src = d[name][0]
                if len(src.shape) == 2:
                    src = src.rearrange("a b -> (a b)")
                act.dma_start(rows[at:at + n, :], src.rearrange("(a b) -> a b", b=P)).then_inc(S("rows_landed"), 16)
                at += n
            for h in range(A_HEADS):
                r, c = at + h // 2, 64 * (h % 2)
                act.dma_start(rows[r:r + 1, c:c + A_DK], d["a_b2"][0:1, h * A_DK:(h + 1) * A_DK]
                               ).then_inc(S("rows_landed"), 16)
            for t in range(NT):
                act.wait_ge(S(f"x_landed{t}"), 16)
                act.activation(view(CVR + D * t, D), xs[:, t, :], ACT.Square,
                               accum_out=stat[:, 0, t:t + 1]).then_inc(S("ss_ready"), 1)
            act.wait_ge(S("ms_ready"), 1)
            act.activation(stat[:, 2, :], stat[:, 1, :], ACT.Sqrt).then_inc(S("rms_ready"), 1)
            for c in range(2):
                csplit(c)
            act.wait_ge(S("cols_ready"), 1)
            def hi_main(dst, **kw):
                n = state["main"]
                act.wait_ge(S("main_full"), n + 1)
                act.activation(dst, main[n % 2][:, :], ACT.Copy, **kw).then_inc(S("main_hi"), 1)
                state["main"] = n + 1

            def tile_out(dst, scale=1.0, rows_=P, n=T):
                c = state["chunk"]
                if c + AHEAD < NC_:
                    csplit(c + AHEAD)
                state["chunk"] = c + 1
                kind = CHUNKS[c][0]
                drain_main(lambda b: act.activation(dst, b[0:rows_, 0:n] if kind != "R" else
                                                    b[:, :].rearrange("p (t c) -> p t c", c=P), ACT.Copy, scale=scale / WSCALE))

            def group_T(dst, scale=1.0):
                for c in range(KW):
                    tile_out(dst[:, c, :], scale)

            def group_R(dst):
                for c in range(KW):
                    tile_out(dst[:, :, c * P:(c + 1) * P])

            for c in range(KD):
                hi_main(xh[:, c, :], scale=c_norm1[:, c:c + 1])
                if c in (1, 3):
                    csplit(c // 2 + 2)
            act.wait_ge(S("lam_abs"), 1)
            act.activation(sp[:, 1, :], sp[:, 0, :], ACT.Exp).then_inc(S("lam_exp"), 1)
            tile_out(iqT, IDX_DIM ** -0.5)
            tile_out(ikT)
            tile_out(iw[:, :, :].rearrange("p a b -> p (a b)"), IDX_HEADS ** -0.5, n=NT * IDX_HEADS)
            group_T(dxp[:, :, 3:3 + T])
            n = 0
            for i in range(1, NT):
                for h in range(IDX_HEADS):
                    if n in (2, 4):
                        tile_out(dyT[:, n // 2 - 1, :])
                    act.wait_ge(S("idx_full"), n + 1)
                    if n >= 2:
                        act.wait_ge(S("rel_used"), n - 1)
                    act.activation(rel[:, n % 2, 0:(i + 1) * P], lgb[n % 2][:, 0:(i + 1) * P], ACT.Relu
                                   ).then_inc(S("rel_ready"), 1)
                    n += 1
            tile_out(dyT[:, 2, :])
            act.wait_ge(S("cols_ready"), 2)
            n = 0
            for m, dst in ((0, tr), (1, ti)):
                for c in range(KW):
                    act.wait_ge(S("lru_full"), n + 1)
                    act.activation(dst[:, c, :], aux[n % 2][:, :], ACT.Tanh, scale=0.5,
                                   bias=half[:, 32 + 3 * m + c:33 + 3 * m + c]).then_inc(S("lru_tanh"), 1)
                    n += 1
            act.wait_ge(S("sp_ready"), 1)
            act.wait_ge(S("lru_tanh"), 3)
            for c in range(KW):
                act.activation(tr[:, c, :], tr[:, c, :], ACT.Tanh, scale=sp[:, 7, c:c + 1], bias=sp[:, 7, c:c + 1]
                               ).then_inc(S("lru_t2"), 1)
            act.wait_ge(S("lru_t2"), 3)
            act.wait_ge(S("scratch_stored"), 16)
            act.activation(sq_, tr, ACT.Sqrt).then_inc(S("lru_sqrt"), 1)
            tile_out(alrT[0:A_RANK, :], rows_=A_RANK)
            for dst, scale in ((aqT, A_DK ** -0.5), (akT, 1.0)):
                for i in range(2):
                    tile_out(dst[:, i, :], scale)
            group_R(av)
            act.wait_ge(S("gla_na"), 1)
            link(act.activation(na, na, ACT.Exp))
            act.activation(na, na, ACT.Ln, bias=ones[:, 0:1]).then_inc(S("gla_ln"), 1)
            act.wait_ge(S("lru_u"), 1)
            act.activation(sq_, dyT, ACT.Square).then_inc(S("y2_ready"), 1)
            tile_out(ag[:, :, 0:P])
            act.wait_ge(S("gelu_in"), 1)
            act.activation(sq_, sq_, ACT.Tanh, scale=GELU_C).then_inc(S("gelu_tanh"), 1)
            tile_out(ag[:, :, P:2 * P])
            act.wait_ge(S("gla_b"), 1)
            act.activation(eb, b16, ACT.Exp, scale=1.0 / A_TAU).then_inc(S("gla_e"), 1)
            act.activation(kd, b16, ACT.Exp, scale=-1.0 / A_TAU).then_inc(S("gla_e"), 1)
            act.wait_ge(S("gla_d"), 1)
            act.activation(ek, ek, ACT.Exp, scale=1.0 / A_TAU).then_inc(S("gla_e"), 1)
            tile_out(ag[:, :, 2 * P:3 * P])
            group_T(bqT, HD ** -0.5)
            group_T(bkT)
            for i in range(2):
                act.wait_ge(S("ke_full"), i + 1)
                act.activation(keR[:, :, i * P:(i + 1) * P], ps[6 + i][:, :].rearrange("p (t c) -> p t c", c=P), ACT.Copy
                               ).then_inc(S("ke_ready"), 1)
            act.wait_ge(S("lru_u"), 2)
            group_R(bv)
            for c in range(2):
                tile_out(cqT[:, c, :], HD ** -0.5)
            for t in range(NT):
                act.wait_ge(S("oa_full"), t + 1)
                for hh in range(2):
                    act.activation(oA[:, t, :].rearrange("p (i h v) -> p i h v", h=2, v=A_DV)[:, :, hh, :],
                                   oa_bank[t % 2][hh][:, 0:2 * A_DV].rearrange("p (i v) -> p i v", v=A_DV), ACT.Copy
                                   ).then_inc(S("oa_copied"), 1)
            act.wait_ge(S("oa_copied"), 2 * NT)
            act.activation(oA2, oA, ACT.Square).then_inc(S("oa_sq"), 1)
            act.wait_ge(S("oa_ms"), 1)
            act.activation(ostat[:, :], ostat[:, :], ACT.Sqrt).then_inc(S("oa_rms"), 1)
            act.wait_ge(S("oa_mean"), 1)
            act.activation(oA2, ag, ACT.Tanh, scale=0.5).then_inc(S("oa_tanh"), 1)
            tile_out(cqT[:, 2, :], HD ** -0.5)
            group_T(ckT)
            group_R(cv)
            for c in range(KW):
                hi_main(oTh[0][:, c, :])

            def probs(n):
                i = (n // HEADS) % NT
                nk = (i + 1) * P
                act.wait_ge(S("lg_ready"), n + 1)
                if n >= 3:
                    act.wait_ge(S("pT_full"), n - 2)
                if n >= 2 * HEADS and n % HEADS == 0:
                    act.wait_ge(S("rl_ready"), n // HEADS - 1)
                act.activation(pr[n % 3][:, 0:nk], lg[n % 3][:, 0:nk], ACT.Exp, bias=nmx[:, n % 4:n % 4 + 1],
                               accum_out=lsum[:, (n // HEADS) % 2, n % HEADS:n % HEADS + 1]).then_inc(S("p_ready"), 1)

            def ptrans(n):
                i = (n // HEADS) % NT
                nk = (i + 1) * P
                act.wait_ge(S("pT_full"), n + 1)
                if n >= 2:
                    act.wait_ge(S("pT_used"), n - 1)
                act.activation(pT[:, n % 2, 0:nk], aux[n % 2][:, 0:nk], ACT.Copy).then_inc(S("pT_ready"), 1)

            def early_gate(g):
                col = half[:, 8 * (g % NBR) + g // NBR:8 * (g % NBR) + g // NBR + 1]
                drain_main(lambda b: act.activation(gate_early[g], b[:, :], ACT.Tanh, scale=0.5 / WSCALE, bias=col))
                csplit(state["chunk"] + AHEAD)
                state["chunk"] += 1

            units = 2 * NT * HEADS
            for n in range(units + 2):
                if n < units:
                    probs(n)
                if n >= 2:
                    ptrans(n - 2)
                if n % HEADS == 1 and HEADS < n < units:
                    early_gate(n // HEADS - 1)
            early_gate(2 * NT - 1)
            for k in (2, 1):
                for c in range(KW):
                    hi_main(oTh[k][:, c, :])

            def merged_hi(m):
                act.wait_ge(S("merge_done"), NBR * (m + 1))
                act.activation(mh[:, m, :], merged[:, m, :], ACT.Copy, scale=0.5 / WSCALE).then_inc(S("mh_done"), 1)

            for n in range(NBR * KD):
                m, b_ = n // NBR, n % NBR
                if m < EARLY_M:
                    if b_ % 2 == 0:
                        csplit(state["chunk"] + AHEAD)
                        state["chunk"] += 1
                    if b_ == 2 and m:
                        merged_hi(m - 1)
                    continue
                csplit(state["chunk"] + AHEAD)
                if b_ % 2 and state["chunk"] + 1 + AHEAD < NC_:
                    csplit(state["chunk"] + 1 + AHEAD)
                state["chunk"] += 1 + b_ % 2
                act.wait_ge(S("merge_done"), n - 1)
                drain_main(lambda b: act.activation(
                    gate_t[:, n % 2, :], b[:, :], ACT.Tanh, scale=0.5 / WSCALE, bias=half[:, 8 * b_ + m:8 * b_ + m + 1]))
                if b_ == 2 and m:
                    merged_hi(m - 1)
            merged_hi(KD - 1)
            def split(c):
                act.wait_ge(S(f"stage_landed{c % NS}"), 16 * (c // NS + 1))
                if c >= NW:
                    act.wait_ge(S("chunk_used"), c - NW + 1)
                act.activation(w_hi[c % NW], stage[c % NS], ACT.Copy, scale=WSCALE).then_inc(S("hi_done"), 1)

            act.wait_ge(S("ml_done"), KD)
            for m in range(KD):
                if CEND["merge"] + AHEAD + m < NC_:
                    csplit(CEND["merge"] + AHEAD + m)
                act.wait_ge(S("h_done"), m + 1)
                if m:
                    act.wait_ge(S("ssq_ready"), NT * m)
                for t in range(NT):
                    act.activation(sq_dump[:, t, :], hres[:, t, m * P:(m + 1) * P], ACT.Square, accum_out=ssq[:, t, m:m + 1]
                                   ).then_inc(S("ssq_ready"), 1)
                if m >= 2:
                    act.wait_ge(S("hgT_used"), m - 1)
                drain_main(lambda b, m=m: act.activation(hgT_f[:, m % 2, :], b[:, :], ACT.Copy))
                if m in SPLIT_AT:
                    if m > KD - AHEAD:
                        act.wait_ge(S("c_split"), NC_)
                    split(SPLIT_AT.index(m))
            act.dma_start(nf, d["norm_f"].rearrange("(a n) -> a n", a=1).to_broadcast([P, D])).then_inc(S("nf_landed"), 16)
            act.wait_ge(S("ms_ready"), 2)
            act.activation(stat[:, 2, :], stat[:, 1, :], ACT.Sqrt).then_inc(S("rms_ready"), 1)

            act.wait_ge(S("rstd2_ready"), 1)
            for t in range(NT):
                act.activation(xs[:, t, :], hg[:, t, :], ACT.Copy, scale=stat[:, 3, t:t + 1]).then_inc(S("x2_ready"), 1)
            act.wait_ge(S("rt_sub"), 1)
            act.activation(rt[:, 2, :, :], rt[:, 1, :, :], ACT.Exp).then_inc(S("rt_exp"), 1)
            act.wait_ge(S("rt_diff"), 1)
            act.activation(rt[:, 9, :, 0], rt[:, 8, :, 0], ACT.Exp).then_inc(S("rt_exp"), 1)
            act.wait_ge(S("token_full"), 1)
            for c in range(FIRST, NW):
                split(c)
            act.wait_ge(S("dense_known"), 1)
            over = act.value_load(dense[:, :], min_val=0, max_val=1)
            with act.If(over):
                act.wait_ge(S("xg_clear"), 1)
                for c in range(KD):
                    drain_main(lambda b, c=c: act.activation(xnT[:, c, :], b[:, :], ACT.Copy))
                n = 0
                for e in range(NE):
                    for m in range(KH):
                        act.wait_ge(S("gu_full"), n + 1)
                        if n >= 2:
                            act.wait_ge(S("hT_ready"), n - 1)
                        act.activation(sg[:, n % 2, :], ps[n % 2][:, :], ACT.Tanh, scale=0.5).then_inc(S("sg_ready"), 1)
                        n += 1
            with act.Else():
                def x_hi(e):
                    for j in range(2):
                        act.wait_ge(S("xgT_full"), 2 * e + j + 1)
                        if e >= 2:
                            act.wait_ge(S("chunk_used"), steps_to("u", e - 2))
                        act.activation(xgT[e % 2][0][:, 4 * j:4 * j + 4, :].rearrange("p a b -> p (a b)"), ps[6 + j][:, :],
                                       ACT.Copy).then_inc(S("xhi_done"), 1)

                x_hi(0)
                for c, (kind, e, hf) in enumerate(STEPS):
                    if NW <= c + FIRST < len(STEPS):
                        split(c + FIRST)
                    if kind == "g" and hf:
                        act.wait_ge(S("chunk_used"), steps_to("g", e))
                        if e >= 2:
                            act.wait_ge(S("h_ready"), e - 1)
                        act.activation(sgr[e % 2], ps[2 * (e % 2)][:, :], ACT.Tanh, scale=0.5 / WSCALE).then_inc(S("sgr_ready"), 1)
                    if kind == "u" and not hf and e >= 1:
                        act.wait_ge(S("hgT_full"), e)
                        if e >= 3:
                            act.wait_ge(S("chunk_used"), steps_to("d", e - 3))
                        act.activation(hgT[(e - 1) % 2][0].rearrange("p a b -> p (a b)"), ps[6][:, :], ACT.Copy
                                       ).then_inc(S("hhi_done"), 1)
                    if kind == "u" and hf and e + 1 < NE:
                        x_hi(e + 1)
                    if kind == "d" and hf:
                        act.wait_ge(S("chunk_used"), steps_to("d", e))
                        if e >= 2:
                            act.wait_ge(S(f"y_stored{e % 2}"), 16 * (e // 2))
                        for j in range(2):
                            act.activation(yout[e % 2][:, 512 * j:512 * (j + 1)], ps[4 + j][:, :], ACT.Copy,
                                           scale=1.0 / (WSCALE * HSCALE)).then_inc(S("y_out"), 1)
                    if kind == "d" and not hf and e == NE - 1:
                        act.wait_ge(S("hgT_full"), NE)
                        act.activation(hgT[(NE - 1) % 2][0].rearrange("p a b -> p (a b)"), ps[6][:, :], ACT.Copy
                                       ).then_inc(S("hhi_done"), 1)
            def rms(t):
                act.wait_ge(S("ms_ready"), 3 + t)
                act.activation(stat[:, 2, t:t + 1], stat[:, 1, t:t + 1], ACT.Sqrt).then_inc(S("rms_ready"), 1)

            for t in range(NT):
                act.wait_ge(S("moe_done"), t + 1)
                act.activation(onorm[:, t, :], hres[:, t, :], ACT.Square, accum_out=stat[:, 0, t:t + 1]).then_inc(S("ss_ready"), 1)
                if t >= 1:
                    rms(t - 1)
            rms(NT - 1)

        @block.tensor
        def _(pe):
            state = {"main": 0, "chunk": 0}

            def main_bank():
                n = state["main"]
                if n >= 2:
                    pe.wait_ge(S("main_empty"), n - 1)
                return main[n % 2]

            def main_full(ins):
                ins.then_inc(S("main_full"), 1)
                state["main"] += 1

            def products(outb, lhs, rhs, first, last_):
                pe.matmul(outb, lhs[0], rhs[0], start=first, stop=False, skip_group_check=True)
                pe.matmul(outb, lhs[0], rhs[1], start=False, stop=False, skip_group_check=True)
                return pe.matmul(outb, lhs[1], rhs[0], start=False, stop=last_, skip_group_check=True)

            def next_chunk():
                c = state["chunk"]
                pe.wait_ge(S("c_split"), c + 1)
                state["chunk"] = c + 1
                return c_hi[c % CW], c_lo[c % CW]

            def tile_T(rows_=P):
                w = [v[:, 0:KD * rows_].rearrange("p (k n) -> p k n", n=rows_) for v in next_chunk()]
                b = main_bank()
                for k in range(KD):
                    last = products(b[0:rows_, :], [v[:, k, :] for v in w], (xh[:, k, :], xl[:, k, :]), k == 0, k == KD - 1)
                main_full(last)

            def rows_tile(b, xs_, width, last_column=False):
                w = [v[:, 0:KD * width].rearrange("p (k n) -> p k n", n=width) for v in next_chunk()]
                for t in range(NT):
                    for k in range(KD):
                        if t == 0 and k == KD - 1 and last_column:
                            pe.wait_ge(S("ml_done"), KD)
                        last = products(b[:, t * width:(t + 1) * width], [v[:, k, t * P:(t + 1) * P] for v in xs_],
                                        [v[:, k, :] for v in w], k == 0, k == KD - 1)
                return last

            def tile_R(width=P):
                main_full(rows_tile(main_bank(), (xh, xl), width))

            def proj_t(n=KW):
                for _ in range(n):
                    tile_T()

            def proj_r():
                for _ in range(KW):
                    tile_R()

            pe.wait_ge(S("cst_landed"), 16)
            pe.wait_ge(S("rows_landed"), 16 * 12)
            pe.transpose(ps[6][:, 0:NROW], rows[:, :], ident[0:NROW, 0:NROW]).then_inc(S("rows_T"), 1)
            pe.wait_ge(S("xs_ready"), NT)
            for c in range(KD):
                b = main_bank()
                for t in range(NT):
                    last = pe.transpose(b[:, t * P:(t + 1) * P], xs[:, t, c * P:(c + 1) * P], ident)
                main_full(last)
            pe.wait_ge(S("btab_landed"), 48)
            pe.matmul(aux[0][0:2 * HEADS, :], relb[:, :], btab[:, 0:T], start=True, stop=True)
            pe.matmul(aux[1][0:2 * HEADS, 0:P], relb[:, :], btab[:, T:T + P], start=True, stop=True
                      ).then_inc(S("bias_mm"), 1)
            pe.wait_ge(S("main_empty"), MEND["xT"])
            tile_T()
            tile_T()
            tile_R(IDX_HEADS)
            proj_t()
            pe.wait_ge(S("main_empty"), MEND["iw"])
            n = 0
            for i in range(1, NT):
                for h in range(IDX_HEADS):
                    if n in (2, 4):
                        tile_T()
                    if n >= 2:
                        pe.wait_ge(S("rel_ready"), n - 1)
                    r = slice(IDX_DIM * h, IDX_DIM * (h + 1))
                    pe.matmul(lgb[n % 2][:, 0:(i + 1) * P], iqT[r, i * P:(i + 1) * P], ikT[r, 0:(i + 1) * P],
                              start=True, stop=True).then_inc(S("idx_full"), 1)
                    n += 1
            tile_T()
            pe.wait_ge(S("bd_landed"), 16 * 20)
            pe.wait_ge(S("xc_ready"), 1)
            pe.wait_ge(S("bias_rows_ready"), 2)
            n = 0
            for m in range(2):
                for c in range(KW):
                    if n >= 2:
                        pe.wait_ge(S("lru_tanh"), n - 1)
                    ks = [k for k in range(KW) if abs(k - c) <= 1]
                    for k in ks:
                        last = pe.matmul(aux[n % 2][:, :], bd[:, m, k, c * P:(c + 1) * P], xc[:, k, :],
                                         start=(k == ks[0]), stop=(k == ks[-1]))
                    last.then_inc(S("lru_full"), 1)
                    n += 1
            tile_T(A_RANK)
            proj_t(4)
            pe.wait_ge(S("wa2_landed"), 64)
            pe.wait_ge(S("main_empty"), MEND["alr"])
            pe.wait_ge(S("cols_ready"), 1)
            for i in range(2):
                pe.matmul(ps[6 + i][:, :], wa2[:, i * P:(i + 1) * P], alrT[0:A_RANK, :], start=True, stop=True
                          ).then_inc(S("z_full"), 1)
            proj_r()
            proj_r()
            proj_t()
            proj_t()
            pe.wait_ge(S("ke_T"), 1)
            pe.wait_ge(S("zb_ready"), 2)
            for i in range(2):
                for t in range(NT):
                    last = pe.transpose(ps[6 + i][:, t * P:(t + 1) * P], akT[:, i, t * P:(t + 1) * P], ident)
                last.then_inc(S("ke_full"), 1)
            proj_r()
            pe.wait_ge(S("ke_ready"), 2)
            pe.wait_ge(S("main_empty"), MEND["av"])
            pe.wait_ge(S("rel_ready"), 12)
            for i in range(2):
                if i:
                    tile_T()
                    pe.wait_ge(S("u_used"), 1)
                for ch in range(NCH):
                    t, r, c = ch // 2, (ch % 2) * A_CHUNK, ch // 2
                    for hh in range(2):
                        h = 2 * i + hh
                        last = pe.matmul(lgb[ch % 2][64 * hh:64 * hh + 64, c * A_DV:(c + 1) * A_DV],
                                         keR[r:r + A_CHUNK, t, h * 64:h * 64 + 64],
                                         av[r:r + A_CHUNK, t, h * A_DV:(h + 1) * A_DV], start=True, stop=True,
                                         skip_group_check=True)
                last.then_inc(S("u_full"), 1)
            tile_T()
            pe.wait_ge(S("qk_ready"), 1)
            pe.wait_ge(S("lru_tanh"), 6)

            def gla_att(t):
                if t >= 2:
                    pe.wait_ge(S("attm_ready"), 2 * (t - 1))
                for h in range(A_HEADS):
                    r = slice(64 * (h % 2), 64 * (h % 2) + 64)
                    c0 = (h // 2) * P
                    last = pe.matmul(att_bank[t % 2][h % 2][:, c0:c0 + P], kd[r, h // 2, t * P:(t + 1) * P],
                                     aqT[r, h // 2, t * P:(t + 1) * P], start=True, stop=True, skip_group_check=True)
                last.then_inc(S("att_full"), 1)

            def gla_out(t):
                pe.wait_ge(S("attm_ready"), 2 * (t + 1))
                if t >= 2:
                    pe.wait_ge(S("oa_copied"), 2 * (t - 1))
                for h in range(A_HEADS):
                    i, r0 = h // 2, 64 * (h % 2)
                    b = oa_bank[t % 2][h % 2]
                    cs, vs = slice(i * A_DV, (i + 1) * A_DV), slice(h * A_DV, (h + 1) * A_DV)
                    last = pe.matmul(b[:, cs], attm[:, t % 2, h, :], av[:, t, vs], start=True, stop=False, skip_group_check=True)
                    for hf in range(2):
                        ch = 2 * t + hf
                        if ch == 0:
                            continue
                        last = pe.matmul(b[64 * hf:64 * hf + 64, cs], aqT[r0:r0 + 64, i, ch * A_CHUNK:(ch + 1) * A_CHUNK],
                                         St[r0:r0 + 64, i, ch, :], start=False, stop=True, skip_group_check=True)
                last.then_inc(S("oa_full"), 1)
                pe.drain().then_inc(S("gla_pe_done"), 1)

            pe.wait_ge(S("main_empty"), MEND["bv"] + 2)
            gla_att(0)
            pe.wait_ge(S("u_used"), 2)
            for t in range(NT):
                if t + 1 < NT:
                    gla_att(t + 1)
                gla_out(t)
            tile_T()
            proj_t()
            proj_r()

            def to_T(src):
                for c in range(KW):
                    b = main_bank()
                    for t in range(NT):
                        last = pe.transpose(b[:, t * P:(t + 1) * P], src[:, t, c * P:(c + 1) * P], ident)
                    main_full(last)

            pe.wait_ge(S("oa_ready"), 1)
            to_T(oA)

            def unit(n):
                br, i, h = n // (NT * HEADS), (n // HEADS) % NT, n % HEADS
                q, k, v = ((cqT, ckT, cv), (bqT, bkT, bv))[br]
                return br, i, h, q, k, v

            def logits(n):
                br, i, h, q, k, v = unit(n)
                if n >= 2:
                    pe.wait_ge(S("lg_read"), n - 1)
                r = slice(64 * (h % 2), 64 * (h % 2) + 64)
                pe.matmul(lgb[n % 2][:, 0:(i + 1) * P], q[r, h // 2, i * P:(i + 1) * P], k[r, h // 2, 0:(i + 1) * P],
                          start=True, stop=True).then_inc(S("lg_full"), 1)

            def transp(n):
                br, i, h, q, k, v = unit(n)
                pe.wait_ge(S("p_ready"), n + 1)
                if n >= 2:
                    pe.wait_ge(S("pT_ready"), n - 1)
                for b in range(i + 1):
                    last = pe.transpose(aux[n % 2][:, b * P:(b + 1) * P], pr[n % 3][:, b * P:(b + 1) * P], ident)
                last.then_inc(S("pT_full"), 1)

            def attend(n):
                br, i, h, q, k, v = unit(n)
                pe.wait_ge(S("pT_ready"), n + 1)
                g = n // HEADS
                if h == 0 and g >= 2:
                    pe.wait_ge(S("o_done"), g - 1)
                for b in range(i + 1):
                    last = pe.matmul(ps[6 + g % 2][:, h * HD:(h + 1) * HD], pT[:, n % 2, b * P:(b + 1) * P],
                                     v[:, b, h * HD:(h + 1) * HD], start=(b == 0), stop=(b == i), skip_group_check=True)
                last.then_inc(S("pT_used"), 1)

            units = 2 * NT * HEADS
            pe.wait_ge(S("main_empty"), MEND["cv"])
            pe.wait_ge(S("u_used"), 2)
            pe.wait_ge(S("attm_ready"), 2 * NT)
            pe.wait_ge(S("oa_copied"), 2 * NT)
            step = {"n": 0}

            def early_gates(upto):
                while step["n"] < upto:
                    k = step["n"] % KD
                    if k == 0:
                        step["w"] = [v[:, 0:KD * P].rearrange("p (k n) -> p k n", n=P) for v in next_chunk()]
                        step["bank"] = main_bank()
                    last = products(step["bank"][:, :], [v[:, k, :] for v in step["w"]], (xh[:, k, :], xl[:, k, :]),
                                    k == 0, k == KD - 1)
                    if k == KD - 1:
                        main_full(last)
                    step["n"] += 1

            for n in range(units + 3):
                if n < units:
                    logits(n)
                    early_gates((n + 1) * KD * NBR * EARLY_M // units)
                if 2 <= n <= units + 1:
                    transp(n - 2)
                if n >= 3:
                    attend(n - 3)
            pe.wait_ge(S("o_done"), NT)
            to_T(oR[1])
            pe.wait_ge(S("o_done"), 2 * NT)
            to_T(oR[0])
            pe.wait_ge(S("main_empty"), MEND["oTb"])
            n = 0
            for m in range(KD):
                for b_ in (0, 2):
                    if m >= EARLY_M:
                        proj_t(2)
                    w = [v[:, 0:2 * KW * P].rearrange("p (j k n) -> p j k n", j=2, n=P) for v in next_chunk()]
                    for j in range(2):
                        if n >= 2:
                            pe.wait_ge(S("merge_done"), n - 1)
                        for k in range(KW):
                            last = products(aux[n % 2][:, :], [v[:, j, k, :] for v in w],
                                            (oTh[b_ + j][:, k, :], oTl[b_ + j][:, k, :]), k == 0, k == KW - 1)
                        last.then_inc(S("br_full"), 1)
                        n += 1
            pe.wait_ge(S("ml_done"), KD - 1)
            nr = GROUPS + NE
            pe.wait_ge(S("wr_landed"), 80)
            for m in range(KD + 2):
                if m < KD:
                    if m >= 2:
                        pe.wait_ge(S("h_done"), m - 1)
                    rows_tile(lgb[m % 2], (mh, ml), P, last_column=m == 0).then_inc(S("out_full"), 1)
                if 1 <= m <= KD:
                    pe.wait_ge(S("hg_ready"), m)
                    b = main_bank()
                    for t in range(NT):
                        last = pe.transpose(b[:, t * P:(t + 1) * P], hg[:, t, (m - 1) * P:m * P], ident)
                    main_full(last)
                if m >= 2:
                    k = m - 2
                    pe.wait_ge(S("main_empty"), MEND["gate"] + k + 1)
                    for t in range(NT):
                        last = pe.matmul(rt_bank[t][:, 0:nr], hgT_f[:, k % 2, t * P:(t + 1) * P], wr[:, k, :],
                                         start=(k == 0), stop=(k == KD - 1), skip_group_check=True)
                    last.then_inc(S("hgT_used"), 1)
            pe.wait_ge(S("sel_ready"), 1)
            for t in range(NT):
                for t2 in range(t + 1):
                    pe.matmul(ps[5][:, t * NE:(t + 1) * NE], earlier if t2 == t else allones, sel16[:, t2, :],
                              start=(t2 == 0), stop=(t2 == t))
            for t in range(NT):
                last = pe.matmul(ps[5][:, NT * NE:(NT + 1) * NE], allones, sel16[:, t, :], start=(t == 0), stop=(t == NT - 1))
            last.then_inc(S("rank_full"), 1)
            pe.wait_ge(S("onehot_ready"), NT)
            for e in range(NE):
                for t in range(NT):
                    last = pe.matmul(ps[7][:, 3 * e:3 * e + 3], onehot[:, t, :].rearrange("p (c e) -> p e c", e=NE)[:, e, :], told[:, t, :, e],
                                     start=(t == 0), stop=(t == NT - 1))
            last.then_inc(S("token_full"), 1)
            pe.wait_ge(S("dense_known"), 1)
            over = pe.value_load(dense[:, :], min_val=0, max_val=1)
            with pe.If(over):
                for c in range(KD):
                    b = main_bank()
                    for t in range(NT):
                        last = pe.transpose(b[:, t * P:(t + 1) * P], xs[:, t, c * P:(c + 1) * P], ident)
                    main_full(last)
                pe.wait_ge(S("main_empty"), MEND["x2T"])
                n = y = 0
                for e in range(NE):
                    s = e % 2
                    pe.wait_ge(S(f"e_landed{s}"), 48 * (e // 2 + 1))
                    for m in range(KH):
                        if n >= 2:
                            pe.wait_ge(S("hT_ready"), n - 1)
                        for k in range(KD):
                            pe.matmul(ps[n % 2][:, :], wg[s][:, k, m * P:(m + 1) * P], xnT[:, k, :], start=(k == 0), stop=(k == KD - 1))
                        for k in range(KD):
                            last = pe.matmul(ps[2 + n % 2][:, :], wu[s][:, k, m * P:(m + 1) * P], xnT[:, k, :],
                                             start=(k == 0), stop=(k == KD - 1))
                        last.then_inc(S("gu_full"), 1)
                        n += 1
                    pe.wait_ge(S("hT_ready"), n)
                    if e == 0:
                        pe.wait_ge(S("rt_read"), NT)
                    for t in range(NT):
                        for hf in range(2):
                            if y >= 4:
                                pe.wait_ge(S("acc_done"), y - 3)
                            for k in range(KH):
                                last = pe.matmul(ps[4 + y % 4][:, :], hT[:, k, t * P:(t + 1) * P], wd[s][:, k, hf * 512:(hf + 1) * 512],
                                                 start=(k == 0), stop=(k == KH - 1))
                            last.then_inc(S("y_full"), 1)
                            y += 1
                    pe.drain().then_inc(S("e_used"), 1)
            with pe.Else():
                def x_transposes(e):
                    pe.wait_ge(S(f"xg_landed{e % 2}"), 16 * (e // 2 + 1))
                    if e == 0:
                        pe.wait_ge(S("token_read"), 1)
                    else:
                        pe.wait_ge(S("xlo_done"), 2 * e)
                        pe.wait_ge(S("hlo_done"), e - 1) if e >= 2 else None
                    for j in range(2):
                        for k in range(4):
                            last = pe.transpose(ps[6 + j][:, k * P:(k + 1) * P], xg[e % 2][:, (4 * j + k) * P:(4 * j + k + 1) * P],
                                                ident)
                        last.then_inc(S("xgT_full"), 1)

                def h_transposes(e):
                    pe.wait_ge(S("h_ready"), e + 1)
                    pe.wait_ge(S("xlo_done"), 2 * min(e + 2, NE))
                    for k in range(KH):
                        last = pe.transpose(ps[6][:, k * P:(k + 1) * P], hrow[e % 2][:, k * P:(k + 1) * P], ident)
                    last.then_inc(S("hgT_full"), 1)

                x_transposes(0)
                for c, (kind, e, hf) in enumerate(STEPS):
                    if kind == "u" and not hf and e >= 1:
                        h_transposes(e - 1)
                    if kind == "d" and not hf:
                        if e == NE - 1:
                            h_transposes(e)
                        pe.wait_ge(S("hlo_done"), e + 1)
                        if e >= 1:
                            pe.wait_ge(S("y_out"), 2 * e)
                    if kind == "g" and not hf:
                        pe.wait_ge(S("xlo_done"), 2 * (e + 1))
                        if e >= 2:
                            pe.wait_ge(S("h_ready"), e - 1)
                    pe.wait_ge(S("split_done"), c + 1)
                    if kind == "d":
                        v = [w[c % NW].rearrange("p (k n) -> p k n", k=2) for w in (w_hi, w_lo)]
                        hi, lo = hgT[e % 2]
                        for k in range(2):
                            for j in range(2):
                                cs = slice(512 * j, 512 * (j + 1))
                                last = products(ps[4 + j][:, :], (hi[:, 2 * hf + k, :], lo[:, 2 * hf + k, :]),
                                                (v[0][:, k, cs], v[1][:, k, cs]), hf == 0 and k == 0, hf == 1 and k == 1)
                    else:
                        v = [w[c % NW].rearrange("p (k n) -> p k n", k=4) for w in (w_hi, w_lo)]
                        hi, lo = xgT[e % 2]
                        bank = ps[2 * (e % 2) + (kind == "u")]
                        for k in range(4):
                            last = products(bank[:, :], (hi[:, 4 * hf + k, :], lo[:, 4 * hf + k, :]),
                                            (v[0][:, k, :], v[1][:, k, :]), hf == 0 and k == 0, hf == 1 and k == 3)
                    last.then_inc(S("chunk_used"), 1)
                    if kind == "u" and hf and e + 1 < NE:
                        x_transposes(e + 1)

        @block.vector
        def _(dve):
            state = {"chain": "dve_step", "step": 0, "sig": {}, "chunk": 0, "main_hi": 0, "bank": 0}

            def link(ins):
                state["step"] += 1
                ins.then_inc(S(state["chain"]), 1)
                dve.wait_ge(S(state["chain"]), state["step"])

            def new_chain(name, sig):
                state.update(chain=name, step=0, sig=dict(sig))

            def sig(name, ins):
                n = state["sig"][name] = state["sig"].get(name, 0) + 1
                ins.then_inc(S(name), 1)
                dve.wait_ge(S(name), n)

            def tell(name, ins):
                state["sig"][name] = state["sig"].get(name, 0) + 1
                ins.then_inc(S(name), 1)

            ts, tt, stt = dve.tensor_scalar, dve.tensor_tensor, dve.scalar_tensor_tensor

            def flat(v):
                s = v.shape
                if len(s) == 3:
                    return v.rearrange("p a b -> p (a b)")
                return v

            dve.memset(ones[:, :], 1.0).then_inc(S("memsets"), 1)
            dve.memset(seg, 1.0).then_inc(S("memsets"), 1)
            dve.memset(dxp[:, :, 0:3], 0.0).then_inc(S("memsets"), 1)
            dve.wait_ge(S("memsets"), 3)
            link(dve.memset(seg.rearrange("p (a b) -> p a b", b=A_CHUNK)[:, :, 0:1], 0.0))

            def norm_scale(src, count):
                dve.wait_ge(S("ss_ready"), NT * count)
                sig("ms_ready", ts(stat[:, 1, :], stat[:, 0, :], 1.0 / D, EPS, ALU.mult, ALU.add))
                dve.wait_ge(S("rms_ready"), count)
                link(dve.reciprocal(stat[:, 3, :], stat[:, 2, :]))

            def advance(upto):
                while state["chunk"] < min(upto, NC_):
                    c = state["chunk"]
                    dve.wait_ge(S("c_hi_done"), c + 1)
                    hi, src = split_views(c, c_hi)
                    lo, _ = split_views(c, c_lo)
                    if CHUNKS[c][0] == "pad":
                        for v in (c_hi, c_lo):
                            link(dve.memset(v[c % CW].rearrange("p (a c) -> p a c", c=64)[:, :, A_DK:64], 0.0))
                    if CHUNKS[c][0] == "ik":
                        for h in range(IDX_HEADS):
                            ins = stt(lo[:, :, h, :], src[:, :, h, :], WSCALE, hi[:, :, h, :], ALU.mult, ALU.subtract)
                            if h < IDX_HEADS - 1:
                                link(ins)
                    else:
                        ins = stt(lo, src, WSCALE, hi, ALU.mult, ALU.subtract)
                    tell("c_split", ins)
                    state["chunk"] = c + 1

            def lo_main(lo, hi, scale=1.0):
                n = state["main_hi"] = state["main_hi"] + 1
                dve.wait_ge(S("main_hi"), n)
                ins = stt(lo, main[state["bank"] % 2][:, :], scale, hi, ALU.mult, ALU.subtract)
                state["bank"] += 1
                ins.then_inc(S("main_empty"), 1)

            norm_scale(xs, 1)
            for t in range(NT):
                sig("xs_ready", ts(xs[:, t, :], xs[:, t, :], stat[:, 3, t:t + 1], None, ALU.mult))
            dve.wait_ge(S("rows_T"), 1)
            sig("cols_ready", dve.tensor_copy(cols[:, :], ps[6][:, 0:NROW]))
            for c in range(KD):
                lo_main(xl[:, c, :], xh[:, c, :], c_norm1[:, c:c + 1])
                if c % 2:
                    advance(c // 2 + 1)
            link(ts(half[:, 0:32], c_bgate, 0.5, None, ALU.mult))
            sig("cols_ready", ts(half[:, 32:38], cols[:, 63:69], 0.5, None, ALU.mult))
            link(ts(sp[:, 0, :], c_lam, -1.0, None, ALU.mult))
            sig("lam_abs", tt(sp[:, 0, :], sp[:, 0, :], c_lam, ALU.min))
            dve.wait_ge(S("bias_mm"), 1)
            sig("bias_rows_ready", dve.tensor_copy(bias_rows[:, 0:T], aux[0][0:2 * HEADS, :]))
            sig("bias_rows_ready", dve.tensor_copy(bias_rows[:, T:T + P], aux[1][0:2 * HEADS, 0:P]))
            dve.wait_ge(S("lam_exp"), 1)
            e_, z_, z2, pl = sp[:, 1, :], sp[:, 2, :], sp[:, 3, :], sp[:, 4, :]
            link(ts(z_, e_, 2.0, None, ALU.add))
            link(dve.reciprocal(z_, z_))
            link(tt(z_, z_, e_, ALU.mult))
            link(tt(z2, z_, z_, ALU.mult))
            link(ts(pl, z2, 1.0 / 19, 1.0 / 17, ALU.mult, ALU.add))
            for o in (15, 13, 11, 9, 7, 5, 3, 1):
                link(tt(pl, pl, z2, ALU.mult))
                link(ts(pl, pl, 1.0 / o, None, ALU.add))
            link(tt(pl, pl, z_, ALU.mult))
            link(ts(sp[:, 5, :], c_lam, -1.0, 0.0, ALU.mult, ALU.max))
            link(stt(sp[:, 6, :], pl, 2.0, sp[:, 5, :], ALU.mult, ALU.add))
            sig("sp_ready", ts(sp[:, 7, :], sp[:, 6, :], LRU_C / 4, None, ALU.mult))
            advance(CEND["dx"] + AHEAD)
            dve.wait_ge(S("main_empty"), MEND["dx"])
            for c in range(KW):
                link(ts(xc[:, c, :], dxp[:, c, 3:3 + T], c_convw[:, 9 + c:10 + c], c_convb[:, c:c + 1], ALU.mult, ALU.add))
                for j in range(3):
                    ins = stt(xc[:, c, :], dxp[:, c, j:j + T], c_convw[:, 3 * j + c:3 * j + c + 1], xc[:, c, :], ALU.mult, ALU.add)
                    if c == KW - 1 and j == 2:
                        sig("xc_ready", ins)
                    else:
                        link(ins)
            n = 0
            for i in range(1, NT):
                nk = (i + 1) * P
                for h in range(IDX_HEADS):
                    dve.wait_ge(S("rel_ready"), n + 1)
                    w1 = iw[:, i, h:h + 1]
                    if h == 0:
                        ins = ts(sel[i], rel[:, n % 2, 0:nk], w1, None, ALU.mult)
                    else:
                        ins = stt(sel[i], rel[:, n % 2, 0:nk], w1, sel[i], ALU.mult, ALU.add)
                    sig("rel_used", ins)
                    n += 1
                link(tt(sel[i][:, i * P:nk], sel[i][:, i * P:nk], future, ALU.add))

            def take_best(i):
                link(dve.max(out=m8[:, :], in_=sel[i]))
                link(dve.match_replace(out=sel[i], in_to_replace=m8[:, :], in_values=sel[i], imm_value=TAKEN))

            def mask_rest(i):
                link(ts(sel[i], sel[i], -2e38, BIG, ALU.is_gt, ALU.mult))

            def topk(i, upto):
                for r in range(TOPK // 8):
                    if r % 3 == 2:
                        advance(min(upto, state["chunk"] + 1))
                    take_best(i)
                mask_rest(i)

            topk(1, CEND["dy"] + 1)
            advance(CEND["dy"] + AHEAD)
            dve.wait_ge(S("lru_sqrt"), 1)
            link(ts(flat(tr), flat(tr), 1.0, None, ALU.add))
            link(dve.reciprocal(flat(tr), flat(tr)))
            dve.wait_ge(S("lru_tanh"), 6)
            link(stt(flat(ti), flat(ti), 1.0, flat(xc), ALU.add, ALU.mult))
            link(tt(flat(ti), flat(ti), flat(tr), ALU.mult))
            advance(CEND["alr"] + AHEAD)
            sig("lru_u", tt(flat(ti), flat(ti), flat(sq_), ALU.mult))
            link(ts(flat(tr), flat(tr), 2.0, -1.0, ALU.mult, ALU.add))
            for c in range(KW):
                link(dve.tensor_tensor_scan(out=xc[:, c, :], data0=tr[:, c, :], data1=ti[:, c, :], initial=0.0,
                                            op0=ALU.mult, op1=ALU.add))
            advance(CEND["aqk"] + AHEAD)
            dve.wait_ge(S("z_full"), 2)
            for i in range(2):
                sig("zb_ready", ts(zb[:, i, :], ps[6 + i][:, :], c_b2[:, i:i + 1], None, ALU.add))
            link(ts(flat(na), flat(zb), -1.0, None, ALU.mult))
            sig("gla_na", tt(flat(na), flat(na), flat(zb), ALU.min))
            advance(CEND["av"] + AHEAD)
            dve.wait_ge(S("gla_ln"), 1)
            link(stt(flat(zb), flat(zb), 0.0, flat(na), ALU.min, ALU.subtract))
            sig("gla_b", dve.tensor_tensor_scan(out=flat(b16), data0=seg, data1=flat(zb), initial=0.0,
                                                op0=ALU.mult, op1=ALU.add))
            dve.wait_ge(S("y2_ready"), 1)
            link(ts(flat(sq_), flat(sq_), 0.044715, 1.0, ALU.mult, ALU.add))
            sig("gelu_in", tt(flat(sq_), flat(sq_), flat(dyT), ALU.mult))
            b4 = flat(b16).rearrange("p (n c) -> p n c", c=A_CHUNK)
            e4 = flat(ek).rearrange("p (n c) -> p n c", c=A_CHUNK)
            sig("gla_d", tt(e4, b4[:, :, A_CHUNK - 1:A_CHUNK].to_broadcast([P, 2 * NCH, A_CHUNK]), b4, ALU.subtract))
            dve.wait_ge(S("gelu_tanh"), 1)
            link(stt(flat(sq_), flat(sq_), 1.0, flat(dyT), ALU.add, ALU.mult))
            link(stt(flat(xc), flat(sq_), 0.5, flat(xc), ALU.mult, ALU.mult))
            link(dve.tensor_copy(flat(oTh[3]), flat(xc)))
            sig("lru_u", tt(flat(oTl[3]), flat(xc), flat(oTh[3]), ALU.subtract))
            advance(CEND["av"] + AHEAD + 2)
            dve.wait_ge(S("main_empty"), MEND["aqk"])
            dve.wait_ge(S("gla_e"), 3)
            link(tt(flat(kd), flat(kd), flat(akT), ALU.mult))
            sig("ke_T", tt(flat(akT), flat(akT), flat(ek), ALU.mult))
            sig("qk_ready", tt(flat(aqT), flat(aqT), flat(eb), ALU.mult))
            link(dve.memset(St[:, :, 0, :], 0.0))
            topk(2, CEND["bk"] + AHEAD)
            advance(CEND["bv"] + AHEAD)
            for i in range(2):
                dve.wait_ge(S("u_full"), i + 1)
                for ch in range(NCH):
                    ins = stt(St[:, i, ch + 1, :], St[:, i, ch, :], eb[:, i, ch * A_CHUNK + A_CHUNK - 1:(ch + 1) * A_CHUNK],
                              lgb[ch % 2][:, (ch // 2) * A_DV:(ch // 2 + 1) * A_DV], ALU.mult, ALU.add)
                    if ch == NCH - 1:
                        sig("u_used", ins)
                    else:
                        link(ins)
            for t in range(NT):
                dve.wait_ge(S("att_full"), t + 1)
                if t >= 2:
                    dve.wait_ge(S("gla_pe_done"), t - 1)
                for hh in range(2):
                    sig("attm_ready", tt(attm[:, t % 2, :, :].rearrange("p (i h) c -> p i h c", h=2)[:, :, hh, :],
                                         att_bank[t % 2][hh][:, 0:2 * P].rearrange("p (i c) -> p i c", c=P),
                                         glamask.unsqueeze(1).to_broadcast([P, 2, P]), ALU.mult))
            advance(CEND["bv"] + AHEAD + 2)
            dve.wait_ge(S("oa_sq"), 1)
            link(dve.tensor_reduce(ostat[:, :], flat(oA2).rearrange("p (n v) -> p n v", v=A_DV), axis=AX.X, op=ALU.add))
            sig("oa_ms", ts(ostat[:, :], ostat[:, :], 1.0 / A_DV, EPS, ALU.mult, ALU.add))
            dve.wait_ge(S("oa_rms"), 1)
            link(dve.reciprocal(ostat[:, :], ostat[:, :]))
            o3 = flat(oA).rearrange("p (n v) -> p n v", v=A_DV)
            sig("oa_mean", tt(o3, o3, ostat[:, :].unsqueeze(2).to_broadcast([P, NT * A_HEADS, A_DV]), ALU.mult))
            dve.wait_ge(S("gain_landed"), 16)
            link(tt(oA, oA, gain[:, :].unsqueeze(1).to_broadcast([P, NT, W]), ALU.mult))
            dve.wait_ge(S("oa_tanh"), 1)
            link(stt(flat(oA2), flat(oA2), 1.0, flat(ag), ALU.add, ALU.mult))
            sig("oa_ready", stt(flat(oA), flat(oA2), 0.5, flat(oA), ALU.mult, ALU.mult))
            advance(CEND["cv"] + AHEAD)
            state["bank"] = MEND["cv"]
            for c in range(KW):
                lo_main(oTl[0][:, c, :], oTh[0][:, c, :])
            dve.wait_ge(S("bias_landed"), 16)
            units = 2 * NT * HEADS

            def scores(n):
                br, i, h = n // (NT * HEADS), (n // HEADS) % NT, n % HEADS
                nk = (i + 1) * P
                head = h if br else HEADS + h
                dve.wait_ge(S("lg_full"), n + 1)
                if n >= 3:
                    dve.wait_ge(S("p_ready"), n - 2)
                l = lg[n % 3][:, 0:nk]
                sig("lg_read", tt(l, lgb[n % 2][:, 0:nk], bias[:, head, T - nk:T], ALU.add))
                if br and i:
                    link(tt(l, l, sel[i], ALU.add))
                tell("lg_ready", dve.tensor_reduce(nmx[:, n % 4:n % 4 + 1], l, axis=AX.X, op=ALU.max, negate=True))

            def finish(g):
                br, i = g // NT, g % NT
                dve.wait_ge(S("p_ready"), (g + 1) * HEADS)
                sig("rl_ready", dve.reciprocal(rl[:, g % 2, :], lsum[:, g % 2, :]))
                dve.wait_ge(S("pT_used"), (g + 1) * HEADS)
                if g == 0:
                    dve.wait_ge(S("main_empty"), MEND["oTa"])
                tell("o_done", tt(oR[0 if br else 1][:, i, :].rearrange("p (h c) -> p h c", c=HD),
                                 ps[6 + g % 2][:, 0:W].rearrange("p (h c) -> p h c", c=HD),
                                 rl[:, g % 2, :].unsqueeze(2).to_broadcast([P, HEADS, HD]), ALU.mult))

            for n in range(units):
                scores(n)
                if n % 2 == 0 and n < TOPK // 4:
                    take_best(NT - 1)
                    if n == TOPK // 4 - 2:
                        mask_rest(NT - 1)
                if n % HEADS == 3 and n > HEADS:
                    finish(n // HEADS - 1)
                    advance(CEND["cv"] + n // HEADS + AHEAD)
            finish(2 * NT - 1)
            advance(CEND["early"] + AHEAD)
            for k in (2, 1):
                for c in range(KW):
                    lo_main(oTl[k][:, c, :], oTh[k][:, c, :])

            def merged_lo(m):
                dve.wait_ge(S("mh_done"), m + 1)
                sig("ml_done", stt(ml[:, m, :], merged[:, m, :], 0.5 / WSCALE, mh[:, m, :], ALU.mult, ALU.subtract))

            for n in range(NBR * KD):
                m, b_ = n // NBR, n % NBR
                early = m < EARLY_M
                if n < NBR * KD - 2:
                    advance(PAIR0[m, b_ - b_ % 2] + (0 if early else b_ % 2) + AHEAD + 1)
                dve.wait_ge(S("br_full"), n + 1)
                if not early:
                    dve.wait_ge(S("main_empty"), MEND["oTb"] + n - NBR * EARLY_M + 1)
                g_ = gate_early[n] if early else gate_t[:, n % 2, :]
                if b_ == 0:
                    sig("merge_done", stt(merged[:, m, :], g_, 1.0, aux[n % 2][:, :], ALU.add, ALU.mult))
                else:
                    link(stt(gterm, g_, 1.0, aux[n % 2][:, :], ALU.add, ALU.mult))
                    sig("merge_done", tt(merged[:, m, :], merged[:, m, :], gterm, ALU.add))
                if b_ == 2 and m:
                    merged_lo(m - 1)
            merged_lo(KD - 1)
            dve.wait_ge(S("xres_landed"), 16)
            def split(c):
                dve.wait_ge(S("hi_done"), c + 1)
                tell("split_done", stt(w_lo[c % NW], stage[c % NS], WSCALE, w_hi[c % NW], ALU.mult, ALU.subtract))

            dve.wait_ge(S("gain2_landed"), 32)
            for m in range(KD):
                advance(CEND["merge"] + m + AHEAD)
                if m - 1 in SPLIT_AT:
                    split(SPLIT_AT.index(m - 1))
                dve.wait_ge(S("out_full"), m + 1)
                h_ = hres[:, :, m * P:(m + 1) * P]
                sig("h_done", stt(h_, lgb[m % 2][:, :].rearrange("p (t c) -> p t c", c=P), 1.0 / WSCALE, h_, ALU.mult, ALU.add))

                tell("hg_ready", tt(hg[:, :, m * P:(m + 1) * P], h_,
                                   gain2[:, m * P:(m + 1) * P].unsqueeze(1).to_broadcast([P, NT, P]), ALU.mult))

            dve.wait_ge(S("ssq_ready"), NT * KD)
            link(dve.tensor_reduce(stat[:, 0, :], ssq[:, :, :], axis=AX.X, op=ALU.add))
            sig("ms_ready", ts(stat[:, 1, :], stat[:, 0, :], 1.0 / D, EPS, ALU.mult, ALU.add))
            dve.wait_ge(S("rms_ready"), 2)
            sig("rstd2_ready", dve.reciprocal(stat[:, 3, :], stat[:, 2, :]))
            dve.wait_ge(S("hgT_used"), KD)
            nr = GROUPS + NE
            for t in range(NT):
                sig("rt_read", ts(rlog[:, t, :], rt_bank[t][:, 0:nr], stat[:, 3, t:t + 1], None, ALU.mult))
            gl = glog[:, :, :]
            link(tt(gl, rlog[:, :, 0:GROUPS], rbias[:, 0:GROUPS].unsqueeze(1).to_broadcast([P, NT, GROUPS]), ALU.add))
            link(tt(elog[:, :, :], rlog[:, :, GROUPS:], rbias[:, GROUPS:].unsqueeze(1).to_broadcast([P, NT, NE]), ALU.add))

            def R(i):
                return rt[:, i, :, :]

            def R1(i, j=0):
                return rt[:, i, :, j:j + 1]

            def wide(x):
                return x.to_broadcast([P, NT, 4])

            def argmax(dst, src, mx, tmp):
                link(dve.tensor_reduce(mx, src, axis=AX.X, op=ALU.max))
                link(tt(dst, src, wide(mx), ALU.is_equal))
                link(tt(dst, dst, prio.unsqueeze(1).to_broadcast([P, NT, 4]), ALU.mult))
                link(dve.tensor_reduce(tmp, dst, axis=AX.X, op=ALU.max))
                link(tt(dst, dst, wide(tmp), ALU.is_equal))

            argmax(R(3), gl, R1(0), R1(0, 1))
            sig("rt_sub", tt(R(1), gl, wide(R1(0)), ALU.subtract))
            link(tt(flat(elog[:, :, :]).rearrange("p (g e) -> p g e", e=EPG), flat(elog[:, :, :]).rearrange("p (g e) -> p g e", e=EPG),
                    flat(R(3)).unsqueeze(2).to_broadcast([P, NT * GROUPS, EPG]), ALU.mult))
            link(dve.tensor_reduce(R(4), elog[:, :, :].rearrange("p t (g e) -> p t e g", e=EPG), axis=AX.X, op=ALU.add))
            argmax(R(6), R(4), R1(7, 0), R1(0, 1))
            link(stt(flat(R(5)), flat(R(6)), BIG, flat(R(4)), ALU.mult, ALU.add))
            argmax(R(10), R(5), R1(7, 1), R1(0, 1))
            sig("rt_diff", tt(R1(8), R1(7, 1), R1(7, 0), ALU.subtract))
            dve.wait_ge(S("rt_exp"), 2)
            link(dve.tensor_reduce(R1(11), R(2), axis=AX.X, op=ALU.add))
            link(dve.reciprocal(R1(11), R1(11)))
            link(ts(R1(12), R1(9), 1.0, None, ALU.add))
            link(dve.reciprocal(R1(12), R1(12)))
            w1, w2 = wsel[:, 0, :].unsqueeze(2), wsel[:, 1, :].unsqueeze(2)
            link(tt(w1, R1(12), R1(11), ALU.mult))
            link(tt(w2, w1, R1(9), ALU.mult))

            def spread(dst, r):
                link(tt(dst.rearrange("p t (g e) -> p t g e", e=EPG), r.unsqueeze(2).to_broadcast([P, NT, GROUPS, EPG]),
                        R(3).unsqueeze(3).to_broadcast([P, NT, GROUPS, EPG]), ALU.mult))

            spread(selj[:, 0, :, :], R(6))
            spread(selj[:, 1, :, :], R(10))
            sig("sel_ready", tt(sel16[:, :, :], selj[:, 0, :, :], selj[:, 1, :, :], ALU.add))
            link(dve.tensor_copy(told[:, :, 0, :], tokid.unsqueeze(2).to_broadcast([P, NT, NE])))
            link(dve.tensor_copy(told[:, :, 1, :], selj[:, 1, :, :]))
            link(dve.memset(told[:, :, 2, :], 1.0))
            dve.wait_ge(S("rank_full"), 1)
            link(dve.tensor_reduce(total[:, 0:1], ps[5][:, NT * NE:(NT + 1) * NE], axis=AX.X, op=ALU.max))
            link(ts(dense[:, :], total[0:1, 0:1], float(CAP), None, ALU.is_gt))
            link(stt(flat(rank[:, :, :]), ps[5][:, 0:NT * NE], 1.0, flat(sel16[:, :, :]), ALU.add, ALU.mult))
            link(ts(rank[:, :, :], rank[:, :, :], -1.0, None, ALU.add))
            for t in range(NT):
                tell("onehot_ready", tt(*onehot_views(t), ALU.is_equal))
            dve.wait_ge(S("token_full"), 1)
            got = ps[7][:, 0:3 * NE].rearrange("p (e a) -> p a e", a=3)
            link(ts(slotv[:, 0, :], got[:, 2, :], -float(NOWHERE), float(NOWHERE), ALU.mult, ALU.add))
            link(tt(slotv[:, 1, :], slotv[:, 0, :], got[:, 0, :], ALU.add))
            link(dve.tensor_copy(token_of[:, :], slotv[:, 1, :]))
            sig("token_read", stt(slotv[:, 2, :], got[:, 1, :], float(T), slotv[:, 1, :], ALU.mult, ALU.add))
            link(dve.tensor_copy(row_of[:, :], slotv[:, 2, :]))
            sig("dense_known", ts(total[:, 1:2], total[:, 0:1], 1.0, None, ALU.mult))
            for c in range(FIRST, NW):
                split(c)

            def ending(add_experts):
                def mean(t):
                    dve.wait_ge(S("ss_ready"), NT + t + 1)
                    sig("ms_ready", ts(stat[:, 1, t:t + 1], stat[:, 0, t:t + 1], 1.0 / D, EPS, ALU.mult, ALU.add))

                def normed(t):
                    dve.wait_ge(S("rms_ready"), 3 + t)
                    link(dve.reciprocal(stat[:, 3, t:t + 1], stat[:, 2, t:t + 1]))
                    if t == 0:
                        dve.wait_ge(S("nf_landed"), 16)
                    sig("y_done", stt(onorm[:, t, :], hres[:, t, :], stat[:, 3, t:t + 1], nf, ALU.mult, ALU.mult))

                for t in range(NT + 2):
                    if t < NT:
                        add_experts(t)
                    if t >= 2:
                        normed(t - 2)
                    if 1 <= t <= NT:
                        mean(t - 1)

            over = dve.value_load(dense[:, :], min_val=0, max_val=1)
            before = dict(state["sig"])
            with dve.If(over):
                new_chain("dve_step_dense", before)
                link(tt(R(6), R(6), wide(w1), ALU.mult))
                link(tt(R(10), R(10), wide(w2), ALU.mult))
                link(tt(R(6), R(6), R(10), ALU.add))
                link(ts(R(6), R(6), 0.5, None, ALU.mult))
                spread(gates[:, :, :], R(6))
                n = y = 0
                for e in range(NE):
                    for m in range(KH):
                        dve.wait_ge(S("sg_ready"), n + 1)
                        if m == 0 and e >= 1:
                            dve.wait_ge(S("e_used"), e)
                        link(stt(sg[:, n % 2, :], sg[:, n % 2, :], 1.0, ps[n % 2][:, :], ALU.add, ALU.mult))
                        sig("hT_ready", tt(hT[:, m, :], sg[:, n % 2, :], ps[2 + n % 2][:, :], ALU.mult))
                        n += 1
                    for t in range(NT):
                        for hf in range(2):
                            dve.wait_ge(S("y_full"), y + 1)
                            h_ = hres[:, t, hf * 512:(hf + 1) * 512]
                            sig("acc_done", stt(h_, ps[4 + y % 4][:, :], gates[:, t, e:e + 1], h_, ALU.mult, ALU.add))
                            y += 1
                ending(lambda t: sig("moe_done", ts(total[:, 1:2], total[:, 0:1], 1.0, None, ALU.mult)))
            with dve.Else():
                new_chain("dve_step_routed", before)
                def x_lo(e):
                    for j in range(2):
                        dve.wait_ge(S("xhi_done"), 2 * e + j + 1)
                        tell("xlo_done", tt(xgT[e % 2][1][:, 4 * j:4 * j + 4, :].rearrange("p a b -> p (a b)"), ps[6 + j][:, :],
                                           xgT[e % 2][0][:, 4 * j:4 * j + 4, :].rearrange("p a b -> p (a b)"), ALU.subtract))

                def h_lo(e):
                    dve.wait_ge(S("hhi_done"), e + 1)
                    tell("hlo_done", tt(hgT[e % 2][1].rearrange("p a b -> p (a b)"), ps[6][:, :],
                                       hgT[e % 2][0].rearrange("p a b -> p (a b)"), ALU.subtract))

                x_lo(0)
                for c, (kind, e, hf) in enumerate(STEPS):
                    if NW <= c + FIRST < len(STEPS):
                        split(c + FIRST)
                    if kind == "u" and not hf and e >= 1:
                        h_lo(e - 1)
                    if kind == "d" and not hf and e == NE - 1:
                        h_lo(e)
                    if kind == "u" and hf:
                        if e + 1 < NE:
                            x_lo(e + 1)
                        dve.wait_ge(S("sgr_ready"), e + 1)
                        dve.wait_ge(S("chunk_used"), steps_to("u", e))
                        if e >= 2:
                            dve.wait_ge(S("hgT_full"), e - 1)
                        b0 = 2 * (e % 2)
                        link(stt(sgr[e % 2], sgr[e % 2], 1.0, ps[b0][:, :], ALU.add, ALU.mult))
                        tell("h_ready", stt(hrow[e % 2], sgr[e % 2], 0.5 * HSCALE / WSCALE ** 2, ps[b0 + 1][:, :], ALU.mult, ALU.mult))
                def add_rows(t):
                    dve.wait_ge(S(f"yg_landed{t}"), 16)
                    link(stt(hres[:, t, :], yg[t][:, 0, :], wsel[:, 0, t:t + 1], hres[:, t, :], ALU.mult, ALU.add))
                    sig("moe_done", stt(hres[:, t, :], yg[t][:, 1, :], wsel[:, 1, t:t + 1], hres[:, t, :], ALU.mult, ALU.add))

                ending(add_rows)


_INS = ["x", "w_in", "a_w2", "a_b2", "a_gain", "conv_w", "conv_b", "lru_wr", "lru_br", "lru_wi", "lru_bi", "lru_lambda",
        "w_gate", "b_gate", "w_branch", "w_out", "rel_bias", "norm1", "norm2", "norm_f", "moe_wrg", "moe_brg",
        "moe_wre", "moe_bre", "moe_wg", "moe_wu", "moe_wd"]


def kernel(**inputs):
    import concourse.bacc as _bacc
    from concourse.bass_utils import run_bass_kernel_spmd as _run

    nc = _bacc.Bacc("TRN2", target_bir_lowering=False, num_devices=1)
    arrays, d = {}, {}
    given = {n: np.ascontiguousarray(inputs[n]) for n in _INS}
    given.update(zip(("c_sq", "c_half", "c_slots", "c_tab", "c_sel"), constants()))
    for name, a in given.items():
        arrays[f"in_{name}"] = a
        d[name] = nc.dram_tensor(f"in_{name}", a.shape, mybir.dt.from_np(a.dtype), kind="ExternalInput").ap()
    d["bias_scratch"] = nc.dram_tensor("bias_scratch", (2 * HEADS, P, T + P), F32, kind="Internal").ap()
    d["x2_rows"] = nc.dram_tensor("x2_rows", (T, D), F32, kind="Internal").ap()
    d["y_rows"] = nc.dram_tensor("y_rows", (2 * T, D), F32, kind="Internal").ap()
    out = nc.dram_tensor("out_0", (1, T, D), F32, kind="ExternalOutput").ap()
    build(nc, d, out)
    r = _run(nc, [arrays], core_ids=[0])
    return r.results[0]["out_0"]
```
